# Optimizing a Trainium2 kernel written in Bass

```python
import jax, jax.numpy as jnp
from jax import lax
import numpy as np

D_MODEL = 1024
BATCH = 1
SEQ = 256
DEPTH = 2

PLE_DIM = 256
D_FF = 2816
POOL_WINDOWS = (2, 4, 8, 16)
POOL_GROUP = D_MODEL // 8
POOL_WIDTH = len(POOL_WINDOWS) * POOL_GROUP
SGU_HEADS = 4
SGU_HEAD_DIM = D_MODEL // 8
SGU_WIDTH = SGU_HEADS * SGU_HEAD_DIM
CHUNK = 128
CONV_WIDTH = D_MODEL // 2
CONV_KERNEL = 31
N_BRANCH = 3
OFF_POOL = 0
OFF_U = OFF_POOL + POOL_WIDTH
OFF_V = OFF_U + SGU_WIDTH
OFF_GLU_A = OFF_V + SGU_WIDTH
OFF_GLU_B = OFF_GLU_A + CONV_WIDTH
OFF_GATES = OFF_GLU_B + CONV_WIDTH
IN_COLS = OFF_GATES + N_BRANCH * D_MODEL
EPS = 1e-6

kernel_name = "hybrid_pool_sgu_conformer_gated_trunk"

def rms_norm(x, g):
    xf = x.astype(jnp.float32)
    y = xf * lax.rsqrt(jnp.mean(xf * xf, axis=-1, keepdims=True) + EPS)
    return (y * g.astype(jnp.float32)).astype(x.dtype)

def layer_norm(x, g, b):
    xf = x.astype(jnp.float32)
    mu = jnp.mean(xf, axis=-1, keepdims=True)
    xc = xf - mu
    y = xc * lax.rsqrt(jnp.mean(xc * xc, axis=-1, keepdims=True) + EPS)
    return (y * g.astype(jnp.float32) + b.astype(jnp.float32)).astype(x.dtype)

def swiglu(x, w_gate, w_up, w_down):
    return (jax.nn.silu(x @ w_gate) * (x @ w_up)) @ w_down

def pool_mixer(xa, w_grp, scale):
    b_, s_, _ = xa.shape
    xf = xa.astype(jnp.float32).reshape(b_, s_, len(POOL_WINDOWS), POOL_GROUP)
    csum = jnp.cumsum(xf, axis=1)
    pos = jnp.arange(s_)
    outs = []
    for gi, w in enumerate(POOL_WINDOWS):
        cg = csum[:, :, gi]
        shifted = jnp.pad(cg, ((0, 0), (w, 0), (0, 0)))[:, :s_]
        count = jnp.minimum(pos + 1, w).astype(jnp.float32)[None, :, None]
        outs.append((cg - shifted) / count - xf[:, :, gi])
    pooled = jnp.stack(outs, axis=2).astype(xa.dtype)
    y = jnp.einsum('bsgi,gio->bsgo', pooled, w_grp)
    return y.reshape(b_, s_, POOL_WIDTH) * scale

def sgu_mixer(u, v, ln_g, ln_b, w_s, b_s):
    b_, s_, _ = u.shape
    u = jax.nn.gelu(u, approximate=False)
    v = layer_norm(jax.nn.gelu(v, approximate=False), ln_g, ln_b)
    vc = v.reshape(b_, s_ // CHUNK, CHUNK, SGU_HEADS, SGU_HEAD_DIM)
    causal = jnp.tril(jnp.ones((CHUNK, CHUNK), dtype=bool))
    w = jnp.where(causal[None], w_s, jnp.zeros_like(w_s))
    s = jnp.einsum('hts,bcshd->bcthd', w, vc) + b_s.T[None, None, :, :, None]
    return u * s.reshape(b_, s_, SGU_WIDTH)

def conv_mixer(a, gate, dw_k, dw_b, ln_g, ln_b):
    xg = a * jax.nn.sigmoid(gate)
    y = lax.conv_general_dilated(
        xg, dw_k, window_strides=(1,), padding=[(CONV_KERNEL - 1, 0)],
        dimension_numbers=('NWC', 'WIO', 'NWC'), feature_group_count=CONV_WIDTH) + dw_b
    return jax.nn.silu(layer_norm(y, ln_g, ln_b))

def setup_inputs(seed: int = 0) -> dict:
    key = jax.random.key(seed)
    ks = iter(jax.random.split(key, 40))
    L = DEPTH

    def w(shape, fan_in):
        return jax.random.normal(next(ks), shape, jnp.float32) * (fan_in ** -0.5)

    def gain(shape):
        return 1.0 + 0.05 * jax.random.normal(next(ks), shape, jnp.float32)

    def bias(shape):
        return 0.02 * jax.random.normal(next(ks), shape, jnp.float32)

    return {
        "x": jax.random.normal(next(ks), (BATCH, SEQ, D_MODEL), jnp.float32),
        "p": jax.random.normal(next(ks), (DEPTH, BATCH, SEQ, PLE_DIM), jnp.float32),
        "ffn1_pre_g": gain((L, D_MODEL)),
        "ffn1_w_gate": w((L, D_MODEL, D_FF), D_MODEL),
        "ffn1_w_up": w((L, D_MODEL, D_FF), D_MODEL),
        "ffn1_w_down": w((L, D_FF, D_MODEL), D_FF),
        "ffn1_post_g": gain((L, D_MODEL)),
        "mix_pre_g": gain((L, D_MODEL)),
        "w_in": w((L, D_MODEL, IN_COLS), D_MODEL),
        "pool_w": w((L, len(POOL_WINDOWS), POOL_GROUP, POOL_GROUP), POOL_GROUP),
        "pool_scale": gain((L, POOL_WIDTH)),
        "w_pool_out": w((L, POOL_WIDTH, D_MODEL), POOL_WIDTH),
        "sgu_ln_g": gain((L, SGU_WIDTH)),
        "sgu_ln_b": bias((L, SGU_WIDTH)),
        "sgu_w_s": w((L, SGU_HEADS, CHUNK, CHUNK), CHUNK),
        "sgu_b_s": 1.0 + 0.1 * jax.random.normal(next(ks), (L, SGU_HEADS, CHUNK), jnp.float32),
        "w_sgu_out": w((L, SGU_WIDTH, D_MODEL), SGU_WIDTH),
        "conv_dw_k": w((L, CONV_KERNEL, 1, CONV_WIDTH), CONV_KERNEL),
        "conv_dw_b": bias((L, CONV_WIDTH)),
        "conv_ln_g": gain((L, CONV_WIDTH)),
        "conv_ln_b": bias((L, CONV_WIDTH)),
        "w_conv_out": w((L, CONV_WIDTH, D_MODEL), CONV_WIDTH),
        "w_out": w((L, D_MODEL, D_MODEL), D_MODEL),
        "mix_post_g": gain((L, D_MODEL)),
        "ffn2_pre_g": gain((L, D_MODEL)),
        "ffn2_w_gate": w((L, D_MODEL, D_FF), D_MODEL),
        "ffn2_w_up": w((L, D_MODEL, D_FF), D_MODEL),
        "ffn2_w_down": w((L, D_FF, D_MODEL), D_FF),
        "ffn2_post_g": gain((L, D_MODEL)),
        "ple_w_proj": w((L, PLE_DIM, D_MODEL), PLE_DIM),
        "ple_pre_g": gain((L, D_MODEL)),
        "ple_w_gate": w((L, D_MODEL, D_MODEL), D_MODEL),
        "ple_post_g": gain((L, D_MODEL)),
    }

def reference(x, p, ffn1_pre_g, ffn1_w_gate, ffn1_w_up, ffn1_w_down, ffn1_post_g,
              mix_pre_g, w_in, pool_w, pool_scale, w_pool_out,
              sgu_ln_g, sgu_ln_b, sgu_w_s, sgu_b_s, w_sgu_out,
              conv_dw_k, conv_dw_b, conv_ln_g, conv_ln_b, w_conv_out,
              w_out, mix_post_g,
              ffn2_pre_g, ffn2_w_gate, ffn2_w_up, ffn2_w_down, ffn2_post_g,
              ple_w_proj, ple_pre_g, ple_w_gate, ple_post_g):
    h = x
    b_, s_, _ = x.shape
    for i in range(DEPTH):
        f = swiglu(rms_norm(h, ffn1_pre_g[i]), ffn1_w_gate[i], ffn1_w_up[i], ffn1_w_down[i])
        h = h + 0.5 * rms_norm(f, ffn1_post_g[i])

        n = rms_norm(h, mix_pre_g[i])
        z = n @ w_in[i]
        z_pool = z[..., OFF_POOL:OFF_U]
        z_u = z[..., OFF_U:OFF_V]
        z_v = z[..., OFF_V:OFF_GLU_A]
        z_a = z[..., OFF_GLU_A:OFF_GLU_B]
        z_b = z[..., OFF_GLU_B:OFF_GATES]
        gates = jax.nn.sigmoid(z[..., OFF_GATES:]).reshape(b_, s_, N_BRANCH, D_MODEL)

        y_pool = pool_mixer(z_pool, pool_w[i], pool_scale[i]) @ w_pool_out[i]
        y_sgu = sgu_mixer(z_u, z_v, sgu_ln_g[i], sgu_ln_b[i], sgu_w_s[i], sgu_b_s[i]) @ w_sgu_out[i]
        y_conv = conv_mixer(z_a, z_b, conv_dw_k[i], conv_dw_b[i],
                            conv_ln_g[i], conv_ln_b[i]) @ w_conv_out[i]
        merged = gates[:, :, 0] * y_pool + gates[:, :, 1] * y_sgu + gates[:, :, 2] * y_conv
        h = h + rms_norm(merged @ w_out[i], mix_post_g[i])

        f = swiglu(rms_norm(h, ffn2_pre_g[i]), ffn2_w_gate[i], ffn2_w_up[i], ffn2_w_down[i])
        h = h + 0.5 * rms_norm(f, ffn2_post_g[i])

        e = p[i] @ ple_w_proj[i]
        g = jax.nn.sigmoid(rms_norm(h, ple_pre_g[i]) @ ple_w_gate[i])
        h = h + rms_norm(g * e, ple_post_g[i])
    return h


_drawn_inputs = setup_inputs


def setup_inputs(seed=0):
    import zlib

    import numpy as np

    out = dict(_drawn_inputs(seed))
    spreads = {}
    factors = {'sgu_ln_g': 4.472,
     'sgu_ln_b': 8.0,
     'conv_dw_b': 3.565,
     'conv_ln_g': 2.745,
     'conv_ln_b': 8.0,
     'ffn2_post_g': 3.133,
     'ple_pre_g': 4.16}
    for name, (base, spread) in spreads.items():
        noise = np.random.default_rng([zlib.crc32(name.encode()), seed]).standard_normal(out[name].shape)
        drawn = base * np.exp(spread * noise) if base else spread * noise
        out[name] = __import__('jax').numpy.asarray(drawn.astype(out[name].dtype))
    for name, factor in factors.items():
        out[name] = (out[name] * factor).astype(out[name].dtype)
    return out
```

```python
from contextlib import ExitStack

import concourse.bass as bass
from concourse import mybir

ALU = mybir.AluOpType
ACT = mybir.ActivationFunctionType
F32 = mybir.dt.float32
F32R = mybir.dt.float32r

P = 128
EPS = 1e-6
RING = 3
UNIT = 2048
BANK = 512
POOL_WINDOWS = (2, 4, 8, 16)


def hybrid_trunk(nc, A, out):
    DEPTH, D, F = A["ffn1_w_gate"].shape
    SEQ = A["x"].shape[1]
    TT = SEQ // P
    KD = D // P
    FC = 2 * P
    NCH = F // FC
    GR = len(POOL_WINDOWS)
    WB = A["w_pool_out"].shape[1]
    CB = WB // P
    TAPS = A["conv_dw_k"].shape[1]
    PAD = TAPS - 1
    PLE = A["p"].shape[3]
    assert (SEQ, D, NCH * FC, WB, PLE) == (2 * P, 8 * P, F, 4 * P, 2 * P) and NCH == 11

    FFN_UNITS = 3 * NCH
    U_FFN1 = 0
    U_MIX = U_FFN1 + FFN_UNITS
    U_V, U_GLU, U_POOL, U_U = U_MIX, U_MIX + 2, U_MIX + 6, U_MIX + 8
    n = U_U + 2
    U_GATE = [[n, n + 1, n + 2, n + 4], list(range(n + 7, n + 11)), list(range(n + 11, n + 15))]
    U_PW = n + 3
    U_OUT = [[n + 5, n + 6], [n + 15, n + 16], [n + 17, n + 18]]
    U_WOUT = n + 19
    U_FFN2 = U_WOUT + 4
    U_EMB = U_FFN2 + FFN_UNITS
    U_PLEG = U_EMB + 1
    UNITS = U_PLEG + 5
    assert UNITS % RING == 0 and U_FFN2 % RING == 0

    def width(n):
        n = n % UNITS
        return GR * P if n == U_PW else 1024 if n >= UNITS - 2 else UNIT

    with ExitStack() as ctx:
        def sb(name, shape, dt=F32):
            return ctx.enter_context(nc.sbuf_tensor(name, [P] + shape, dt))

        per_layer = {}

        def sem(name, per=None):
            s = ctx.enter_context(nc.semaphore(name))
            per_layer[name] = per
            sems[name] = s
            return name

        sems = {}

        def at(name, l, k, by=1):
            return l * (per_layer[name] * by) + k * by

        raw = sb("raw", [RING, UNIT])
        w_hi = sb("w_hi", [RING, UNIT], F32R)
        w_lo = sb("w_lo", [RING, UNIT], F32R)
        h = sb("h", [TT, D])
        xs = sb("xs", [TT, D])
        nt_hi = sb("nt_hi", [KD, SEQ], F32R)
        nt_lo = sb("nt_lo", [KD, SEQ], F32R)
        pre_gain = sb("pre_gain", [D])
        gain = sb("gain", [2, D])
        sg = sb("sg", [2, 2, SEQ])
        prod = sb("prod", [2, 2, SEQ])
        act_hi = sb("act_hi", [2, 2, SEQ], F32R)
        act_lo = sb("act_lo", [2, 2, SEQ], F32R)
        xg = sb("xg", [CB, PAD + SEQ])
        acc = sb("acc", [CB, SEQ])
        gates = sb("gates", [KD, SEQ])
        merged = sb("merged", [KD, SEQ])
        y_hi = sb("y_hi", [3, CB, SEQ], F32R)
        y_lo = sb("y_lo", [3, CB, SEQ], F32R)
        u = sb("u", [CB, SEQ])
        ctmp = sb("ctmp", [CB, SEQ])
        wst_hi = sb("wst_hi", [4, P], F32R)
        wst_lo = sb("wst_lo", [4, P], F32R)
        bs = sb("bs", [4, P])
        vln_g = sb("vln_g", [WB])
        vln_b = sb("vln_b", [WB])
        pt_hi = sb("pt_hi", [2, SEQ], F32R)
        pt_lo = sb("pt_lo", [2, SEQ], F32R)
        ident = sb("ident", [P])
        ones = sb("ones", [P])
        mean_w = sb("mean_w", [P])
        diag = sb("diag", [TT, P])
        inv = sb("inv", [GR, 16])
        minus_half = sb("minus_half", [1])
        ss = sb("ss", [8, TT])
        ms = sb("ms", [8, TT])
        rs = sb("rs", [8, TT])
        vst = sb("vst", [TT, 6])
        vmv = sb("vmv", [TT, 2])
        vms = sb("vms", [TT])
        vrs = sb("vrs", [TT])
        cvar = sb("cvar", [TT])
        crs = sb("crs", [TT])
        VECS = ("pool_scale", "conv_dw_b", "conv_ln_g", "conv_ln_b")
        NV = len(VECS)
        vec4 = sb("vec4", [NV, CB])
        tap = sb("tap", [TAPS, CB])
        vec_rows = u[:, 0, 0:P]
        tap_rows = u[:, 1, 0:P]
        ws = ctmp[:, 0:2, :].rearrange("p c (h s) -> p (c h) s", h=2)
        p_in = ctmp[:, 2:4, :]
        pooled = merged[:, 0:CB, :]
        gate_of = lambda b, m: (gates[:, m:m + 4, :] if b != 1 else (sum_a, sum_b)[m // 4][:, 0:4, :])
        sum_a = sg[:, :, :, :].rearrange("p a b n -> p (a b) n")
        sum_b = prod[:, :, :, :].rearrange("p a b n -> p (a b) n")
        pl_hi = act_hi[:, :, :, :].rearrange("p a b n -> p (a b) n")
        pl_lo = act_lo[:, :, :, :].rearrange("p a b n -> p (a b) n")
        vf = xs[:, 0, :].rearrange("p (t n) -> p t n", t=TT)
        us = xs[:, 0, :].rearrange("p (c n) -> p c n", c=CB)
        s1 = xs[:, 1, :].rearrange("p (c n) -> p c n", c=CB)
        v_hi = y_hi[:, 2, :, :].rearrange("p c n -> p (c n)").rearrange("p (t n) -> p t n", t=TT)
        v_lo = y_lo[:, 2, :, :].rearrange("p c n -> p (c n)").rearrange("p (t n) -> p t n", t=TT)
        ge = merged[:, :, :].rearrange("p k n -> p (k n)").rearrange("p (t n) -> p t n", t=TT)

        ps = ctx.enter_context(nc.psum_tensor("ps", [P, 8, BANK], F32))

        def pair(b):
            return ps[:, b, :].rearrange("p (c n) -> p c n", c=2)

        def gate_bank(c):
            return 4 + 2 * (c % 2)

        def up_bank(c):
            return 5 + 2 * (c % 2)

        def quads(base, t, b):
            return ps[:, base + 2 * t + b, :].rearrange("p (k n) -> p k n", k=4)

        def rows(t, base=0):
            return ps[:, base + 2 * t:base + 2 * t + 2, :].rearrange("p b n -> p (b n)")

        landed = [sem(f"landed{s}", UNITS // RING) for s in range(RING)]
        for name, per in {
            "w_hi_ready": UNITS, "w_lo_ready": UNITS, "unit_done": UNITS,
            "h_ready": 8, "ssq_ready": 16, "ms_ready": 16, "rstd_ready": 16, "xn_ready": 8,
            "xt_done": 16, "nt_hi_ready": 16, "nt_lo_ready": 16, "pre_gain_landed": 4, "row_scaled": 8, "tile0_done": 4,
            "vecs_ready": 2, "vecs_turned": 1, "vec_landed": NV + 1,
            "sg_ready": 2 * NCH, "gate_read": 2 * NCH, "prod_ready": 2 * NCH,
            "act_hi_ready": 2 * NCH, "act_lo_ready": 2 * NCH,
            "ws_landed": 1, "ws_masked": 1, "p_landed": 1, "gain_landed0": 2, "gain_landed1": 2,
            "rowvecs_landed": 3, "prep_done": 2, "prep_hi": 2, "prep_lo": 2,
            "glu_sig": 2, "xg_ready": 2, "px_ready": 2, "dve_step": 0, "pooled_ready": 1,
            "pooled_hi": 1, "pooled_lo": 1, "v_gelu": 2, "v_stats": 2, "v_ready": 1,
            "v_ms": 2, "v_rstd": 2, "v_hi_ready": 1, "v_lo_ready": 1,
            "u_gelu": 2, "yp_hi": 4, "yp_lo": 4, "act_turned": 2,
            "s_done": 1, "us_ready": 1, "us_hi": 1, "us_lo": 1,
            "gate_sig": 12, "out_read": 6, "merged_ready": 4, "mg_hi": 2, "mg_lo": 2,
            "tap_added": TAPS * CB, "stat_done": 3, "centred": 1, "csq_ready": 1, "cvar_ready": 1,
            "crstd_ready": 1, "diag_ready": 1, "z_ready": 1, "zsig_ready": 1,
            "conv_y": 1, "cy_hi": 1, "cy_lo": 1,
            "ple_sig": 2, "ge_ready": 2,
            "x_landed": 0, "zero_ready": 0, "ident_ready": 0, "const_ready": 0,
            "inv_ready": 0, "stored": 0,
            "sp_waited": 0, "pool_waited": 0, "dve_waited": 0, "pe_waited": 0,
        }.items():
            sem(name, per)
        S = sems
        DVE_STEPS = 12
        per_layer["dve_step"] = DVE_STEPS

        NORM_IN = (0, 2, 4, 6)
        NORM_OUT = (1, 3, 5, 7)

        def sums(name, l, q, k):
            return at(name, l, 4 * q + k) + TT

        def landing(n):
            return n % RING, n // RING + 1

        def after(eng, name):
            eng.sem_inc(S[name], 1)

        block = ctx.enter_context(nc.Block())

        @block.sync
        def _(sp):
            def load(src, l, n, first=False, wait=None):
                s = n % RING
                if not first:
                    sp.wait_ge(S["w_lo_ready"], at("w_lo_ready", l, n - 2) if wait is None else wait)
                    after(sp, "sp_waited")
                k = src.shape[1]
                dst = raw[:, s, 0:k * src.shape[2]].rearrange("p (k n) -> p k n", k=k)
                sp.dma_start(dst, src).then_inc(S[landed[s]], 16)

            def cols(name, l, c, n):
                w = A[name]
                return w[bass.ds(l, 1), :, bass.ds(c, n)].rearrange("o (k p) n -> p (o k) n", p=P)

            def rws(name, l, r, n):
                w = A[name]
                return w[bass.ds(l, 1), bass.ds(r, n), :].rearrange("o (k p) n -> p (o k) n", p=P)

            def ffn(l, f, base):
                g, u_, d = f"{f}_w_gate", f"{f}_w_up", f"{f}_w_down"
                if f == "ffn2":
                    load(cols(g, l, 0, FC), l, base)
                    load(cols(u_, l, 0, FC), l, base + 1)
                    load(cols(g, l, FC, FC), l, base + 2)
                load(cols(u_, l, FC, FC), l, base + 3)
                load(rws(d, l, 0, FC), l, base + 4)
                with sp.Fori(0, (NCH - 3) // 2) as i:
                    for k in range(2):
                        n = base + 5 + 3 * k
                        lo = at("w_lo_ready", l, n - 2) + i * 6
                        load(cols(g, l, i * (2 * FC) + (2 + k) * FC, FC), l, n, wait=lo)
                        load(cols(u_, l, i * (2 * FC) + (2 + k) * FC, FC), l, n + 1, wait=lo + 1)
                        load(rws(d, l, i * (2 * FC) + (1 + k) * FC, FC), l, n + 2, wait=lo + 2)
                load(cols(g, l, (NCH - 1) * FC, FC), l, base + 3 * NCH - 4)
                load(cols(u_, l, (NCH - 1) * FC, FC), l, base + 3 * NCH - 3)
                load(rws(d, l, (NCH - 2) * FC, FC), l, base + 3 * NCH - 2)
                load(rws(d, l, (NCH - 1) * FC, FC), l, base + 3 * NCH - 1)

            def first_units(l, first):
                load(cols("ffn1_w_gate", l, 0, FC), l, 0, first)
                load(cols("ffn1_w_up", l, 0, FC), l, 1, first)
                load(cols("ffn1_w_gate", l, FC, FC), l, 2, first)

            sp.dma_start(xs[:, :, :], A["x"][0].rearrange("(t p) n -> p t n", p=P)).then_inc(S["x_landed"], 16)
            first_units(0, True)
            with sp.Fori(0, DEPTH) as l:
                ffn(l, "ffn1", U_FFN1)
                OFF_U, OFF_V, OFF_A, OFF_B, OFF_G = WB, 2 * WB, 3 * WB, 4 * WB, 5 * WB
                blocks = [OFF_V, OFF_V + FC, OFF_A, OFF_B, OFF_A + FC, OFF_B + FC, 0, FC, OFF_U, OFF_U + FC]
                for k, c in enumerate(blocks):
                    load(cols("w_in", l, c, FC), l, U_V + k)
                for b, name in enumerate(("w_pool_out", "w_sgu_out", "w_conv_out")):
                    if b < 2:
                        branches = [b] if b == 0 else [1, 2]
                        for bb in branches:
                            for k, n in enumerate(U_GATE[bb]):
                                if n == U_PW + 1:
                                    load(A["pool_w"][bass.ds(l, 1)].rearrange("o g i n -> i (o g) n"), l, U_PW)
                                load(cols("w_in", l, OFF_G + bb * D + k * FC, FC), l, n)
                    for k, n in enumerate(U_OUT[b]):
                        load(cols(name, l, k * BANK, BANK), l, n)
                for k in range(4):
                    load(rws("w_out", l, k * FC, FC), l, U_WOUT + k)
                ffn(l, "ffn2", U_FFN2)
                load(rws("ple_w_proj", l, 0, PLE), l, U_EMB)
                for k in range(3):
                    load(rws("ple_w_gate", l, k * FC, FC), l, U_PLEG + k)
                for k in range(2):
                    load(rws("ple_w_gate", l, 3 * FC + k * P, P), l, U_PLEG + 3 + k)
                with sp.If(DEPTH - 1 - l):
                    first_units(nc.s_assert_within(
                        l + 1, 1, DEPTH - 1, skip_runtime_bounds_check_because="this If runs below the last layer only"), False)
            o = out[0].rearrange("(t p) n -> t p n", p=P)
            for t in range(TT):
                sp.wait_ge(S["h_ready"], 8 * DEPTH + t + 1)
                sp.dma_start(o[t], h[:, t, :]).then_inc(S["stored"], 16)
            sp.wait_ge(S["stored"], 16 * TT)

        @block.gpsimd
        def _(pool):
            g = nc.gpsimd
            g.memset(ident[:, :], 1.0).then_inc(S["zero_ready"], 1)
            g.memset(minus_half[:, :], -0.5).then_inc(S["const_ready"], 1)
            pool.wait_ge(S["zero_ready"], 1)
            g.affine_select(out=ident[:, :], in_=ident[:, :], compare_op=ALU.is_equal, fill=0.0, base=0,
                            pattern=[[-1, P]], channel_multiplier=1).then_inc(S["ident_ready"], 1)
            g.memset(ones[:, :], 1.0).then_inc(S["const_ready"], 1)
            g.memset(mean_w[:, :], 1.0 / WB).then_inc(S["const_ready"], 1)
            for j in range(16):
                last = g.memset(inv[:, GR - 1, j:j + 1], 1.0 / (j + 1))
            last.then_inc(S["inv_ready"], 1)
            pool.wait_ge(S["const_ready"], 1)

            def rstd(e, t, val):
                pool.wait_ge(S["ssq_ready"], val)
                after(pool, "pool_waited")
                g.tensor_scalar(ms[:, e, t:t + 1], ss[:, e, t:t + 1], 1.0 / D, EPS, ALU.mult, ALU.add
                                ).then_inc(S["ms_ready"], 1)
                pool.wait_ge(S["ms_ready"], val)
                g.tensor_tensor(rs[:, e, t:t + 1], ms[:, e, t:t + 1], minus_half[:, :], ALU.pow
                                ).then_inc(S["rstd_ready"], 1)

            def boundary(l, q):
                for t in range(TT):
                    rstd(NORM_OUT[q], t, sums("ssq_ready", l, q, 2 * t + 1))
                    rstd(NORM_IN[(q + 1) % 4], t, sums("ssq_ready", l, q, 2 * t + 2))

            def row(name, l):
                v = A[name]
                return v[bass.ds(l, 1), :].broadcast_to([P, v.shape[1]])

            def load_gain(dst, name, l, landed_):
                pool.dma_start(dst, row(name, l)).then_inc(S[landed_], 16)

            def load_pre_gain(name, l, l_before, s_before):
                if s_before is not None:
                    pool.wait_ge(S["xn_ready"], at("xn_ready", l_before, 2 * s_before + TT))
                    after(pool, "pool_waited")
                load_gain(pre_gain[:, :], name, l, "pre_gain_landed")

            def small_loads(l):
                pool.dma_start(ws, A["sgu_w_s"][bass.ds(l, 1)].rearrange("o h t s -> t (o h) s")
                               ).then_inc(S["ws_landed"], 16)
                pool.dma_start(p_in, A["p"][bass.ds(l, 1), 0].rearrange("o (t q) n -> q (o t) n", q=P)
                               ).then_inc(S["p_landed"], 16)
                for k, name in enumerate(VECS):
                    pool.dma_start(vec_rows[k * CB:(k + 1) * CB, :], A[name][bass.ds(l, 1), :]
                                   .rearrange("o (k p) -> (o k) p", p=P)).then_inc(S["vec_landed"], 16)
                pool.dma_start(tap_rows[0:TAPS * CB, :], A["conv_dw_k"][bass.ds(l, 1)]
                               .rearrange("a t o (c p) -> (a t o c) p", p=P)).then_inc(S["vec_landed"], 16)
                pool.dma_start(vln_g[:, :], row("sgu_ln_g", l)).then_inc(S["rowvecs_landed"], 16)
                pool.dma_start(vln_b[:, :], row("sgu_ln_b", l)).then_inc(S["rowvecs_landed"], 16)
                pool.dma_start(bs[:, :, :], A["sgu_b_s"][bass.ds(l, 1)].rearrange("o h t -> o (h t)")
                               .broadcast_to([P, 4 * P]).rearrange("p (h t) -> p h t", h=4)
                               ).then_inc(S["rowvecs_landed"], 16)

            def mask(l):
                pool.wait_ge(S["ws_landed"], at("ws_landed", l, 1, 16))
                after(pool, "pool_waited")
                g.affine_select(out=ws, in_=ws, compare_op=ALU.is_ge, fill=0.0, base=0,
                                pattern=[[0, 4], [-1, P]], channel_multiplier=1).then_inc(S["ws_masked"], 1)

            load_pre_gain("ffn1_pre_g", 0, None, None)
            for t in range(TT):
                rstd(NORM_IN[0], t, t + 1)
            load_pre_gain("mix_pre_g", 0, 0, 0)
            small_loads(0)
            load_gain(gain[:, 0, :], "ffn1_post_g", 0, "gain_landed0")
            load_gain(gain[:, 1, :], "mix_post_g", 0, "gain_landed1")
            mask(0)
            with pool.Fori(0, DEPTH) as l:
                boundary(l, 0)
                load_pre_gain("ffn2_pre_g", l, l, 1)
                load_gain(gain[:, 0, :], "ffn2_post_g", l, "gain_landed0")
                for t in range(TT):
                    pool.wait_ge(S["v_stats"], at("v_stats", l, t + 1))
                    after(pool, "pool_waited")
                    g.tensor_scalar(vms[:, t:t + 1], vmv[:, t, 1:2], 1.0, EPS, ALU.mult, ALU.add
                                    ).then_inc(S["v_ms"], 1)
                    pool.wait_ge(S["v_ms"], at("v_ms", l, t + 1))
                    g.tensor_tensor(vrs[:, t:t + 1], vms[:, t:t + 1], minus_half[:, :], ALU.pow
                                    ).then_inc(S["v_rstd"], 1)
                pool.wait_ge(S["cvar_ready"], at("cvar_ready", l, 1))
                g.tensor_tensor(crs[:, :], cvar[:, :], minus_half[:, :].broadcast_to([P, TT]), ALU.pow
                                ).then_inc(S["crstd_ready"], 1)
                boundary(l, 1)
                load_pre_gain("ple_pre_g", l, l, 2)
                load_gain(gain[:, 1, :], "ple_post_g", l, "gain_landed1")
                boundary(l, 2)
                with pool.If(DEPTH - 1 - l):
                    following = nc.s_assert_within(
                        l + 1, 1, DEPTH - 1, skip_runtime_bounds_check_because="this If runs below the last layer only")
                    load_pre_gain("ffn1_pre_g", following, l, 3)
                    load_gain(gain[:, 0, :], "ffn1_post_g", following, "gain_landed0")
                    small_loads(following)
                    mask(l + 1)
                    boundary(l, 3)
                    load_pre_gain("mix_pre_g", following, l + 1, 0)
                    load_gain(gain[:, 1, :], "mix_post_g", following, "gain_landed1")
                with pool.Else():
                    for t in range(TT):
                        rstd(NORM_OUT[3], t, sums("ssq_ready", l, 3, t + 1))

        @block.scalar
        def _(act):
            sc = nc.scalar

            def split(l, n, ud=None, ld=None):
                s, k = landing(n)
                act.wait_ge(S[landed[s]], at(landed[s], l, k, 16) if ld is None else ld)
                if ud is not False:
                    act.wait_ge(S["unit_done"], at("unit_done", l, n - 2) if ud is None else ud)
                w = width(n)
                sc.activation(w_hi[:, s, 0:w], raw[:, s, 0:w], ACT.Copy).then_inc(S["w_hi_ready"], 1)

            def square_in(l, s, t):
                act.wait_ge(S["h_ready"], at("h_ready", l, 2 * s + t + 1))
                sc.activation(xs[:, t, :], h[:, t, :], ACT.Square, accum_out=ss[:, NORM_IN[s], t:t + 1]
                              ).then_inc(S["ssq_ready"], 1)

            def square_out(s, t, source, name, val):
                act.wait_ge(S[name], val)
                sc.activation(xs[:, t, :], source, ACT.Square, accum_out=ss[:, NORM_OUT[s], t:t + 1]
                              ).then_inc(S["ssq_ready"], 1)

            def rows_hi(l, s, t):
                base = 0 if s == 3 else 4
                for b in range(2):
                    act.wait_ge(S["xt_done"], at("xt_done", l, 4 * s + 2 * t + b + 1))
                    sc.activation(nt_hi[:, 4 * b:4 * b + 4, t * P:(t + 1) * P], quads(base, t, b), ACT.Copy
                                  ).then_inc(S["nt_hi_ready"], 1)

            def boundary(l, q, a):
                square_out(q, 0, rows(0), "tile0_done", at("tile0_done", l, q + 1))
                split(l, a + 3)
                square_in(l, q + 1, 0)
                square_out(q, 1, rows(1), "unit_done", at("unit_done", l, a + 2))
                rows_hi(l, q + 1, 0)
                square_in(l, q + 1, 1)
                split(l, a + 4)
                rows_hi(l, q + 1, 1)

            def sigmoid_gate(l, c, par, n_done, j):
                act.wait_ge(S["unit_done"], n_done)
                sc.activation(sg[:, par, :, :], pair(gate_bank(par)), ACT.Sigmoid).then_inc(S["sg_ready"], 1)

            def chunk_hi(par, prod_val, free_val):
                act.wait_ge(S["prod_ready"], prod_val)
                if free_val is not None:
                    act.wait_ge(S["unit_done"], free_val)
                sc.activation(act_hi[:, par, :, :], prod[:, par, :, :], ACT.Copy).then_inc(S["act_hi_ready"], 1)

            def ffn(l, f, base):
                c0 = NCH * f

                def chunk(c, n, off=0, loff=0, freed=None, coff=0):
                    par = c % 2
                    sigmoid_gate(l, c, par, at("unit_done", l, n + 1) + off, 0)
                    s, k = landing(n + 3)
                    split(l, n + 3, ud=False, ld=at(landed[s], l, k, 16) + loff)
                    s, k = landing(n + 4)
                    if c == NCH - 1:
                        chunk_hi(par, at("prod_ready", l, c0 + c + 1) + coff, freed)
                    split(l, n + 4, ud=at("unit_done", l, n + 2) + off, ld=at(landed[s], l, k, 16) + loff)
                    if c < NCH - 1:
                        chunk_hi(par, at("prod_ready", l, c0 + c + 1) + coff, freed)

                def down(n, off=0, loff=0):
                    s, k = landing(n + 3)
                    split(l, n + 3, ud=at("unit_done", l, n + 1) + off, ld=at(landed[s], l, k, 16) + loff)

                sigmoid_gate(l, 0, 0, at("unit_done", l, base + 1), 0)
                split(l, base + 3, ud=False)
                if f == 0:
                    for k, (dst, b) in enumerate(((wst_hi[:, :, :], 1), (pt_hi[:, :, :], 2))):
                        act.wait_ge(S["prep_done"], at("prep_done", l, k + 1))
                        src = ps[:, b, :].rearrange("p (c n) -> p c n", c=dst.shape[1])
                        sc.activation(dst, src, ACT.Copy).then_inc(S["prep_hi"], 1)
                split(l, base + 4)
                act.wait_ge(S["act_turned"], at("act_turned", l, f + 1))
                sc.activation(act_hi[:, 0, :, :], pair(gate_bank(0)), ACT.Copy).then_inc(S["act_hi_ready"], 1)
                chunk(1, base + 2)
                down(base + 4)
                with act.Fori(0, (NCH - 3) // 2) as i:
                    for k in range(2):
                        n = base + 5 + 3 * k
                        chunk(2 + k, n, off=i * 6, loff=i * (2 * 16), coff=i * 2,
                              freed=at("unit_done", l, n) + i * 6)
                        down(n + 2, off=i * 6, loff=i * (2 * 16))
                n = base + 3 * NCH - 4
                chunk(NCH - 1, n, freed=at("unit_done", l, n))
                boundary(l, 2 * f, n + 2)

            split(0, 0, ud=False)
            for t in range(TT):
                square_in(0, 0, t)
            split(0, 1, ud=False)
            for t in range(TT):
                rows_hi(0, 0, t)
            split(0, 2, ud=False)
            with act.Fori(0, DEPTH) as l:
                ffn(l, 0, U_FFN1)
                split(l, U_V + 3)
                act.wait_ge(S["unit_done"], at("unit_done", l, U_V + 2))
                for t in range(TT):
                    sc.activation(vf[:, t, :], ps[:, 4 + t, :], ACT.Gelu).then_inc(S["v_gelu"], 1)
                split(l, U_V + 4)
                for i in range(2):
                    split(l, U_GLU + 2 * i + 3)
                    act.wait_ge(S["unit_done"], at("unit_done", l, U_GLU + 2 * i + 2))
                    sc.activation(ctmp[:, 2 * i:2 * i + 2, :], pair(2 * i + 1), ACT.Sigmoid
                                  ).then_inc(S["glu_sig"], 1)
                    split(l, U_GLU + 2 * i + 4)
                act.wait_ge(S["v_ready"], at("v_ready", l, 1))
                sc.activation(v_hi, vf, ACT.Copy).then_inc(S["v_hi_ready"], 1)
                for i in range(2):
                    act.wait_ge(S["unit_done"], at("unit_done", l, U_POOL + i + 1))
                    sc.activation(pooled[:, 2 * i:2 * i + 2, :], pair(6 + i), ACT.Copy).then_inc(S["px_ready"], 1)
                    split(l, U_POOL + i + 3)
                for i in range(2):
                    act.wait_ge(S["unit_done"], at("unit_done", l, U_U + i + 1))
                    sc.activation(u[:, 2 * i:2 * i + 2, :], pair(i), ACT.Gelu).then_inc(S["u_gelu"], 1)
                    split(l, U_U + i + 3)
                act.wait_ge(S["pooled_ready"], at("pooled_ready", l, 1))
                sc.activation(pl_hi, pooled, ACT.Copy).then_inc(S["pooled_hi"], 1)
                for b in range(3):
                    for k, n in enumerate(U_GATE[b]):
                        act.wait_ge(S["unit_done"], at("unit_done", l, n + 1))
                        if b == 1 and k == 0:
                            act.wait_ge(S["pooled_ready"], at("pooled_ready", l, 1))
                        if b == 2 and k % 2 == 0:
                            act.wait_ge(S["out_read"], at("out_read", l, k // 2 + 1))
                        sc.activation(gate_of(b, 4 * (k // 2))[:, 2 * (k % 2):2 * (k % 2) + 2, :],
                                      pair(6 + k % 2), ACT.Sigmoid).then_inc(S["gate_sig"], 1)
                        split(l, n + 3)
                        if n == U_PW - 1:
                            act.wait_ge(S["unit_done"], at("unit_done", l, U_PW + 1))
                            for i in range(GR):
                                sc.activation(y_hi[:, 0, i, :], pair(2 + i // 2)[:, i % 2, :], ACT.Copy,
                                              scale=vec4[:, 0, i:i + 1]).then_inc(S["yp_hi"], 1)
                            split(l, U_PW + 3)
                        if b == 1 and k == 1:
                            act.wait_ge(S["us_ready"], at("us_ready", l, 1))
                            sc.activation(y_hi[:, 1, :, :], us, ACT.Copy).then_inc(S["us_hi"], 1)
                    if b == 0:
                        for n in U_OUT[0]:
                            split(l, n + 3)
                act.wait_ge(S["centred"], at("centred", l, 1))
                sc.activation(ctmp[:, :, :], acc[:, :, :], ACT.Square).then_inc(S["csq_ready"], 1)
                split(l, U_OUT[1][0] + 3)
                act.wait_ge(S["z_ready"], at("z_ready", l, 1))
                for c in range(CB):
                    last = sc.activation(ctmp[:, c, :], acc[:, c, :], ACT.Sigmoid,
                                         bias=vec4[:, 3, c:c + 1], scale=vec4[:, 2, c:c + 1])
                last.then_inc(S["zsig_ready"], 1)
                act.wait_ge(S["conv_y"], at("conv_y", l, 1))
                sc.activation(y_hi[:, 2, :, :], xs[:, 0, :].rearrange("p (c n) -> p c n", c=CB),
                              ACT.Copy).then_inc(S["cy_hi"], 1)
                split(l, U_OUT[1][1] + 3)
                for k, n in enumerate(U_OUT[2]):
                    split(l, n + 3)
                    act.wait_ge(S["merged_ready"], at("merged_ready", l, 2 + k + 1))
                    sc.activation(nt_hi[:, 4 * k:4 * k + 4, :], merged[:, 4 * k:4 * k + 4, :], ACT.Copy
                                  ).then_inc(S["mg_hi"], 1)
                for k in range(2):
                    split(l, U_WOUT + k + 3)
                boundary(l, 1, U_WOUT + 2)
                ffn(l, 1, U_FFN2)
                split(l, U_EMB + 3)
                for k in range(2):
                    split(l, U_PLEG + k + 3)

                def gate_sigmoid(t):
                    if t == 0:
                        act.wait_ge(S["tile0_done"], at("tile0_done", l, 4))
                    else:
                        act.wait_ge(S["unit_done"], at("unit_done", l, UNITS))
                    sc.activation(ge[:, t, :], rows(t), ACT.Sigmoid).then_inc(S["ple_sig"], 1)

                gate_sigmoid(0)
                with act.If(DEPTH - 1 - l):
                    split(l, UNITS)
                    square_out(3, 0, ge[:, 0, :], "ge_ready", at("ge_ready", l, 1))
                    gate_sigmoid(1)
                    square_in(l + 1, 0, 0)
                    square_out(3, 1, ge[:, 1, :], "ge_ready", at("ge_ready", l, 2))
                    split(l, UNITS + 1)
                    rows_hi(l + 1, 0, 0)
                    square_in(l + 1, 0, 1)
                    split(l, UNITS + 2)
                    rows_hi(l + 1, 0, 1)
                with act.Else():
                    square_out(3, 0, ge[:, 0, :], "ge_ready", at("ge_ready", l, 1))
                    gate_sigmoid(1)
                    square_out(3, 1, ge[:, 1, :], "ge_ready", at("ge_ready", l, 2))

        @block.vector
        def _(dve):
            v = nc.vector

            def split(l, n, hi=None):
                s, w = n % RING, width(n)
                dve.wait_ge(S["w_hi_ready"], at("w_hi_ready", l, n + 1) if hi is None else hi)
                v.tensor_tensor(w_lo[:, s, 0:w], raw[:, s, 0:w], w_hi[:, s, 0:w].bitcast(F32), ALU.subtract
                                ).then_inc(S["w_lo_ready"], 1)

            def scale_rows(l, s, t, val):
                e = NORM_IN[s]
                dve.wait_ge(S["rstd_ready"], val)
                if t == 0:
                    dve.wait_ge(S["pre_gain_landed"], at("pre_gain_landed", l, s + 1, 16))
                v.scalar_tensor_tensor(xs[:, t, :], h[:, t, :], rs[:, e, t:t + 1], pre_gain[:, :], ALU.mult, ALU.mult
                                       ).then_inc(S["xn_ready"], 1)

            def rows_lo(l, s, t):
                base = 0 if s == 3 else 4
                for b in range(2):
                    dve.wait_ge(S["nt_hi_ready"], at("nt_hi_ready", l, 4 * s + 2 * t + b + 1))
                    part = (slice(None), slice(4 * b, 4 * b + 4), slice(t * P, (t + 1) * P))
                    v.tensor_tensor(nt_lo[part], quads(base, t, b), nt_hi[part].bitcast(F32), ALU.subtract
                                    ).then_inc(S["nt_lo_ready"], 1)

            def add_rows(l, s, t, weight, source, gain_slot, val):
                e = NORM_OUT[s]
                dve.wait_ge(S["rstd_ready"], val)
                v.scalar_tensor_tensor(xs[:, t, :], source, rs[:, e, t:t + 1], gain[:, gain_slot, :],
                                       ALU.mult, ALU.mult).then_inc(S["row_scaled"], 1)
                dve.wait_ge(S["row_scaled"], at("row_scaled", l, 2 * s + t + 1))
                v.scalar_tensor_tensor(h[:, t, :], xs[:, t, :], weight, h[:, t, :], ALU.mult, ALU.add
                                       ).then_inc(S["h_ready"], 1)

            def boundary(l, q, a, weight):
                slot, count = q % 2, q // 2 + 1
                dve.wait_ge(S[f"gain_landed{slot}"], at(f"gain_landed{slot}", l, count, 16))
                add_rows(l, q, 0, weight, rows(0), slot, sums("rstd_ready", l, q, 1))
                split(l, a + 3)
                scale_rows(l, q + 1, 0, sums("rstd_ready", l, q, 2))
                add_rows(l, q, 1, weight, rows(1), slot, sums("rstd_ready", l, q, 3))
                rows_lo(l, q + 1, 0)
                scale_rows(l, q + 1, 1, sums("rstd_ready", l, q, 4))
                split(l, a + 4)
                rows_lo(l, q + 1, 1)

            def ffn(l, f, base):
                c0 = NCH * f

                def prepare():
                    dve.wait_ge(S["vecs_turned"], at("vecs_turned", l, 1))
                    v.tensor_copy(vec4[:, :, :], ps[:, 0, 0:NV * CB].rearrange("p (a c) -> p a c", a=NV)
                                  ).then_inc(S["vecs_ready"], 1)
                    v.tensor_copy(tap[:, :, :], ps[:, 0, P:P + TAPS * CB].rearrange("p (a c) -> p a c", c=CB)
                                  ).then_inc(S["vecs_ready"], 1)
                    for k, (hi, lo, b) in enumerate(((wst_hi, wst_lo, 1), (pt_hi, pt_lo, 2))):
                        dve.wait_ge(S["prep_hi"], at("prep_hi", l, k + 1))
                        src = ps[:, b, :].rearrange("p (c n) -> p c n", c=hi.shape[1])
                        v.tensor_tensor(lo[:, :, :], src, hi[:, :, :].bitcast(F32), ALU.subtract
                                        ).then_inc(S["prep_lo"], 1)

                def chunk(c, n, off=0, coff=0):
                    par = c % 2
                    dve.wait_ge(S["sg_ready"], at("sg_ready", l, c0 + c + 1) + coff)
                    v.tensor_tensor(sg[:, par, :, :], sg[:, par, :, :], pair(gate_bank(par)), ALU.mult
                                    ).then_inc(S["gate_read"], 1)
                    split(l, n + 3, hi=at("w_hi_ready", l, n + 4) + off)
                    dve.wait_ge(S["unit_done"], at("unit_done", l, n + 2) + off)
                    dve.wait_ge(S["gate_read"], at("gate_read", l, c0 + c + 1) + coff)
                    v.tensor_tensor(prod[:, par, :, :], sg[:, par, :, :], pair(up_bank(par)), ALU.mult
                                    ).then_inc(S["prod_ready"], 1)
                    if c == 0 and f == 0:
                        prepare()
                    if c < NCH - 1:
                        split(l, n + 4, hi=at("w_hi_ready", l, n + 5) + off)
                    dve.wait_ge(S["act_hi_ready"], at("act_hi_ready", l, c0 + c + 1) + coff)
                    whole = pair(gate_bank(0)) if c == 0 else prod[:, par, :, :]
                    v.tensor_tensor(act_lo[:, par, :, :], whole, act_hi[:, par, :, :].bitcast(F32),
                                    ALU.subtract).then_inc(S["act_lo_ready"], 1)
                    if c == NCH - 1:
                        split(l, n + 4)

                chunk(0, base)
                chunk(1, base + 2)
                split(l, base + 7)
                with dve.Fori(0, (NCH - 3) // 2) as i:
                    for k in range(2):
                        n = base + 5 + 3 * k
                        chunk(2 + k, n, off=i * 6, coff=i * 2)
                        split(l, n + 5, hi=at("w_hi_ready", l, n + 6) + i * 6)
                n = base + 3 * NCH - 4
                chunk(NCH - 1, n)
                boundary(l, 2 * f, n + 2, 0.5)

            v.memset(xg[:, :, 0:PAD], 0.0)
            dve.wait_ge(S["inv_ready"], 1)
            for gi in range(GR - 1):
                last = v.tensor_scalar(inv[:, gi, :], inv[:, GR - 1, :], 1.0 / POOL_WINDOWS[gi], None, ALU.max)
            last.then_inc(S["const_ready"], 1)
            dve.wait_ge(S["x_landed"], 16)
            for t in range(TT):
                v.tensor_copy(h[:, t, :], xs[:, t, :]).then_inc(S["h_ready"], 1)
            split(0, 0)
            for t in range(TT):
                scale_rows(0, 0, t, t + 1)
            split(0, 1)
            for t in range(TT):
                rows_lo(0, 0, t)
            split(0, 2)

            with dve.Fori(0, DEPTH) as l:
                ffn(l, 0, U_FFN1)

                jobs = [(j, c) for half in range(2) for j in range(TAPS) for c in (2 * half, 2 * half + 1)]
                total = len(jobs)

                def convolve(count):
                    if not jobs:
                        return
                    for _ in range(min(count, len(jobs))):
                        j, c = jobs.pop(0)
                        src = xg[:, c, j:j + SEQ]
                        if j > 0:
                            dve.wait_ge(S["tap_added"], at("tap_added", l, total - len(jobs) - 2))
                        if j == 0:
                            ins = v.tensor_scalar(acc[:, c, :], src, tap[:, 0, c:c + 1], vec4[:, 1, c:c + 1],
                                                  ALU.mult, ALU.add)
                        else:
                            ins = v.scalar_tensor_tensor(acc[:, c, :], src, tap[:, j, c:c + 1], acc[:, c, :],
                                                         ALU.mult, ALU.add)
                        ins.then_inc(S["tap_added"], 1)

                steps = [0]

                def step(ins):
                    steps[0] += 1
                    ins.then_inc(S["dve_step"], 1)

                def steps_done():
                    dve.wait_ge(S["dve_step"], at("dve_step", l, steps[0]))

                split(l, U_V + 3)
                for t in range(TT):
                    dve.wait_ge(S["v_gelu"], at("v_gelu", l, t + 1))
                    step(v.bn_stats(vst[:, t, :], vf[:, t, :]))
                steps_done()
                after(dve, "dve_waited")
                for t in range(TT):
                    v.bn_aggr(vmv[:, t, :], vst[:, t, :]).then_inc(S["v_stats"], 1)
                split(l, U_V + 4)
                dve.wait_ge(S["rowvecs_landed"], at("rowvecs_landed", l, 3, 16))
                dve.wait_ge(S["v_stats"], at("v_stats", l, 2))
                for t in range(TT):
                    step(v.scalar_tensor_tensor(vf[:, t, :], vf[:, t, :], vmv[:, t, 0:1], vln_g[:, :],
                                                ALU.subtract, ALU.mult))
                split(l, U_GLU + 3)
                steps_done()
                dve.wait_ge(S["v_rstd"], at("v_rstd", l, 2))
                for t in range(TT):
                    last = v.scalar_tensor_tensor(vf[:, t, :], vf[:, t, :], vrs[:, t:t + 1], vln_b[:, :],
                                                  ALU.mult, ALU.add)
                last.then_inc(S["v_ready"], 1)
                dve.wait_ge(S["vecs_ready"], at("vecs_ready", l, 2))
                for i in range(2):
                    dve.wait_ge(S["glu_sig"], at("glu_sig", l, i + 1))
                    v.tensor_tensor(xg[:, 2 * i:2 * i + 2, PAD:], ctmp[:, 2 * i:2 * i + 2, :], pair(2 * i), ALU.mult
                                    ).then_inc(S["xg_ready"], 1)
                    dve.wait_ge(S["xg_ready"], at("xg_ready", l, i + 1))
                    if i == 0:
                        split(l, U_GLU + 4)
                        convolve(8)
                        split(l, U_GLU + 5)
                        convolve(4)
                    else:
                        split(l, U_GLU + 6)
                        dve.wait_ge(S["v_hi_ready"], at("v_hi_ready", l, 1))
                        v.tensor_tensor(v_lo, vf, v_hi.bitcast(F32), ALU.subtract).then_inc(S["v_lo_ready"], 1)
                        convolve(8)
                split(l, U_POOL + 3)

                dve.wait_ge(S["px_ready"], at("px_ready", l, 2))
                source = pooled
                for gi, w in enumerate(POOL_WINDOWS):
                    d = w // 2
                    target = (sum_a, sum_b)[gi % 2]
                    v.tensor_copy(target[:, gi:, 0:d], source[:, gi:, 0:d])
                    step(v.tensor_tensor(target[:, gi:, d:], source[:, gi:, d:], source[:, gi:, 0:SEQ - d], ALU.add))
                    steps_done()
                    source = target
                W0 = POOL_WINDOWS[-1]
                for k, part_sums in enumerate((sum_a, sum_b)):
                    ins = v.tensor_tensor(part_sums[:, k::2, 0:W0], part_sums[:, k::2, 0:W0], inv[:, k::2, :], ALU.mult)
                step(ins)
                for gi, w in enumerate(POOL_WINDOWS):
                    part_sums = (sum_a, sum_b)[gi % 2]
                    v.scalar_tensor_tensor(pooled[:, gi, W0:], part_sums[:, gi, W0:], 1.0 / w, pooled[:, gi, W0:],
                                           ALU.mult, ALU.subtract)
                steps_done()
                for k, part_sums in enumerate((sum_a, sum_b)):
                    ins = v.tensor_tensor(pooled[:, k::2, 0:W0], part_sums[:, k::2, 0:W0], pooled[:, k::2, 0:W0],
                                          ALU.subtract)
                ins.then_inc(S["pooled_ready"], 1)
                split(l, U_POOL + 4)
                convolve(4)
                dve.wait_ge(S["pooled_hi"], at("pooled_hi", l, 1))
                v.tensor_tensor(pl_lo, pooled, pl_hi.bitcast(F32), ALU.subtract).then_inc(S["pooled_lo"], 1)

                for i in range(2):
                    split(l, U_U + i + 3)
                    convolve(5)
                xa = xs[:, 0, :].rearrange("p (c n) -> p c n", c=CB)

                def merge(b, k):
                    made = ps[:, 2 * k:2 * k + 2, :].rearrange("p b (c n) -> p (b c) n", c=2)
                    m = slice(4 * k, 4 * k + 4)
                    gate = gate_of(b, 4 * k)
                    dve.wait_ge(S["unit_done"], at("unit_done", l, U_OUT[b][k] + 1))
                    dve.wait_ge(S["gate_sig"], at("gate_sig", l, 4 * b + 2 * k + 2))
                    if b == 0:
                        v.tensor_tensor(merged[:, m, :], gate, made, ALU.mult).then_inc(S["out_read"], 1)
                        return
                    v.tensor_tensor(gate, gate, made, ALU.mult).then_inc(S["out_read"], 1)
                    dve.wait_ge(S["out_read"], at("out_read", l, 2 * b + k + 1))
                    v.tensor_tensor(merged[:, m, :], merged[:, m, :], gate, ALU.add
                                    ).then_inc(S["merged_ready"], 1)

                for k, n in enumerate(U_GATE[0]):
                    split(l, n + 3)
                    convolve(8 if k < 3 else 5)
                    if n == U_PW - 1:
                        for i in range(GR):
                            if i % 2 == 0:
                                dve.wait_ge(S["yp_hi"], at("yp_hi", l, i + 2))
                            v.scalar_tensor_tensor(y_lo[:, 0, i, :], pair(2 + i // 2)[:, i % 2, :],
                                                   vec4[:, 0, i:i + 1], y_hi[:, 0, i, :].bitcast(F32),
                                                   ALU.mult, ALU.subtract).then_inc(S["yp_lo"], 1)
                        split(l, U_PW + 3)
                for k, n in enumerate(U_OUT[0]):
                    merge(0, k)
                    split(l, n + 3)
                    convolve(5)
                for k, n in enumerate(U_GATE[1] + U_GATE[2]):
                    if k == 7:
                        dve.wait_ge(S["stat_done"], at("stat_done", l, 1))
                        mean = ps[:, 4, 0:SEQ].unsqueeze(1).broadcast_to([P, CB, SEQ])
                        v.tensor_tensor(acc[:, :, :], acc[:, :, :], mean, ALU.subtract
                                        ).then_inc(S["centred"], 1)
                    split(l, n + 3)
                    if k == 1:
                        dve.wait_ge(S["s_done"], at("s_done", l, 1))
                        for c in range(TT):
                            part = (slice(None), slice(None), slice(c * P, (c + 1) * P))
                            gated = ps[:, 4:6, :].rearrange("p b (c n) -> p (b c) n", c=2)
                            step(v.tensor_tensor(s1[part], gated[part], bs[:, :, :], ALU.add))
                        steps_done()
                        dve.wait_ge(S["u_gelu"], at("u_gelu", l, 2))
                        v.tensor_tensor(us, s1, u[:, :, :], ALU.mult).then_inc(S["us_ready"], 1)
                        convolve(4)
                        dve.wait_ge(S["us_hi"], at("us_hi", l, 1))
                        v.tensor_tensor(y_lo[:, 1, :, :], us, y_hi[:, 1, :, :].bitcast(F32), ALU.subtract
                                        ).then_inc(S["us_lo"], 1)
                    else:
                        convolve(8 if k < 6 else len(jobs))
                assert not jobs
                dve.wait_ge(S["stat_done"], at("stat_done", l, 2))
                v.tensor_scalar(cvar[:, :], ps[:, 5, 0:TT], EPS, None, ALU.add).then_inc(S["cvar_ready"], 1)
                dve.wait_ge(S["crstd_ready"], at("crstd_ready", l, 1))
                for t in range(TT):
                    ins = v.tensor_scalar(diag[:, t, :], ident[:, :], crs[:, t:t + 1], None, ALU.mult)
                ins.then_inc(S["diag_ready"], 1)
                merge(1, 0)
                split(l, U_OUT[1][0] + 3)
                dve.wait_ge(S["stat_done"], at("stat_done", l, 3))
                rstd = ps[:, 4, SEQ:2 * SEQ].unsqueeze(1).broadcast_to([P, CB, SEQ])
                v.tensor_tensor(acc[:, :, :], acc[:, :, :], rstd, ALU.mult).then_inc(S["z_ready"], 1)
                dve.wait_ge(S["z_ready"], at("z_ready", l, 1))
                for c in range(CB):
                    ins = v.tensor_scalar(xa[:, c, :], acc[:, c, :], vec4[:, 2, c:c + 1], vec4[:, 3, c:c + 1],
                                          ALU.mult, ALU.add)
                step(ins)
                steps_done()
                dve.wait_ge(S["zsig_ready"], at("zsig_ready", l, 1))
                v.tensor_tensor(xa, xa, ctmp[:, :, :], ALU.mult).then_inc(S["conv_y"], 1)
                dve.wait_ge(S["cy_hi"], at("cy_hi", l, 1))
                v.tensor_tensor(y_lo[:, 2, :, :], xa, y_hi[:, 2, :, :].bitcast(F32), ALU.subtract
                                ).then_inc(S["cy_lo"], 1)
                merge(1, 1)
                split(l, U_OUT[1][1] + 3)
                for k, n in enumerate(U_OUT[2]):
                    merge(2, k)
                    split(l, n + 3)
                    dve.wait_ge(S["mg_hi"], at("mg_hi", l, k + 1))
                    m = slice(4 * k, 4 * k + 4)
                    v.tensor_tensor(nt_lo[:, m, :], merged[:, m, :], nt_hi[:, m, :].bitcast(F32), ALU.subtract
                                    ).then_inc(S["mg_lo"], 1)
                assert steps[0] == DVE_STEPS, steps
                for k in range(2):
                    split(l, U_WOUT + k + 3)
                boundary(l, 1, U_WOUT + 2, 1.0)
                ffn(l, 1, U_FFN2)
                split(l, U_EMB + 3)
                for k in range(2):
                    split(l, U_PLEG + k + 3)

                def gate_rows(t):
                    dve.wait_ge(S["ple_sig"], at("ple_sig", l, t + 1))
                    v.tensor_tensor(ge[:, t, :], ge[:, t, :], rows(t, 4), ALU.mult).then_inc(S["ge_ready"], 1)

                gate_rows(0)
                with dve.If(DEPTH - 1 - l):
                    split(l, UNITS)
                    dve.wait_ge(S["gain_landed1"], at("gain_landed1", l, 2, 16))
                    add_rows(l, 3, 0, 1.0, ge[:, 0, :], 1, sums("rstd_ready", l, 3, 1))
                    gate_rows(1)
                    scale_rows(l + 1, 0, 0, sums("rstd_ready", l, 3, 2))
                    add_rows(l, 3, 1, 1.0, ge[:, 1, :], 1, sums("rstd_ready", l, 3, 3))
                    split(l, UNITS + 1)
                    rows_lo(l + 1, 0, 0)
                    scale_rows(l + 1, 0, 1, sums("rstd_ready", l, 3, 4))
                    split(l, UNITS + 2)
                    rows_lo(l + 1, 0, 1)
                with dve.Else():
                    dve.wait_ge(S["gain_landed1"], at("gain_landed1", l, 2, 16))
                    add_rows(l, 3, 0, 1.0, ge[:, 0, :], 1, sums("rstd_ready", l, 3, 1))
                    gate_rows(1)
                    add_rows(l, 3, 1, 1.0, ge[:, 1, :], 1, sums("rstd_ready", l, 3, 2))

        @block.tensor
        def _(pe):
            te = nc.tensor

            def product(o, a_hi, a_lo, b_hi, b_lo, start, stop):
                te.matmul(o, a_hi, b_hi, start=start, stop=False)
                te.matmul(o, a_hi, b_lo, start=False, stop=False)
                return te.matmul(o, a_lo, b_hi, start=False, stop=stop)

            def loaded(l, n, off=0):
                pe.wait_ge(S["w_lo_ready"], at("w_lo_ready", l, n + 1) + off)

            def turn(l, s, t):
                base = 0 if s == 3 else 4
                pe.wait_ge(S["xn_ready"], at("xn_ready", l, 2 * s + t + 1))
                for k in range(KD):
                    ins = te.transpose(quads(base, t, k // 4)[:, k % 4, :], xs[:, t, k * P:(k + 1) * P], ident[:, :])
                    if k % 4 == 3:
                        ins.then_inc(S["xt_done"], 1)

            def rows_split(l, s, t):
                pe.wait_ge(S["nt_lo_ready"], at("nt_lo_ready", l, 4 * s + 2 * t + 2))

            def by_channel(n, bank, x_hi, x_lo, kt, tiles, t=None):
                s = n % RING
                w = width(n) // kt
                tok = slice(0, SEQ) if t is None else slice(t * P, (t + 1) * P)
                for c in range(tiles):
                    for k in range(kt):
                        at_ = slice(k * w + c * P, k * w + (c + 1) * P)
                        ins = product(pair(bank + c // 2)[:, c % 2, tok], w_hi[:, s, at_], w_lo[:, s, at_],
                                      x_hi[:, k, tok], x_lo[:, k, tok], k == 0, k == kt - 1)
                return ins

            def across(n, bank, col, t):
                x_at = slice(t * P, (t + 1) * P)
                for k in range(KD):
                    at_ = slice(k * FC, (k + 1) * FC)
                    ins = product(ps[:, bank, col:col + FC], nt_hi[:, k, x_at], nt_lo[:, k, x_at],
                                  w_hi[:, n % RING, at_], w_lo[:, n % RING, at_], k == 0, k == KD - 1)
                return ins

            def first_two(l, s, n, place):
                turn(l, s, 0)
                loaded(l, n)
                rows_split(l, s, 0)
                across(n, *place(0, 0), 0)
                turn(l, s, 1)
                loaded(l, n + 1)
                across(n + 1, *place(1, 0), 0)
                rows_split(l, s, 1)
                for i in range(2):
                    done(across(n + i, *place(i, 1), 1))

            def by_token(t, n, base, x_hi, x_lo, k0, kt, start, stop):
                s = n % RING
                x_at = slice(t * P, (t + 1) * P)
                for k in range(kt):
                    for half in range(2):
                        at_ = slice(k * D + half * BANK, k * D + (half + 1) * BANK)
                        ins = product(ps[:, base + 2 * t + half, :], x_hi[:, k0 + k, x_at], x_lo[:, k0 + k, x_at],
                                      w_hi[:, s, at_], w_lo[:, s, at_], start and k == 0, stop and k == kt - 1)
                return ins

            def done(ins):
                ins.then_inc(S["unit_done"], 1)

            def ffn(l, f, base):
                c0 = NCH * f

                def gate(c, n, off=0, coff=0, free=True):
                    loaded(l, n, off)
                    if free:
                        pe.wait_ge(S["gate_read"], at("gate_read", l, c0 + c - 1) + coff)
                    done(by_channel(n, gate_bank(c), nt_hi, nt_lo, KD, 2))

                def up(c, n, off=0, coff=0, free=True):
                    loaded(l, n, off)
                    if free:
                        pe.wait_ge(S["prod_ready"], at("prod_ready", l, c0 + c - 1) + coff)
                    done(by_channel(n, up_bank(c), nt_hi, nt_lo, KD, 2))

                def down(c, n, off=0, coff=0, start=False, stop=False, t=None):
                    loaded(l, n, off)
                    pe.wait_ge(S["act_lo_ready"], at("act_lo_ready", l, c0 + c + 1) + coff)
                    for tt in range(TT) if t is None else [t]:
                        ins = by_token(tt, n, 0, act_hi[:, c % 2, :, :], act_lo[:, c % 2, :, :], 0, 2, start, stop)
                    if t != 0:
                        done(ins)
                    return ins

                first_two(l, 2 * f, base, lambda i, t: ((gate_bank(0), up_bank(0))[i], t * FC))
                if f == 0:
                    pe.wait_ge(S["vec_landed"], at("vec_landed", l, NV + 1, 16))
                    after(pe, "pe_waited")
                    te.transpose(ps[:, 0, 0:NV * CB], vec_rows[0:NV * CB, :], ident[0:NV * CB, 0:NV * CB])
                    te.transpose(ps[:, 0, P:P + TAPS * CB], tap_rows[0:TAPS * CB, :], ident[0:TAPS * CB, 0:TAPS * CB]
                                 ).then_inc(S["vecs_turned"], 1)
                    pe.wait_ge(S["ws_masked"], at("ws_masked", l, 1))
                    for i in range(4):
                        ins = te.transpose(ps[:, 1, i * P:(i + 1) * P], ws[:, i, :], ident[:, :])
                    ins.then_inc(S["prep_done"], 1)
                    pe.wait_ge(S["p_landed"], at("p_landed", l, 1, 16))
                    for k in range(2):
                        for t in range(TT):
                            ins = te.transpose(pair(2)[:, k, t * P:(t + 1) * P], p_in[:, t, k * P:(k + 1) * P],
                                               ident[:, :])
                    ins.then_inc(S["prep_done"], 1)
                gate(1, base + 2, free=False)
                pe.wait_ge(S["prod_ready"], at("prod_ready", l, c0 + 1))
                for k in range(2):
                    for t in range(TT):
                        ins = te.transpose(pair(gate_bank(0))[:, k, t * P:(t + 1) * P],
                                           prod[:, 0, t, k * P:(k + 1) * P], ident[:, :])
                ins.then_inc(S["act_turned"], 1)
                up(1, base + 3, free=False)
                if f == 0:
                    pe.wait_ge(S["vecs_ready"], at("vecs_ready", l, 2))
                    pe.wait_ge(S["prep_lo"], at("prep_lo", l, 2))
                down(0, base + 4, start=True)
                with pe.Fori(0, (NCH - 3) // 2) as i:
                    for k in range(2):
                        n = base + 5 + 3 * k
                        gate(2 + k, n, i * 6, i * 2)
                        up(2 + k, n + 1, i * 6, i * 2)
                        down(1 + k, n + 2, i * 6, i * 2)
                n = base + 3 * NCH - 4
                gate(NCH - 1, n)
                up(NCH - 1, n + 1)
                down(NCH - 2, n + 2, t=0)
                down(NCH - 1, n + 3, stop=True, t=0).then_inc(S["tile0_done"], 1)
                down(NCH - 2, n + 2, t=1)
                down(NCH - 1, n + 3, stop=True, t=1)

            pe.wait_ge(S["ident_ready"], 1)
            with pe.Fori(0, DEPTH) as l:
                ffn(l, 0, U_FFN1)
                first_two(l, 1, U_V, lambda i, t: (4 + t, i * FC))
                for k in range(4):
                    n = U_GLU + k
                    loaded(l, n)
                    done(by_channel(n, k, nt_hi, nt_lo, KD, 2))
                for k in range(2):
                    n = U_POOL + k
                    loaded(l, n)
                    done(by_channel(n, 6 + k, nt_hi, nt_lo, KD, 2))
                for i in range(2):
                    n = U_U + i
                    loaded(l, n)
                    pe.wait_ge(S["xg_ready"], at("xg_ready", l, 1))
                    done(by_channel(n, i, nt_hi, nt_lo, KD, 2))

                def gates_unit(b, k):
                    n, j = U_GATE[b][k], 4 * b + k
                    loaded(l, n)
                    if j >= 2:
                        pe.wait_ge(S["gate_sig"], at("gate_sig", l, j - 1))
                    else:
                        pe.wait_ge(S["px_ready"], at("px_ready", l, j + 1))
                    done(by_channel(n, 6 + k % 2, nt_hi, nt_lo, KD, 2))

                def out_unit(b, k):
                    n = U_OUT[b][k]
                    loaded(l, n)
                    if b > 0:
                        pe.wait_ge(S["out_read"], at("out_read", l, 2 * b - 1 + k))
                    done(by_channel(n, 2 * k, y_hi[:, b, :, :], y_lo[:, b, :, :], CB, 4))

                for k in range(3):
                    gates_unit(0, k)
                loaded(l, U_PW)
                pe.wait_ge(S["xg_ready"], at("xg_ready", l, 2))
                pe.wait_ge(S["pooled_lo"], at("pooled_lo", l, 1))
                s = U_PW % RING
                for i in range(GR):
                    ins = product(pair(2 + i // 2)[:, i % 2, :], w_hi[:, s, i * P:(i + 1) * P],
                                  w_lo[:, s, i * P:(i + 1) * P], pl_hi[:, i, :], pl_lo[:, i, :], True, True)
                done(ins)
                gates_unit(0, 3)
                pe.wait_ge(S["yp_lo"], at("yp_lo", l, 4))
                pe.wait_ge(S["u_gelu"], at("u_gelu", l, 2))
                for k in range(2):
                    out_unit(0, k)
                gates_unit(1, 0)
                pe.wait_ge(S["v_lo_ready"], at("v_lo_ready", l, 1))
                for i in range(4):
                    for t in range(TT):
                        ins = product(pair(4 + i // 2)[:, i % 2, t * P:(t + 1) * P], v_hi[:, t, i * P:(i + 1) * P],
                                      v_lo[:, t, i * P:(i + 1) * P], wst_hi[:, i, :], wst_lo[:, i, :], True, True)
                ins.then_inc(S["s_done"], 1)
                for k in range(1, 4):
                    gates_unit(1, k)
                for k in range(3):
                    gates_unit(2, k)
                pe.wait_ge(S["tap_added"], at("tap_added", l, TAPS * CB))
                for c in range(CB):
                    ins = te.matmul(ps[:, 4, 0:SEQ], mean_w[:, :], acc[:, c, :], start=c == 0, stop=c == CB - 1)
                ins.then_inc(S["stat_done"], 1)
                gates_unit(2, 3)
                pe.wait_ge(S["csq_ready"], at("csq_ready", l, 1))
                for t in range(TT):
                    for c in range(CB):
                        ins = te.matmul(ps[:, 5, t:t + 1], ctmp[:, c, t * P:(t + 1) * P], mean_w[:, 0:1],
                                        start=c == 0, stop=c == CB - 1)
                ins.then_inc(S["stat_done"], 1)
                pe.wait_ge(S["us_lo"], at("us_lo", l, 1))
                out_unit(1, 0)
                pe.wait_ge(S["diag_ready"], at("diag_ready", l, 1))
                for t in range(TT):
                    ins = te.matmul(ps[:, 4, SEQ + t * P:SEQ + (t + 1) * P], ones[:, :], diag[:, t, :],
                                    start=True, stop=True)
                ins.then_inc(S["stat_done"], 1)
                out_unit(1, 1)
                pe.wait_ge(S["cy_lo"], at("cy_lo", l, 1))
                for k in range(2):
                    out_unit(2, k)
                pe.wait_ge(S["out_read"], at("out_read", l, 6))
                for k in range(2):
                    loaded(l, U_WOUT + k)
                    pe.wait_ge(S["mg_lo"], at("mg_lo", l, k + 1))
                    for t in range(TT):
                        ins = by_token(t, U_WOUT + k, 0, nt_hi, nt_lo, 2 * k, 2, k == 0, False)
                    done(ins)
                loaded(l, U_WOUT + 3)
                for t in range(TT):
                    for k in (2, 3):
                        ins = by_token(t, U_WOUT + k, 0, nt_hi, nt_lo, 2 * k, 2, False, k == 3)
                        if t == 1:
                            done(ins)
                    if t == 0:
                        ins.then_inc(S["tile0_done"], 1)
                ffn(l, 1, U_FFN2)
                loaded(l, U_EMB)
                pe.wait_ge(S["prod_ready"], at("prod_ready", l, 2 * NCH))
                by_token(0, U_EMB, 4, pt_hi, pt_lo, 0, 2, True, True)
                turn(l, 3, 0)
                done(by_token(1, U_EMB, 4, pt_hi, pt_lo, 0, 2, True, True))

                def gate_rows(t, k):
                    if t == 0:
                        loaded(l, U_PLEG + k)
                    k0, kt = (2 * k, 2) if k < 3 else (3 + k, 1)
                    ins = by_token(t, U_PLEG + k, 0, nt_hi, nt_lo, k0, kt, k == 0, k == 4)
                    if t == 1:
                        done(ins)
                    return ins

                rows_split(l, 3, 0)
                gate_rows(0, 0)
                turn(l, 3, 1)
                gate_rows(0, 1)
                rows_split(l, 3, 1)
                for k in range(2):
                    gate_rows(1, k)
                for t in range(TT):
                    for k in range(2, 5):
                        ins = gate_rows(t, k)
                    if t == 0:
                        ins.then_inc(S["tile0_done"], 1)


_INS = [
    "x", "p", "ffn1_pre_g", "ffn1_w_gate", "ffn1_w_up", "ffn1_w_down", "ffn1_post_g", "mix_pre_g", "w_in",
    "pool_w", "pool_scale", "w_pool_out", "sgu_ln_g", "sgu_ln_b", "sgu_w_s", "sgu_b_s", "w_sgu_out",
    "conv_dw_k", "conv_dw_b", "conv_ln_g", "conv_ln_b", "w_conv_out", "w_out", "mix_post_g", "ffn2_pre_g",
    "ffn2_w_gate", "ffn2_w_up", "ffn2_w_down", "ffn2_post_g", "ple_w_proj", "ple_pre_g", "ple_w_gate",
    "ple_post_g",
]


def kernel(**inputs):
    import numpy as np
    import concourse.bacc as bacc
    from concourse.bass_utils import run_bass_kernel_spmd

    nc = bacc.Bacc("TRN2", target_bir_lowering=False, num_devices=1)
    arrays, aps = {}, {}
    for name in _INS:
        a = np.ascontiguousarray(inputs[name])
        arrays[f"in_{name}"] = a
        aps[name] = nc.dram_tensor(f"in_{name}", a.shape, mybir.dt.from_np(a.dtype), kind="ExternalInput").ap()
    out = nc.dram_tensor("out", inputs["x"].shape, F32, kind="ExternalOutput").ap()
    hybrid_trunk(nc, aps, out)
    r = run_bass_kernel_spmd(nc, [arrays], core_ids=[0])
    return r.results[0]["out"]
```

```python
from contextlib import ExitStack

import concourse.bass as bass
from concourse import mybir

ALU = mybir.AluOpType
ACT = mybir.ActivationFunctionType
F32 = mybir.dt.float32
F32R = mybir.dt.float32r

P = 128
EPS = 1e-6
RING = 3
UNIT = 2048
BANK = 512
POOL_WINDOWS = (2, 4, 8, 16)


def hybrid_trunk(nc, A, out):
    DEPTH, D, F = A["ffn1_w_gate"].shape
    SEQ = A["x"].shape[1]
    TT = SEQ // P
    KD = D // P
    FC = 2 * P
    NCH = F // FC
    GR = len(POOL_WINDOWS)
    WB = A["w_pool_out"].shape[1]
    CB = WB // P
    TAPS = A["conv_dw_k"].shape[1]
    PAD = TAPS - 1
    PLE = A["p"].shape[3]
    ROOT = 32
    assert ROOT * ROOT == D
    assert (SEQ, D, NCH * FC, WB, PLE) == (2 * P, 8 * P, F, 4 * P, 2 * P) and NCH == 11

    FFN_UNITS = 3 * NCH
    U_FFN1 = 0
    U_MIX = U_FFN1 + FFN_UNITS
    U_V, U_GLU, U_POOL, U_U = U_MIX, U_MIX + 2, U_MIX + 6, U_MIX + 8
    n = U_U + 2
    U_GATE = [[n, n + 1, n + 2, n + 4], list(range(n + 7, n + 11)), list(range(n + 11, n + 15))]
    U_PW = n + 3
    U_OUT = [[n + 5, n + 6], [n + 15, n + 16], [n + 17, n + 18]]
    U_WOUT = n + 19
    U_FFN2 = U_WOUT + 4
    U_EMB = U_FFN2 + FFN_UNITS
    U_PLEG = U_EMB + 1
    UNITS = U_PLEG + 5
    assert UNITS % RING == 0 and U_FFN2 % RING == 0

    def width(n):
        n = n % UNITS
        return GR * P if n == U_PW else D if U_PLEG <= n < U_PLEG + 2 else UNIT

    with ExitStack() as ctx:
        def sb(name, shape, dt=F32):
            return ctx.enter_context(nc.sbuf_tensor(name, [P] + shape, dt))

        per_layer = {}

        def sem(name, per=None):
            s = ctx.enter_context(nc.semaphore(name))
            per_layer[name] = per
            sems[name] = s
            return name

        sems = {}

        def at(name, l, k, by=1):
            return l * (per_layer[name] * by) + k * by

        raw = sb("raw", [RING, UNIT])
        w_hi = sb("w_hi", [RING, UNIT], F32R)
        w_lo = sb("w_lo", [RING, UNIT], F32R)
        h = sb("h", [TT, D])
        xs = sb("xs", [TT, D])
        nt_hi = sb("nt_hi", [KD, SEQ], F32R)
        nt_lo = sb("nt_lo", [KD, SEQ], F32R)
        pre_gain = sb("pre_gain", [D])
        gain = sb("gain", [2, D])
        sg = sb("sg", [2, 2, SEQ])
        prod = sb("prod", [2, 2, SEQ])
        act_hi = sb("act_hi", [2, 2, SEQ], F32R)
        act_lo = sb("act_lo", [2, 2, SEQ], F32R)
        xg = sb("xg", [CB, PAD + SEQ])
        acc = sb("acc", [CB, SEQ])
        gates = sb("gates", [KD, SEQ])
        merged = sb("merged", [KD, SEQ])
        y_hi = sb("y_hi", [3, CB, SEQ], F32R)
        y_lo = sb("y_lo", [3, CB, SEQ], F32R)
        u = sb("u", [CB, SEQ])
        ctmp = sb("ctmp", [CB, SEQ])
        wst_hi = sb("wst_hi", [4, P], F32R)
        wst_lo = sb("wst_lo", [4, P], F32R)
        bs = sb("bs", [4, P])
        vln_g = sb("vln_g", [WB])
        vln_b = sb("vln_b", [WB])
        pt_hi = sb("pt_hi", [2, SEQ], F32R)
        pt_lo = sb("pt_lo", [2, SEQ], F32R)
        ident = sb("ident", [P])
        ones = sb("ones", [P])
        mean_w = sb("mean_w", [P])
        diag = sb("diag", [TT, P])
        inv = sb("inv", [GR, 16])
        minus_half = sb("minus_half", [1])
        ss = sb("ss", [8, TT, 2])
        ms = sb("ms", [8, TT])
        rs = sb("rs", [8, TT])
        vst = sb("vst", [TT, 6])
        vmv = sb("vmv", [TT, 2])
        vms = sb("vms", [TT])
        vrs = sb("vrs", [TT])
        cvar = sb("cvar", [TT])
        crs = sb("crs", [TT])
        VECS = ("pool_scale", "conv_dw_b", "conv_ln_g", "conv_ln_b")
        NV = len(VECS)
        vec4 = sb("vec4", [NV, CB])
        tap = sb("tap", [TAPS, CB])
        vec_rows = u[:, 0, 0:P]
        tap_rows = u[:, 1, 0:P]
        ws = ctmp[:, 0:2, :].rearrange("p c (h s) -> p (c h) s", h=2)
        p_in = ctmp[:, 2:4, :]
        pooled = merged[:, 0:CB, :]
        sum_a = sg[:, :, :, :].rearrange("p a b n -> p (a b) n")
        sum_b = prod[:, :, :, :].rearrange("p a b n -> p (a b) n")
        pl_hi = act_hi[:, :, :, :].rearrange("p a b n -> p (a b) n")
        pl_lo = act_lo[:, :, :, :].rearrange("p a b n -> p (a b) n")

        def gate_of(b, k):
            if b == 0:
                return gates[:, 4 * k:4 * k + 4, :]
            return (sum_a, sum_b)[k] if b == 1 else xs[:, k, :].rearrange("p (c n) -> p c n", c=CB)

        vf = xs[:, 0, :].rearrange("p (t n) -> p t n", t=TT)
        junk = gates[:, :, :].rearrange("p k n -> p (k n)").rearrange("p (t n) -> p t n", t=TT)
        us = xs[:, 0, :].rearrange("p (c n) -> p c n", c=CB)
        s1 = xs[:, 1, :].rearrange("p (c n) -> p c n", c=CB)
        half_sum = [ctmp[:, 0, :], ctmp[:, 1, :]]
        v_hi = y_hi[:, 2, :, :].rearrange("p c n -> p (c n)").rearrange("p (t n) -> p t n", t=TT)
        v_lo = y_lo[:, 2, :, :].rearrange("p c n -> p (c n)").rearrange("p (t n) -> p t n", t=TT)
        ge = merged[:, :, :].rearrange("p k n -> p (k n)").rearrange("p (t n) -> p t n", t=TT)

        ps = ctx.enter_context(nc.psum_tensor("ps", [P, 8, BANK], F32))

        def pair(b):
            return ps[:, b, :].rearrange("p (c n) -> p c n", c=2)

        def gate_bank(c):
            return 4 + 2 * (c % 2)

        def up_bank(c):
            return 5 + 2 * (c % 2)

        def quads(base, t, b):
            return ps[:, base + 2 * t + b, :].rearrange("p (k n) -> p k n", k=4)

        def half(b):
            return slice(b * BANK, (b + 1) * BANK)

        def rows(t, base=0):
            return ps[:, base + 2 * t:base + 2 * t + 2, :].rearrange("p b n -> p (b n)")

        def chunk_parts(c):
            if c == NCH - 1:
                return y_hi[:, 0, 0:2, :], y_lo[:, 0, 0:2, :]
            return act_hi[:, c % 2, :, :], act_lo[:, c % 2, :, :]

        landed = [sem(f"landed{s}", UNITS // RING) for s in range(RING)]
        for name, per in {
            "w_hi_ready": UNITS, "w_lo_ready": UNITS, "unit_done": UNITS,
            "h_ready": 16, "ssq_ready": 32, "ms_ready": 16, "rstd_ready": 16, "xn_ready": 16,
            "xt_done": 16, "nt_hi_ready": 16, "nt_lo_ready": 16, "pre_gain_landed": 4, "row_gained": 16, "tile0_done": 4,
            "vecs_ready": 2, "vecs_turned": 1, "vec_landed": NV + 1,
            "sg_ready": 2 * NCH, "gate_read": 2 * NCH, "prod_ready": 2 * NCH,
            "act_hi_ready": 2 * NCH, "act_lo_ready": 2 * NCH,
            "ws_landed": 1, "ws_masked": 1, "p_landed": 1, "gain_landed0": 2, "gain_landed1": 2,
            "rowvecs_landed": 3, "prep_done": 2, "prep_hi": 2, "prep_lo": 2,
            "glu_sig": 2, "xg_ready": 2, "px_ready": 2, "dve_step": 0, "pooled_ready": 1,
            "pooled_hi": 1, "pooled_lo": 1, "v_gelu": 2, "v_stats": 2, "v_ready": 1,
            "v_ms": 2, "v_rstd": 2, "v_hi_ready": 1, "v_lo_ready": 1,
            "u_gelu": 2, "yp_hi": 4, "yp_lo": 4, "act_turned": 2,
            "s_done": 1, "us_ready": 1, "us_hi": 1, "us_lo": 1,
            "gate_sig": 12, "out_read": 6, "merged_ready": 4, "mg_hi": 2, "mg_lo": 2,
            "tap_added": PAD * CB, "stat_done": 3, "centred": 1, "csq_ready": 1, "cvar_ready": 1,
            "crstd_ready": 1, "diag_ready": 1, "z_ready": 1, "zsig_ready": 1,
            "conv_y": 1, "cy_hi": 1, "cy_lo": 1,
            "ple_sig": 4, "ge_ready": 4, "acc_summed": 2, "conv_begun": 4,
            "first_gain_landed": 0, "x_landed0": 0, "x_landed1": 0, "zero_ready": 0, "ident_ready": 0, "const_ready": 0,
            "inv_ready": 0, "stored": 0,
            "sp_waited": 0, "pool_waited": 0, "dve_waited": 0, "pe_waited": 0,
        }.items():
            sem(name, per)
        S = sems
        DVE_STEPS = 12
        per_layer["dve_step"] = DVE_STEPS

        NORM_IN = (0, 2, 4, 6)
        NORM_OUT = (1, 3, 5, 7)

        def sums(name, l, q, k):
            return at(name, l, 4 * q + k) + TT

        def half_sums(l, q, k, b):
            return at("ssq_ready", l, 8 * q + 2 * k - 1 + b) + 2 * TT

        def landing(n):
            return n % RING, n // RING + 1

        def after(eng, name):
            eng.sem_inc(S[name], 1)

        block = ctx.enter_context(nc.Block())

        @block.sync
        def _(sp):
            def load(src, l, n, first=False, wait=None):
                s = n % RING
                if not first:
                    sp.wait_ge(S["w_lo_ready"], at("w_lo_ready", l, n - 2) if wait is None else wait)
                    after(sp, "sp_waited")
                k = src.shape[1]
                dst = raw[:, s, 0:k * src.shape[2]].rearrange("p (k n) -> p k n", k=k)
                sp.dma_start(dst, src).then_inc(S[landed[s]], 16)

            def cols(name, l, c, n):
                w = A[name]
                return w[bass.ds(l, 1), :, bass.ds(c, n)].rearrange("o (k p) n -> p (o k) n", p=P)

            def rws(name, l, r, n):
                w = A[name]
                return w[bass.ds(l, 1), bass.ds(r, n), :].rearrange("o (k p) n -> p (o k) n", p=P)

            def ffn(l, f, base):
                g, u_, d = f"{f}_w_gate", f"{f}_w_up", f"{f}_w_down"
                if f == "ffn2":
                    load(cols(g, l, 0, FC), l, base)
                    load(cols(u_, l, 0, FC), l, base + 1)
                    load(cols(g, l, FC, FC), l, base + 2)
                load(cols(u_, l, FC, FC), l, base + 3)
                load(rws(d, l, 0, FC), l, base + 4)
                with sp.Fori(0, (NCH - 5) // 2) as i:
                    for k in range(2):
                        n = base + 5 + 3 * k
                        lo = at("w_lo_ready", l, n - 2) + i * 6
                        load(cols(g, l, i * (2 * FC) + (2 + k) * FC, FC), l, n, wait=lo)
                        load(cols(u_, l, i * (2 * FC) + (2 + k) * FC, FC), l, n + 1, wait=lo + 1)
                        load(rws(d, l, i * (2 * FC) + (1 + k) * FC, FC), l, n + 2, wait=lo + 2)
                n = base + 3 * NCH - 10
                for c in range(NCH - 3, NCH):
                    load(cols(g, l, c * FC, FC), l, n)
                    load(cols(u_, l, c * FC, FC), l, n + 1)
                    n += 2
                    if c == NCH - 3:
                        load(rws(d, l, (c - 1) * FC, FC), l, n)
                        n += 1
                for k in range(3):
                    load(rws(d, l, (NCH - 3 + k) * FC, FC), l, n + k)

            def first_units(l, first):
                load(cols("ffn1_w_gate", l, 0, FC), l, 0, first)
                load(cols("ffn1_w_up", l, 0, FC), l, 1, first)
                load(cols("ffn1_w_gate", l, FC, FC), l, 2, first)

            x_in = A["x"][0].rearrange("(t p) n -> t p n", p=P)
            sp.dma_start(h[:, 0, :], x_in[0]).then_inc(S["x_landed0"], 16)
            sp.dma_start(pre_gain[:, :], A["ffn1_pre_g"][0:1, :].broadcast_to([P, D])
                         ).then_inc(S["first_gain_landed"], 16)
            sp.dma_start(h[:, 1, :], x_in[1]).then_inc(S["x_landed1"], 16)
            first_units(0, True)
            with sp.Fori(0, DEPTH) as l:
                ffn(l, "ffn1", U_FFN1)
                OFF_U, OFF_V, OFF_A, OFF_B, OFF_G = WB, 2 * WB, 3 * WB, 4 * WB, 5 * WB
                blocks = [OFF_V, OFF_V + FC, OFF_A, OFF_B, OFF_A + FC, OFF_B + FC, 0, FC, OFF_U, OFF_U + FC]
                for k, c in enumerate(blocks):
                    load(cols("w_in", l, c, FC), l, U_V + k)
                for b, name in enumerate(("w_pool_out", "w_sgu_out", "w_conv_out")):
                    if b < 2:
                        branches = [b] if b == 0 else [1, 2]
                        for bb in branches:
                            for k, n in enumerate(U_GATE[bb]):
                                if n == U_PW + 1:
                                    load(A["pool_w"][bass.ds(l, 1)].rearrange("o g i n -> i (o g) n"), l, U_PW)
                                load(cols("w_in", l, OFF_G + bb * D + k * FC, FC), l, n)
                    for k, n in enumerate(U_OUT[b]):
                        load(cols(name, l, k * BANK, BANK), l, n)
                for k in range(4):
                    load(rws("w_out", l, k * FC, FC), l, U_WOUT + k)
                ffn(l, "ffn2", U_FFN2)
                load(rws("ple_w_proj", l, 0, PLE), l, U_EMB)
                for k in range(2):
                    load(rws("ple_w_gate", l, k * P, P), l, U_PLEG + k)
                for k in range(1, 4):
                    load(rws("ple_w_gate", l, k * FC, FC), l, U_PLEG + 1 + k)
                with sp.If(DEPTH - 1 - l):
                    first_units(nc.s_assert_within(
                        l + 1, 1, DEPTH - 1, skip_runtime_bounds_check_because="this If runs below the last layer only"), False)
            o = out[0].rearrange("(t p) n -> t p n", p=P)
            for t in range(TT):
                sp.wait_ge(S["h_ready"], 16 * DEPTH - 4 + 2 * t + 2)
                sp.dma_start(o[t], h[:, t, :]).then_inc(S["stored"], 16)
            sp.wait_ge(S["stored"], 16 * TT)

        @block.gpsimd
        def _(pool):
            g = nc.gpsimd
            g.memset(ident[:, :], 1.0).then_inc(S["zero_ready"], 1)
            g.memset(minus_half[:, :], -0.5).then_inc(S["const_ready"], 1)
            pool.wait_ge(S["zero_ready"], 1)
            g.affine_select(out=ident[:, :], in_=ident[:, :], compare_op=ALU.is_equal, fill=0.0, base=0,
                            pattern=[[-1, P]], channel_multiplier=1).then_inc(S["ident_ready"], 1)
            g.memset(ones[:, :], 1.0).then_inc(S["const_ready"], 1)
            g.memset(mean_w[:, :], 1.0 / WB).then_inc(S["const_ready"], 1)
            for j in range(16):
                last = g.memset(inv[:, GR - 1, j:j + 1], 1.0 / (j + 1))
            last.then_inc(S["inv_ready"], 1)
            pool.wait_ge(S["const_ready"], 1)

            def rstd(e, t, ssq, val):
                pool.wait_ge(S["ssq_ready"], ssq)
                after(pool, "pool_waited")
                g.tensor_scalar(ms[:, e, t:t + 1], ss[:, e, t, 0:1], ss[:, e, t, 1:2], EPS, ALU.add, ALU.add
                                ).then_inc(S["ms_ready"], 1)
                pool.wait_ge(S["ms_ready"], val)
                g.tensor_tensor(rs[:, e, t:t + 1], ms[:, e, t:t + 1], minus_half[:, :], ALU.pow
                                ).then_inc(S["rstd_ready"], 1)

            def boundary(l, q):
                for t in range(TT):
                    rstd(NORM_OUT[q], t, half_sums(l, q, 2 * t + 1, 1), sums("ms_ready", l, q, 2 * t + 1))
                    rstd(NORM_IN[(q + 1) % 4], t, half_sums(l, q, 2 * t + 2, 1), sums("ms_ready", l, q, 2 * t + 2))

            def row(name, l):
                v = A[name]
                return v[bass.ds(l, 1), :].broadcast_to([P, v.shape[1]])

            def load_gain(dst, name, l, landed_):
                pool.dma_start(dst, row(name, l)).then_inc(S[landed_], 16)

            def load_pre_gain(name, l, l_before, s_before):
                pool.wait_ge(S["xn_ready"], at("xn_ready", l_before, 4 * s_before + 2 * TT))
                after(pool, "pool_waited")
                load_gain(pre_gain[:, :], name, l, "pre_gain_landed")

            def small_loads(l):
                pool.dma_start(ws, A["sgu_w_s"][bass.ds(l, 1)].rearrange("o h t s -> t (o h) s")
                               ).then_inc(S["ws_landed"], 16)
                pool.dma_start(p_in, A["p"][bass.ds(l, 1), 0].rearrange("o (t q) n -> q (o t) n", q=P)
                               ).then_inc(S["p_landed"], 16)
                for k, name in enumerate(VECS):
                    pool.dma_start(vec_rows[k * CB:(k + 1) * CB, :], A[name][bass.ds(l, 1), :]
                                   .rearrange("o (k p) -> (o k) p", p=P)).then_inc(S["vec_landed"], 16)
                pool.dma_start(tap_rows[0:TAPS * CB, :], A["conv_dw_k"][bass.ds(l, 1)]
                               .rearrange("a t o (c p) -> (a t o c) p", p=P)).then_inc(S["vec_landed"], 16)
                pool.dma_start(vln_g[:, :], row("sgu_ln_g", l)).then_inc(S["rowvecs_landed"], 16)
                pool.dma_start(vln_b[:, :], row("sgu_ln_b", l)).then_inc(S["rowvecs_landed"], 16)
                pool.dma_start(bs[:, :, :], A["sgu_b_s"][bass.ds(l, 1)].rearrange("o h t -> o (h t)")
                               .broadcast_to([P, 4 * P]).rearrange("p (h t) -> p h t", h=4)
                               ).then_inc(S["rowvecs_landed"], 16)

            def mask(l):
                pool.wait_ge(S["ws_landed"], at("ws_landed", l, 1, 16))
                after(pool, "pool_waited")
                g.affine_select(out=ws, in_=ws, compare_op=ALU.is_ge, fill=0.0, base=0,
                                pattern=[[0, 4], [-1, P]], channel_multiplier=1).then_inc(S["ws_masked"], 1)

            for t in range(TT):
                rstd(NORM_IN[0], t, 2 * t + 2, t + 1)
            load_pre_gain("mix_pre_g", 0, 0, 0)
            small_loads(0)
            load_gain(gain[:, 0, :], "ffn1_post_g", 0, "gain_landed0")
            load_gain(gain[:, 1, :], "mix_post_g", 0, "gain_landed1")
            mask(0)
            with pool.Fori(0, DEPTH) as l:
                boundary(l, 0)
                load_pre_gain("ffn2_pre_g", l, l, 1)
                load_gain(gain[:, 0, :], "ffn2_post_g", l, "gain_landed0")
                for t in range(TT):
                    pool.wait_ge(S["v_stats"], at("v_stats", l, t + 1))
                    after(pool, "pool_waited")
                    g.tensor_scalar(vms[:, t:t + 1], vmv[:, t, 1:2], 1.0, EPS, ALU.mult, ALU.add
                                    ).then_inc(S["v_ms"], 1)
                    pool.wait_ge(S["v_ms"], at("v_ms", l, t + 1))
                    g.tensor_tensor(vrs[:, t:t + 1], vms[:, t:t + 1], minus_half[:, :], ALU.pow
                                    ).then_inc(S["v_rstd"], 1)
                pool.wait_ge(S["cvar_ready"], at("cvar_ready", l, 1))
                g.tensor_tensor(crs[:, :], cvar[:, :], minus_half[:, :].broadcast_to([P, TT]), ALU.pow
                                ).then_inc(S["crstd_ready"], 1)
                boundary(l, 1)
                load_pre_gain("ple_pre_g", l, l, 2)
                load_gain(gain[:, 1, :], "ple_post_g", l, "gain_landed1")
                boundary(l, 2)
                with pool.If(DEPTH - 1 - l):
                    following = nc.s_assert_within(
                        l + 1, 1, DEPTH - 1, skip_runtime_bounds_check_because="this If runs below the last layer only")
                    load_pre_gain("ffn1_pre_g", following, l, 3)
                    load_gain(gain[:, 0, :], "ffn1_post_g", following, "gain_landed0")
                    small_loads(following)
                    mask(l + 1)
                    boundary(l, 3)
                    load_pre_gain("mix_pre_g", following, l + 1, 0)
                    load_gain(gain[:, 1, :], "mix_post_g", following, "gain_landed1")
                with pool.Else():
                    for t in range(TT):
                        rstd(NORM_OUT[3], t, half_sums(l, 3, t + 1, 1), sums("ms_ready", l, 3, t + 1))

        @block.scalar
        def _(act):
            sc = nc.scalar

            def split(l, n, ud=None, ld=None):
                s, k = landing(n)
                act.wait_ge(S[landed[s]], at(landed[s], l, k, 16) if ld is None else ld)
                if ud is not False:
                    act.wait_ge(S["unit_done"], at("unit_done", l, n - 2) if ud is None else ud)
                w = width(n)
                sc.activation(w_hi[:, s, 0:w], raw[:, s, 0:w], ACT.Copy).then_inc(S["w_hi_ready"], 1)

            def square(e, t, b, source):
                sc.activation(junk[:, t, half(b)], source, ACT.Square, scale=1.0 / ROOT,
                              accum_out=ss[:, e, t, b:b + 1]).then_inc(S["ssq_ready"], 1)

            def square_in(l, s, t):
                for b in range(2):
                    act.wait_ge(S["h_ready"], at("h_ready", l, 4 * (s - 1) + 2 * t + b + 1))
                    square(NORM_IN[s], t, b, h[:, t, half(b)])

            def square_out(q, t, name, val):
                act.wait_ge(S[name], val)
                for b in range(2):
                    square(NORM_OUT[q], t, b, ps[:, 2 * t + b, :])

            def rows_hi(l, s, t):
                base = 0 if s == 3 else 4
                for b in range(2):
                    act.wait_ge(S["xt_done"], at("xt_done", l, 4 * s + 2 * t + b + 1))
                    sc.activation(nt_hi[:, 4 * b:4 * b + 4, t * P:(t + 1) * P], quads(base, t, b), ACT.Copy
                                  ).then_inc(S["nt_hi_ready"], 1)

            def boundary(l, q, a):
                square_out(q, 0, "tile0_done", at("tile0_done", l, q + 1))
                square_in(l, q + 1, 0)
                split(l, a + 3)
                rows_hi(l, q + 1, 0)
                split(l, a + 4)
                square_out(q, 1, "unit_done", at("unit_done", l, a + 3))
                square_in(l, q + 1, 1)
                rows_hi(l, q + 1, 1)
                split(l, a + 5)

            def sigmoid_gate(l, c, par, n_done, j):
                act.wait_ge(S["unit_done"], n_done)
                sc.activation(sg[:, par, :, :], pair(gate_bank(par)), ACT.Sigmoid).then_inc(S["sg_ready"], 1)

            def chunk_hi(c, prod_val, free_val):
                act.wait_ge(S["prod_ready"], prod_val)
                if free_val is not None:
                    act.wait_ge(S["unit_done"], free_val)
                sc.activation(chunk_parts(c)[0], prod[:, c % 2, :, :], ACT.Copy).then_inc(S["act_hi_ready"], 1)

            def ffn(l, f, base):
                c0 = NCH * f

                def chunk(c, n, off=0, loff=0, freed=None, coff=0):
                    par = c % 2
                    sigmoid_gate(l, c, par, at("unit_done", l, n + 1) + off, 0)
                    s, k = landing(n + 3)
                    split(l, n + 3, ud=False, ld=at(landed[s], l, k, 16) + loff)
                    s, k = landing(n + 4)
                    split(l, n + 4, ud=at("unit_done", l, n + 2) + off, ld=at(landed[s], l, k, 16) + loff)
                    chunk_hi(c, at("prod_ready", l, c0 + c + 1) + coff, freed)

                def down(n, off=0, loff=0):
                    s, k = landing(n + 3)
                    split(l, n + 3, ud=at("unit_done", l, n + 1) + off, ld=at(landed[s], l, k, 16) + loff)

                sigmoid_gate(l, 0, 0, at("unit_done", l, base + 1), 0)
                split(l, base + 3, ud=False)
                if f == 0:
                    for k, (dst, b) in enumerate(((wst_hi[:, :, :], 1), (pt_hi[:, :, :], 2))):
                        act.wait_ge(S["prep_done"], at("prep_done", l, k + 1))
                        src = ps[:, b, :].rearrange("p (c n) -> p c n", c=dst.shape[1])
                        sc.activation(dst, src, ACT.Copy).then_inc(S["prep_hi"], 1)
                split(l, base + 4)
                act.wait_ge(S["act_turned"], at("act_turned", l, f + 1))
                sc.activation(act_hi[:, 0, :, :], pair(gate_bank(0)), ACT.Copy).then_inc(S["act_hi_ready"], 1)
                chunk(1, base + 2)
                down(base + 4)
                with act.Fori(0, (NCH - 5) // 2) as i:
                    for k in range(2):
                        n = base + 5 + 3 * k
                        chunk(2 + k, n, off=i * 6, loff=i * (2 * 16), coff=i * 2,
                              freed=at("unit_done", l, n) + i * 6)
                        down(n + 2, off=i * 6, loff=i * (2 * 16))
                n = base + 3 * NCH - 10
                chunk(NCH - 3, n, freed=at("unit_done", l, n))
                down(n + 2)
                chunk(NCH - 2, n + 3, freed=at("unit_done", l, n + 3))
                chunk(NCH - 1, n + 5)
                boundary(l, 2 * f, n + 7)

            for t in range(TT):
                act.wait_ge(S[f"x_landed{t}"], 16)
                for b in range(2):
                    square(NORM_IN[0], t, b, h[:, t, half(b)])
            split(0, 0, ud=False)
            rows_hi(0, 0, 0)
            split(0, 1, ud=False)
            rows_hi(0, 0, 1)
            split(0, 2, ud=False)
            with act.Fori(0, DEPTH) as l:
                ffn(l, 0, U_FFN1)
                split(l, U_V + 3)
                act.wait_ge(S["unit_done"], at("unit_done", l, U_V + 2))
                for t in range(TT):
                    sc.activation(vf[:, t, :], ps[:, 4 + t, :], ACT.Gelu).then_inc(S["v_gelu"], 1)
                split(l, U_V + 4)
                for i in range(2):
                    split(l, U_GLU + 2 * i + 3)
                    act.wait_ge(S["unit_done"], at("unit_done", l, U_GLU + 2 * i + 2))
                    sc.activation(ctmp[:, 2 * i:2 * i + 2, :], pair(2 * i + 1), ACT.Sigmoid
                                  ).then_inc(S["glu_sig"], 1)
                    split(l, U_GLU + 2 * i + 4)
                    act.wait_ge(S["xg_ready"], at("xg_ready", l, i + 1))
                    for c in range(2 * i, 2 * i + 2):
                        sc.activation(acc[:, c, :], xg[:, c, 0:SEQ], ACT.Identity, bias=vec4[:, 1, c:c + 1],
                                      scale=tap[:, 0, c:c + 1]).then_inc(S["conv_begun"], 1)
                for i in range(2):
                    act.wait_ge(S["unit_done"], at("unit_done", l, U_POOL + i + 1))
                    sc.activation(pooled[:, 2 * i:2 * i + 2, :], pair(6 + i), ACT.Copy).then_inc(S["px_ready"], 1)
                    split(l, U_POOL + i + 3)
                for i in range(2):
                    act.wait_ge(S["unit_done"], at("unit_done", l, U_U + i + 1))
                    sc.activation(u[:, 2 * i:2 * i + 2, :], pair(i), ACT.Gelu).then_inc(S["u_gelu"], 1)
                    split(l, U_U + i + 3)
                    if i == 0:
                        act.wait_ge(S["pooled_ready"], at("pooled_ready", l, 1))
                        sc.activation(pl_hi, pooled, ACT.Copy).then_inc(S["pooled_hi"], 1)
                    else:
                        act.wait_ge(S["v_ready"], at("v_ready", l, 1))
                        sc.activation(v_hi, vf, ACT.Copy).then_inc(S["v_hi_ready"], 1)
                for b in range(3):
                    for k, n in enumerate(U_GATE[b]):
                        act.wait_ge(S["unit_done"], at("unit_done", l, n + 1))
                        if b == 1 and k == 0:
                            act.wait_ge(S["pooled_ready"], at("pooled_ready", l, 1))
                        if b == 2 and k == 0:
                            act.wait_ge(S["us_lo"], at("us_lo", l, 1))
                        sc.activation(gate_of(b, k // 2)[:, 2 * (k % 2):2 * (k % 2) + 2, :],
                                      pair(6 + k % 2), ACT.Sigmoid).then_inc(S["gate_sig"], 1)
                        split(l, n + 3)
                        if n == U_PW - 1:
                            act.wait_ge(S["unit_done"], at("unit_done", l, U_PW + 1))
                            for i in range(GR):
                                sc.activation(y_hi[:, 0, i, :], pair(2 + i // 2)[:, i % 2, :], ACT.Copy,
                                              scale=vec4[:, 0, i:i + 1]).then_inc(S["yp_hi"], 1)
                            split(l, U_PW + 3)
                        if b == 1 and k == 1:
                            act.wait_ge(S["us_ready"], at("us_ready", l, 1))
                            sc.activation(y_hi[:, 1, :, :], us, ACT.Copy).then_inc(S["us_hi"], 1)
                        if b == 2 and k == 2:
                            act.wait_ge(S["centred"], at("centred", l, 1))
                            sc.activation(ctmp[:, :, :], acc[:, :, :], ACT.Square).then_inc(S["csq_ready"], 1)
                    if b == 0:
                        for n in U_OUT[0]:
                            split(l, n + 3)
                act.wait_ge(S["z_ready"], at("z_ready", l, 1))
                for c in range(CB):
                    last = sc.activation(ctmp[:, c, :], acc[:, c, :], ACT.Sigmoid,
                                         bias=vec4[:, 3, c:c + 1], scale=vec4[:, 2, c:c + 1])
                last.then_inc(S["zsig_ready"], 1)
                act.wait_ge(S["conv_y"], at("conv_y", l, 1))
                sc.activation(y_hi[:, 2, :, :], u[:, :, :], ACT.Copy).then_inc(S["cy_hi"], 1)
                for n in U_OUT[1]:
                    split(l, n + 3)
                for k, n in enumerate(U_OUT[2]):
                    if k == 0:
                        split(l, n + 3)
                    act.wait_ge(S["merged_ready"], at("merged_ready", l, 2 + k + 1))
                    sc.activation(nt_hi[:, 4 * k:4 * k + 4, :], merged[:, 4 * k:4 * k + 4, :], ACT.Copy
                                  ).then_inc(S["mg_hi"], 1)
                for n in (U_OUT[2][1], U_WOUT):
                    split(l, n + 3)
                boundary(l, 1, U_WOUT + 1)
                ffn(l, 1, U_FFN2)
                split(l, U_EMB + 3)
                for k in range(2):
                    split(l, U_PLEG + k + 3)

                def gate_sigmoid(t):
                    if t == 0:
                        act.wait_ge(S["tile0_done"], at("tile0_done", l, 4))
                    else:
                        act.wait_ge(S["unit_done"], at("unit_done", l, UNITS))
                    for b in range(2):
                        sc.activation(ge[:, t, half(b)], ps[:, 2 * t + b, :], ACT.Sigmoid).then_inc(S["ple_sig"], 1)

                def square_ge(t):
                    for b in range(2):
                        act.wait_ge(S["ge_ready"], at("ge_ready", l, 2 * t + b + 1))
                        square(NORM_OUT[3], t, b, ge[:, t, half(b)])

                gate_sigmoid(0)
                with act.If(DEPTH - 1 - l):
                    square_ge(0)
                    split(l, UNITS)
                    square_in(l + 1, 0, 0)
                    gate_sigmoid(1)
                    square_ge(1)
                    rows_hi(l + 1, 0, 0)
                    split(l, UNITS + 1)
                    square_in(l + 1, 0, 1)
                    rows_hi(l + 1, 0, 1)
                    split(l, UNITS + 2)
                with act.Else():
                    square_ge(0)
                    gate_sigmoid(1)
                    square_ge(1)

        @block.vector
        def _(dve):
            v = nc.vector

            def split(l, n, hi=None):
                s, w = n % RING, width(n)
                dve.wait_ge(S["w_hi_ready"], at("w_hi_ready", l, n + 1) if hi is None else hi)
                v.tensor_tensor(w_lo[:, s, 0:w], raw[:, s, 0:w], w_hi[:, s, 0:w].bitcast(F32), ALU.subtract
                                ).then_inc(S["w_lo_ready"], 1)

            def scale_rows(l, s, t, val, gain_landed=True):
                e = NORM_IN[s]
                dve.wait_ge(S["rstd_ready"], val)
                if t == 0 and gain_landed:
                    dve.wait_ge(S["pre_gain_landed"], at("pre_gain_landed", l, s, 16))
                for b in range(2):
                    v.scalar_tensor_tensor(xs[:, t, half(b)], h[:, t, half(b)], rs[:, e, t:t + 1],
                                           pre_gain[:, half(b)], ALU.mult, ALU.mult).then_inc(S["xn_ready"], 1)

            def rows_lo(l, s, t):
                base = 0 if s == 3 else 4
                for b in range(2):
                    dve.wait_ge(S["nt_hi_ready"], at("nt_hi_ready", l, 4 * s + 2 * t + b + 1))
                    part = (slice(None), slice(4 * b, 4 * b + 4), slice(t * P, (t + 1) * P))
                    v.tensor_tensor(nt_lo[part], quads(base, t, b), nt_hi[part].bitcast(F32), ALU.subtract
                                    ).then_inc(S["nt_lo_ready"], 1)

            def gain_rows(l, q, t, k, weight, source):
                slot, count = q % 2, q // 2 + 1
                if t == 0:
                    dve.wait_ge(S[f"gain_landed{slot}"], at(f"gain_landed{slot}", l, count, 16))
                for b in range(2):
                    dve.wait_ge(S["ssq_ready"], half_sums(l, q, k, b))
                    v.scalar_tensor_tensor(xs[:, t, half(b)], source[:, half(b)], weight, gain[:, slot, half(b)],
                                           ALU.mult, ALU.mult).then_inc(S["row_gained"], 1)

            def add_rows(l, q, t, val):
                e = NORM_OUT[q]
                dve.wait_ge(S["rstd_ready"], val)
                dve.wait_ge(S["row_gained"], at("row_gained", l, 4 * q + 2 * t + 2))
                for b in range(2):
                    v.scalar_tensor_tensor(h[:, t, half(b)], xs[:, t, half(b)], rs[:, e, t:t + 1],
                                           h[:, t, half(b)], ALU.mult, ALU.add).then_inc(S["h_ready"], 1)

            def boundary(l, q, a, weight):
                gain_rows(l, q, 0, 1, weight, rows(0))
                add_rows(l, q, 0, sums("rstd_ready", l, q, 1))
                scale_rows(l, q + 1, 0, sums("rstd_ready", l, q, 2))
                split(l, a + 3)
                rows_lo(l, q + 1, 0)
                split(l, a + 4)
                gain_rows(l, q, 1, 3, weight, rows(1))
                add_rows(l, q, 1, sums("rstd_ready", l, q, 3))
                scale_rows(l, q + 1, 1, sums("rstd_ready", l, q, 4))
                rows_lo(l, q + 1, 1)
                split(l, a + 5)

            def ffn(l, f, base):
                c0 = NCH * f

                def prepare():
                    dve.wait_ge(S["vecs_turned"], at("vecs_turned", l, 1))
                    v.tensor_copy(vec4[:, :, :], ps[:, 0, 0:NV * CB].rearrange("p (a c) -> p a c", a=NV)
                                  ).then_inc(S["vecs_ready"], 1)
                    v.tensor_copy(tap[:, :, :], ps[:, 0, P:P + TAPS * CB].rearrange("p (a c) -> p a c", c=CB)
                                  ).then_inc(S["vecs_ready"], 1)
                    for k, (hi, lo, b) in enumerate(((wst_hi, wst_lo, 1), (pt_hi, pt_lo, 2))):
                        dve.wait_ge(S["prep_hi"], at("prep_hi", l, k + 1))
                        src = ps[:, b, :].rearrange("p (c n) -> p c n", c=hi.shape[1])
                        v.tensor_tensor(lo[:, :, :], src, hi[:, :, :].bitcast(F32), ALU.subtract
                                        ).then_inc(S["prep_lo"], 1)

                def chunk(c, n, off=0, coff=0):
                    par = c % 2
                    dve.wait_ge(S["sg_ready"], at("sg_ready", l, c0 + c + 1) + coff)
                    v.tensor_tensor(sg[:, par, :, :], sg[:, par, :, :], pair(gate_bank(par)), ALU.mult
                                    ).then_inc(S["gate_read"], 1)
                    split(l, n + 3, hi=at("w_hi_ready", l, n + 4) + off)
                    dve.wait_ge(S["unit_done"], at("unit_done", l, n + 2) + off)
                    dve.wait_ge(S["gate_read"], at("gate_read", l, c0 + c + 1) + coff)
                    v.tensor_tensor(prod[:, par, :, :], sg[:, par, :, :], pair(up_bank(par)), ALU.mult
                                    ).then_inc(S["prod_ready"], 1)
                    if c == 0 and f == 0:
                        prepare()
                    split(l, n + 4, hi=at("w_hi_ready", l, n + 5) + off)
                    dve.wait_ge(S["act_hi_ready"], at("act_hi_ready", l, c0 + c + 1) + coff)
                    whole = pair(gate_bank(0)) if c == 0 else prod[:, par, :, :]
                    hi, lo = chunk_parts(c)
                    v.tensor_tensor(lo, whole, hi.bitcast(F32), ALU.subtract).then_inc(S["act_lo_ready"], 1)

                chunk(0, base)
                chunk(1, base + 2)
                split(l, base + 7)
                with dve.Fori(0, (NCH - 5) // 2) as i:
                    for k in range(2):
                        n = base + 5 + 3 * k
                        chunk(2 + k, n, off=i * 6, coff=i * 2)
                        split(l, n + 5, hi=at("w_hi_ready", l, n + 6) + i * 6)
                n = base + 3 * NCH - 10
                chunk(NCH - 3, n)
                split(l, n + 5)
                chunk(NCH - 2, n + 3)
                chunk(NCH - 1, n + 5)
                boundary(l, 2 * f, n + 7, 0.5)

            v.memset(xg[:, :, 0:PAD], 0.0)
            dve.wait_ge(S["inv_ready"], 1)
            for gi in range(GR - 1):
                last = v.tensor_scalar(inv[:, gi, :], inv[:, GR - 1, :], 1.0 / POOL_WINDOWS[gi], None, ALU.max)
            last.then_inc(S["const_ready"], 1)
            dve.wait_ge(S["first_gain_landed"], 16)
            for t in range(TT):
                scale_rows(0, 0, t, t + 1, gain_landed=False)
            split(0, 0)
            for t in range(TT):
                rows_lo(0, 0, t)
                split(0, t + 1)

            with dve.Fori(0, DEPTH) as l:
                ffn(l, 0, U_FFN1)

                jobs = [(j, c + i) for c in range(0, CB, 2) for j in range(1, TAPS) for i in range(2)]
                total = len(jobs)

                def convolve(count):
                    if not jobs:
                        return
                    for _ in range(min(count, len(jobs))):
                        j, c = jobs.pop(0)
                        src = xg[:, c, j:j + SEQ]
                        if j == 1:
                            dve.wait_ge(S["conv_begun"], at("conv_begun", l, c + 1))
                        else:
                            dve.wait_ge(S["tap_added"], at("tap_added", l, total - len(jobs) - 2))
                        ins = v.scalar_tensor_tensor(acc[:, c, :], src, tap[:, j, c:c + 1], acc[:, c, :],
                                                     ALU.mult, ALU.add)
                        ins.then_inc(S["tap_added"], 1)

                steps = [0]

                def step(ins):
                    steps[0] += 1
                    ins.then_inc(S["dve_step"], 1)

                def steps_done():
                    dve.wait_ge(S["dve_step"], at("dve_step", l, steps[0]))

                split(l, U_V + 3)
                for t in range(TT):
                    dve.wait_ge(S["v_gelu"], at("v_gelu", l, t + 1))
                    step(v.bn_stats(vst[:, t, :], vf[:, t, :]))
                steps_done()
                after(dve, "dve_waited")
                for t in range(TT):
                    v.bn_aggr(vmv[:, t, :], vst[:, t, :]).then_inc(S["v_stats"], 1)
                split(l, U_V + 4)
                dve.wait_ge(S["rowvecs_landed"], at("rowvecs_landed", l, 3, 16))
                dve.wait_ge(S["v_stats"], at("v_stats", l, 2))
                for t in range(TT):
                    step(v.scalar_tensor_tensor(vf[:, t, :], vf[:, t, :], vmv[:, t, 0:1], vln_g[:, :],
                                                ALU.subtract, ALU.mult))
                split(l, U_GLU + 3)
                steps_done()
                dve.wait_ge(S["v_rstd"], at("v_rstd", l, 2))
                for t in range(TT):
                    last = v.scalar_tensor_tensor(vf[:, t, :], vf[:, t, :], vrs[:, t:t + 1], vln_b[:, :],
                                                  ALU.mult, ALU.add)
                last.then_inc(S["v_ready"], 1)
                dve.wait_ge(S["vecs_ready"], at("vecs_ready", l, 2))
                for i in range(2):
                    dve.wait_ge(S["glu_sig"], at("glu_sig", l, i + 1))
                    v.tensor_tensor(xg[:, 2 * i:2 * i + 2, PAD:], ctmp[:, 2 * i:2 * i + 2, :], pair(2 * i), ALU.mult
                                    ).then_inc(S["xg_ready"], 1)
                    if i == 0:
                        split(l, U_GLU + 4)
                        convolve(8)
                        split(l, U_GLU + 5)
                        convolve(4)
                    else:
                        split(l, U_GLU + 6)
                        convolve(10)
                split(l, U_POOL + 3)

                dve.wait_ge(S["px_ready"], at("px_ready", l, 2))
                source = pooled
                for gi, w in enumerate(POOL_WINDOWS):
                    d = w // 2
                    target = (sum_a, sum_b)[gi % 2]
                    v.tensor_copy(target[:, gi:, 0:d], source[:, gi:, 0:d])
                    step(v.tensor_tensor(target[:, gi:, d:], source[:, gi:, d:], source[:, gi:, 0:SEQ - d], ALU.add))
                    steps_done()
                    source = target
                W0 = POOL_WINDOWS[-1]
                for k, part_sums in enumerate((sum_a, sum_b)):
                    ins = v.tensor_tensor(part_sums[:, k::2, 0:W0], part_sums[:, k::2, 0:W0], inv[:, k::2, :], ALU.mult)
                step(ins)
                for gi, w in enumerate(POOL_WINDOWS):
                    part_sums = (sum_a, sum_b)[gi % 2]
                    v.scalar_tensor_tensor(pooled[:, gi, W0:], part_sums[:, gi, W0:], 1.0 / w, pooled[:, gi, W0:],
                                           ALU.mult, ALU.subtract)
                steps_done()
                for k, part_sums in enumerate((sum_a, sum_b)):
                    ins = v.tensor_tensor(pooled[:, k::2, 0:W0], part_sums[:, k::2, 0:W0], pooled[:, k::2, 0:W0],
                                          ALU.subtract)
                ins.then_inc(S["pooled_ready"], 1)
                split(l, U_POOL + 4)
                convolve(8)
                split(l, U_U + 3)
                dve.wait_ge(S["pooled_hi"], at("pooled_hi", l, 1))
                v.tensor_tensor(pl_lo, pooled, pl_hi.bitcast(F32), ALU.subtract).then_inc(S["pooled_lo"], 1)
                convolve(6)
                split(l, U_U + 4)
                convolve(5)
                dve.wait_ge(S["v_hi_ready"], at("v_hi_ready", l, 1))
                v.tensor_tensor(v_lo, vf, v_hi.bitcast(F32), ALU.subtract).then_inc(S["v_lo_ready"], 1)
                xa = u[:, :, :]

                def weigh(b, k):
                    bank = 2 * k if b < 2 else 4 + 2 * k
                    made = ps[:, bank:bank + 2, :].rearrange("p b (c n) -> p (b c) n", c=2)
                    dve.wait_ge(S["unit_done"], at("unit_done", l, U_OUT[b][k] + 1))
                    dve.wait_ge(S["gate_sig"], at("gate_sig", l, 4 * b + 2 * k + 2))
                    v.tensor_tensor(merged[:, 4 * k:4 * k + 4, :] if b == 0 else gate_of(b, k), gate_of(b, k), made,
                                    ALU.mult).then_inc(S["out_read"], 1)

                def add_branch(b, k):
                    m = slice(4 * k, 4 * k + 4)
                    dve.wait_ge(S["out_read"], at("out_read", l, 2 * b + k + 1))
                    v.tensor_tensor(merged[:, m, :], merged[:, m, :], gate_of(b, k), ALU.add
                                    ).then_inc(S["merged_ready"], 1)

                for k, n in enumerate(U_GATE[0]):
                    split(l, n + 3)
                    convolve((4, 4, 0, 8)[k])
                    if n == U_PW - 1:
                        for i in range(GR):
                            if i % 2 == 0:
                                dve.wait_ge(S["yp_hi"], at("yp_hi", l, i + 2))
                            v.scalar_tensor_tensor(y_lo[:, 0, i, :], pair(2 + i // 2)[:, i % 2, :],
                                                   vec4[:, 0, i:i + 1], y_hi[:, 0, i, :].bitcast(F32),
                                                   ALU.mult, ALU.subtract).then_inc(S["yp_lo"], 1)
                        split(l, U_PW + 3)
                        convolve(5)
                for n in U_OUT[0]:
                    split(l, n + 3)
                    convolve(8)

                def sum_tiles(i):
                    dve.wait_ge(S["tap_added"], at("tap_added", l, (i + 1) * total // 2))
                    v.tensor_tensor(half_sum[i], acc[:, 2 * i, :], acc[:, 2 * i + 1, :], ALU.add
                                    ).then_inc(S["acc_summed"], 1)

                assert len(jobs) < total // 2
                sum_tiles(0)
                for k, n in enumerate(U_GATE[1] + U_GATE[2]):
                    if k == 7:
                        dve.wait_ge(S["stat_done"], at("stat_done", l, 1))
                        mean = ps[:, 4, 0:SEQ].unsqueeze(1).broadcast_to([P, CB, SEQ])
                        v.tensor_tensor(acc[:, :, :], acc[:, :, :], mean, ALU.subtract
                                        ).then_inc(S["centred"], 1)
                        for i in range(2):
                            weigh(0, i)
                        break
                    split(l, n + 3)
                    if k == 1:
                        dve.wait_ge(S["s_done"], at("s_done", l, 1))
                        for c in range(TT):
                            part = (slice(None), slice(None), slice(c * P, (c + 1) * P))
                            gated = ps[:, 4:6, :].rearrange("p b (c n) -> p (b c) n", c=2)
                            step(v.tensor_tensor(s1[part], gated[part], bs[:, :, :], ALU.add))
                        steps_done()
                        dve.wait_ge(S["u_gelu"], at("u_gelu", l, 2))
                        v.tensor_tensor(us, s1, u[:, :, :], ALU.mult).then_inc(S["us_ready"], 1)
                        convolve(4)
                        dve.wait_ge(S["us_hi"], at("us_hi", l, 1))
                        v.tensor_tensor(y_lo[:, 1, :, :], us, y_hi[:, 1, :, :].bitcast(F32), ALU.subtract
                                        ).then_inc(S["us_lo"], 1)
                    else:
                        convolve(8)
                    if k == 5:
                        assert not jobs
                        sum_tiles(1)
                dve.wait_ge(S["stat_done"], at("stat_done", l, 2))
                v.tensor_scalar(cvar[:, :], ps[:, 5, 0:TT], EPS, None, ALU.add).then_inc(S["cvar_ready"], 1)
                dve.wait_ge(S["crstd_ready"], at("crstd_ready", l, 1))
                for t in range(TT):
                    ins = v.tensor_scalar(diag[:, t, :], ident[:, :], crs[:, t:t + 1], None, ALU.mult)
                ins.then_inc(S["diag_ready"], 1)
                split(l, U_GATE[2][3] + 3)
                dve.wait_ge(S["stat_done"], at("stat_done", l, 3))
                root = ps[:, 4, SEQ:2 * SEQ].unsqueeze(1).broadcast_to([P, CB, SEQ])
                v.tensor_tensor(acc[:, :, :], acc[:, :, :], root, ALU.mult).then_inc(S["z_ready"], 1)
                dve.wait_ge(S["z_ready"], at("z_ready", l, 1))
                for c in range(CB):
                    ins = v.tensor_scalar(xa[:, c, :], acc[:, c, :], vec4[:, 2, c:c + 1], vec4[:, 3, c:c + 1],
                                          ALU.mult, ALU.add)
                step(ins)
                weigh(1, 0)
                steps_done()
                dve.wait_ge(S["zsig_ready"], at("zsig_ready", l, 1))
                v.tensor_tensor(xa, xa, ctmp[:, :, :], ALU.mult).then_inc(S["conv_y"], 1)
                add_branch(1, 0)
                dve.wait_ge(S["cy_hi"], at("cy_hi", l, 1))
                v.tensor_tensor(y_lo[:, 2, :, :], xa, y_hi[:, 2, :, :].bitcast(F32), ALU.subtract
                                ).then_inc(S["cy_lo"], 1)
                split(l, U_OUT[1][0] + 3)
                weigh(1, 1)
                add_branch(1, 1)
                split(l, U_OUT[1][1] + 3)
                for k, n in enumerate(U_OUT[2]):
                    weigh(2, k)
                    add_branch(2, k)
                    if k == 0:
                        split(l, n + 3)
                    dve.wait_ge(S["mg_hi"], at("mg_hi", l, k + 1))
                    m = slice(4 * k, 4 * k + 4)
                    v.tensor_tensor(nt_lo[:, m, :], merged[:, m, :], nt_hi[:, m, :].bitcast(F32), ALU.subtract
                                    ).then_inc(S["mg_lo"], 1)
                split(l, U_OUT[2][1] + 3)
                assert steps[0] == DVE_STEPS, steps
                split(l, U_WOUT + 3)
                boundary(l, 1, U_WOUT + 1, 1.0)
                ffn(l, 1, U_FFN2)
                split(l, U_EMB + 3)
                for k in range(2):
                    split(l, U_PLEG + k + 3)

                def gate_rows(t):
                    for b in range(2):
                        dve.wait_ge(S["ple_sig"], at("ple_sig", l, 2 * t + b + 1))
                        v.tensor_tensor(ge[:, t, half(b)], ge[:, t, half(b)], ps[:, 4 + 2 * t + b, :], ALU.mult
                                        ).then_inc(S["ge_ready"], 1)

                gate_rows(0)
                with dve.If(DEPTH - 1 - l):
                    gain_rows(l, 3, 0, 1, 1.0, ge[:, 0, :])
                    add_rows(l, 3, 0, sums("rstd_ready", l, 3, 1))
                    split(l, UNITS)
                    scale_rows(l + 1, 0, 0, sums("rstd_ready", l, 3, 2))
                    gate_rows(1)
                    gain_rows(l, 3, 1, 3, 1.0, ge[:, 1, :])
                    rows_lo(l + 1, 0, 0)
                    add_rows(l, 3, 1, sums("rstd_ready", l, 3, 3))
                    split(l, UNITS + 1)
                    scale_rows(l + 1, 0, 1, sums("rstd_ready", l, 3, 4))
                    rows_lo(l + 1, 0, 1)
                    split(l, UNITS + 2)
                with dve.Else():
                    gain_rows(l, 3, 0, 1, 1.0, ge[:, 0, :])
                    add_rows(l, 3, 0, sums("rstd_ready", l, 3, 1))
                    gate_rows(1)
                    gain_rows(l, 3, 1, 2, 1.0, ge[:, 1, :])
                    add_rows(l, 3, 1, sums("rstd_ready", l, 3, 2))

        @block.tensor
        def _(pe):
            te = nc.tensor

            def product(o, a_hi, a_lo, b_hi, b_lo, start, stop):
                te.matmul(o, a_hi, b_hi, start=start, stop=False)
                te.matmul(o, a_hi, b_lo, start=False, stop=False)
                return te.matmul(o, a_lo, b_hi, start=False, stop=stop)

            def loaded(l, n, off=0):
                pe.wait_ge(S["w_lo_ready"], at("w_lo_ready", l, n + 1) + off)

            def turn(l, s, t):
                base = 0 if s == 3 else 4
                for k in range(KD):
                    if k % 4 == 0:
                        pe.wait_ge(S["xn_ready"], at("xn_ready", l, 4 * s + 2 * t + k // 4 + 1))
                    ins = te.transpose(quads(base, t, k // 4)[:, k % 4, :], xs[:, t, k * P:(k + 1) * P], ident[:, :])
                    if k % 4 == 3:
                        ins.then_inc(S["xt_done"], 1)

            def rows_split(l, s, t):
                pe.wait_ge(S["nt_lo_ready"], at("nt_lo_ready", l, 4 * s + 2 * t + 2))

            def by_channel(n, bank, x_hi, x_lo, kt, tiles, between=None):
                s = n % RING
                w = width(n) // kt
                tok = slice(0, SEQ)
                for c in range(tiles):
                    if c == tiles // 2 and between is not None:
                        between()
                    for k in range(kt):
                        at_ = slice(k * w + c * P, k * w + (c + 1) * P)
                        ins = product(pair(bank + c // 2)[:, c % 2, tok], w_hi[:, s, at_], w_lo[:, s, at_],
                                      x_hi[:, k, tok], x_lo[:, k, tok], k == 0, k == kt - 1)
                return ins

            def across(n, bank, col, t):
                x_at = slice(t * P, (t + 1) * P)
                for k in range(KD):
                    at_ = slice(k * FC, (k + 1) * FC)
                    ins = product(ps[:, bank, col:col + FC], nt_hi[:, k, x_at], nt_lo[:, k, x_at],
                                  w_hi[:, n % RING, at_], w_lo[:, n % RING, at_], k == 0, k == KD - 1)
                return ins

            def first_two(l, s, n, place):
                loaded(l, n)
                rows_split(l, s, 0)
                across(n, *place(0, 0), 0)
                loaded(l, n + 1)
                across(n + 1, *place(1, 0), 0)
                turn(l, s, 1)
                rows_split(l, s, 1)
                for i in range(2):
                    done(across(n + i, *place(i, 1), 1))

            def by_token(t, n, base, x_hi, x_lo, k0, kt, start, stop, between=None):
                s = n % RING
                x_at = slice(t * P, (t + 1) * P)
                for k in range(kt):
                    if k == kt - 1 and between is not None:
                        between()
                    for b in range(2):
                        at_ = slice(k * D + b * BANK, k * D + (b + 1) * BANK)
                        ins = product(ps[:, base + 2 * t + b, :], x_hi[:, k0 + k, x_at], x_lo[:, k0 + k, x_at],
                                      w_hi[:, s, at_], w_lo[:, s, at_], start and k == 0, stop and k == kt - 1)
                return ins

            def done(ins):
                ins.then_inc(S["unit_done"], 1)

            def last_three(l, n, part, following=None):
                for t in range(TT):
                    for k in range(3):
                        if t == 0:
                            loaded(l, n + k)
                        last = t == 1 and k == 2 and following is not None
                        ins = part(k, t, (lambda: turn(l, following, 0)) if last else None)
                        if t == 1:
                            done(ins)
                    if t == 0:
                        ins.then_inc(S["tile0_done"], 1)

            def ffn(l, f, base):
                c0 = NCH * f

                def gate(c, n, off=0, coff=0, free=True):
                    loaded(l, n, off)
                    if free:
                        pe.wait_ge(S["gate_read"], at("gate_read", l, c0 + c - 1) + coff)
                    done(by_channel(n, gate_bank(c), nt_hi, nt_lo, KD, 2))

                def up(c, n, off=0, coff=0, free=True):
                    loaded(l, n, off)
                    if free:
                        pe.wait_ge(S["prod_ready"], at("prod_ready", l, c0 + c - 1) + coff)
                    done(by_channel(n, up_bank(c), nt_hi, nt_lo, KD, 2))

                def down(c, n, off=0, coff=0, start=False):
                    loaded(l, n, off)
                    pe.wait_ge(S["act_lo_ready"], at("act_lo_ready", l, c0 + c + 1) + coff)
                    for t in range(TT):
                        ins = by_token(t, n, 0, *chunk_parts(c), 0, 2, start, False)
                    done(ins)

                def last_down(k, t, between):
                    c = NCH - 3 + k
                    pe.wait_ge(S["act_lo_ready"], at("act_lo_ready", l, c0 + c + 1))
                    return by_token(t, base + 3 * NCH - 3 + k, 0, *chunk_parts(c), 0, 2, False, k == 2, between)

                if f == 0:
                    turn(l, 0, 0)
                first_two(l, 2 * f, base, lambda i, t: ((gate_bank(0), up_bank(0))[i], t * FC))
                if f == 0:
                    pe.wait_ge(S["vec_landed"], at("vec_landed", l, NV + 1, 16))
                    after(pe, "pe_waited")
                    te.transpose(ps[:, 0, 0:NV * CB], vec_rows[0:NV * CB, :], ident[0:NV * CB, 0:NV * CB])
                    te.transpose(ps[:, 0, P:P + TAPS * CB], tap_rows[0:TAPS * CB, :], ident[0:TAPS * CB, 0:TAPS * CB]
                                 ).then_inc(S["vecs_turned"], 1)
                    pe.wait_ge(S["ws_masked"], at("ws_masked", l, 1))
                    for i in range(4):
                        ins = te.transpose(ps[:, 1, i * P:(i + 1) * P], ws[:, i, :], ident[:, :])
                    ins.then_inc(S["prep_done"], 1)
                    pe.wait_ge(S["p_landed"], at("p_landed", l, 1, 16))
                    for k in range(2):
                        for t in range(TT):
                            ins = te.transpose(pair(2)[:, k, t * P:(t + 1) * P], p_in[:, t, k * P:(k + 1) * P],
                                               ident[:, :])
                    ins.then_inc(S["prep_done"], 1)
                gate(1, base + 2, free=False)
                pe.wait_ge(S["prod_ready"], at("prod_ready", l, c0 + 1))
                for k in range(2):
                    for t in range(TT):
                        ins = te.transpose(pair(gate_bank(0))[:, k, t * P:(t + 1) * P],
                                           prod[:, 0, t, k * P:(k + 1) * P], ident[:, :])
                ins.then_inc(S["act_turned"], 1)
                up(1, base + 3, free=False)
                if f == 0:
                    pe.wait_ge(S["vecs_ready"], at("vecs_ready", l, 2))
                    pe.wait_ge(S["prep_lo"], at("prep_lo", l, 2))
                down(0, base + 4, start=True)
                with pe.Fori(0, (NCH - 5) // 2) as i:
                    for k in range(2):
                        n = base + 5 + 3 * k
                        gate(2 + k, n, i * 6, i * 2)
                        up(2 + k, n + 1, i * 6, i * 2)
                        down(1 + k, n + 2, i * 6, i * 2)
                n = base + 3 * NCH - 10
                for c in range(NCH - 3, NCH):
                    gate(c, n)
                    up(c, n + 1)
                    n += 2
                    if c == NCH - 3:
                        down(c - 1, n)
                        n += 1
                last_three(l, n, last_down, 2 * f + 1)

            pe.wait_ge(S["ident_ready"], 1)
            with pe.Fori(0, DEPTH) as l:
                ffn(l, 0, U_FFN1)
                first_two(l, 1, U_V, lambda i, t: (4 + t, i * FC))
                for k in range(4):
                    n = U_GLU + k
                    loaded(l, n)
                    done(by_channel(n, k, nt_hi, nt_lo, KD, 2))
                for k in range(2):
                    n = U_POOL + k
                    loaded(l, n)
                    done(by_channel(n, 6 + k, nt_hi, nt_lo, KD, 2))
                for i in range(2):
                    n = U_U + i
                    loaded(l, n)
                    pe.wait_ge(S["xg_ready"], at("xg_ready", l, 1))
                    done(by_channel(n, i, nt_hi, nt_lo, KD, 2))

                def gates_unit(b, k, between=None):
                    n, j = U_GATE[b][k], 4 * b + k
                    loaded(l, n)
                    if j >= 2:
                        pe.wait_ge(S["gate_sig"], at("gate_sig", l, j - 1))
                    else:
                        pe.wait_ge(S["px_ready"], at("px_ready", l, j + 1))
                    done(by_channel(n, 6 + k % 2, nt_hi, nt_lo, KD, 2, between))

                def out_unit(b, k, between=None):
                    n = U_OUT[b][k]
                    loaded(l, n)
                    if b == 1:
                        pe.wait_ge(S["out_read"], at("out_read", l, 1 + k))
                    done(by_channel(n, 2 * k if b < 2 else 4 + 2 * k, y_hi[:, b, :, :], y_lo[:, b, :, :], CB, 4,
                                    between=between))

                for k in range(3):
                    gates_unit(0, k)
                loaded(l, U_PW)
                pe.wait_ge(S["xg_ready"], at("xg_ready", l, 2))
                pe.wait_ge(S["pooled_lo"], at("pooled_lo", l, 1))
                s = U_PW % RING
                for i in range(GR):
                    ins = product(pair(2 + i // 2)[:, i % 2, :], w_hi[:, s, i * P:(i + 1) * P],
                                  w_lo[:, s, i * P:(i + 1) * P], pl_hi[:, i, :], pl_lo[:, i, :], True, True)
                done(ins)
                gates_unit(0, 3)
                pe.wait_ge(S["yp_lo"], at("yp_lo", l, 4))
                pe.wait_ge(S["u_gelu"], at("u_gelu", l, 2))
                for k in range(2):
                    out_unit(0, k)
                gates_unit(1, 0)
                pe.wait_ge(S["v_lo_ready"], at("v_lo_ready", l, 1))
                for i in range(4):
                    for t in range(TT):
                        ins = product(pair(4 + i // 2)[:, i % 2, t * P:(t + 1) * P], v_hi[:, t, i * P:(i + 1) * P],
                                      v_lo[:, t, i * P:(i + 1) * P], wst_hi[:, i, :], wst_lo[:, i, :], True, True)
                ins.then_inc(S["s_done"], 1)
                for k in range(1, 4):
                    gates_unit(1, k)
                def means():
                    for i in range(2):
                        pe.wait_ge(S["acc_summed"], at("acc_summed", l, i + 1))
                        ins = te.matmul(ps[:, 4, 0:SEQ], mean_w[:, :], half_sum[i], start=i == 0, stop=i == 1)
                    ins.then_inc(S["stat_done"], 1)

                for k in range(4):
                    gates_unit(2, k, means if k == 3 else None)
                pe.wait_ge(S["csq_ready"], at("csq_ready", l, 1))
                for t in range(TT):
                    for c in range(CB):
                        ins = te.matmul(ps[:, 5, t:t + 1], ctmp[:, c, t * P:(t + 1) * P], mean_w[:, 0:1],
                                        start=c == 0, stop=c == CB - 1)
                ins.then_inc(S["stat_done"], 1)

                def roots():
                    pe.wait_ge(S["diag_ready"], at("diag_ready", l, 1))
                    for t in range(TT):
                        ins = te.matmul(ps[:, 4, SEQ + t * P:SEQ + (t + 1) * P], ones[:, :], diag[:, t, :],
                                        start=True, stop=True)
                    ins.then_inc(S["stat_done"], 1)

                pe.wait_ge(S["us_lo"], at("us_lo", l, 1))
                out_unit(1, 0, roots)
                out_unit(1, 1)
                pe.wait_ge(S["cy_lo"], at("cy_lo", l, 1))
                for k in range(2):
                    out_unit(2, k)
                pe.wait_ge(S["out_read"], at("out_read", l, 4))
                loaded(l, U_WOUT)
                pe.wait_ge(S["mg_lo"], at("mg_lo", l, 1))
                for t in range(TT):
                    ins = by_token(t, U_WOUT, 0, nt_hi, nt_lo, 0, 2, True, False)
                done(ins)

                def last_out(k, t, between):
                    if k == 1:
                        pe.wait_ge(S["mg_lo"], at("mg_lo", l, 2))
                    return by_token(t, U_WOUT + 1 + k, 0, nt_hi, nt_lo, 2 + 2 * k, 2, False, k == 2,
                                    between)

                last_three(l, U_WOUT + 1, last_out, 2)
                ffn(l, 1, U_FFN2)
                loaded(l, U_EMB)
                pe.wait_ge(S["prod_ready"], at("prod_ready", l, 2 * NCH))
                for t in range(TT):
                    ins = by_token(t, U_EMB, 4, pt_hi, pt_lo, 0, 2, True, True)
                done(ins)
                loaded(l, U_PLEG)
                rows_split(l, 3, 0)
                by_token(0, U_PLEG, 0, nt_hi, nt_lo, 0, 1, True, False)
                turn(l, 3, 1)
                rows_split(l, 3, 1)
                done(by_token(1, U_PLEG, 0, nt_hi, nt_lo, 0, 1, True, False))
                loaded(l, U_PLEG + 1)
                for t in range(TT):
                    ins = by_token(t, U_PLEG + 1, 0, nt_hi, nt_lo, 1, 1, False, False)
                done(ins)
                last_three(l, U_PLEG + 2, lambda k, t, between: by_token(
                    t, U_PLEG + 2 + k, 0, nt_hi, nt_lo, 2 + 2 * k, 2, False, k == 2))


_INS = [
    "x", "p", "ffn1_pre_g", "ffn1_w_gate", "ffn1_w_up", "ffn1_w_down", "ffn1_post_g", "mix_pre_g", "w_in",
    "pool_w", "pool_scale", "w_pool_out", "sgu_ln_g", "sgu_ln_b", "sgu_w_s", "sgu_b_s", "w_sgu_out",
    "conv_dw_k", "conv_dw_b", "conv_ln_g", "conv_ln_b", "w_conv_out", "w_out", "mix_post_g", "ffn2_pre_g",
    "ffn2_w_gate", "ffn2_w_up", "ffn2_w_down", "ffn2_post_g", "ple_w_proj", "ple_pre_g", "ple_w_gate",
    "ple_post_g",
]


def kernel(**inputs):
    import numpy as np
    import concourse.bacc as bacc
    from concourse.bass_utils import run_bass_kernel_spmd

    nc = bacc.Bacc("TRN2", target_bir_lowering=False, num_devices=1)
    arrays, aps = {}, {}
    for name in _INS:
        a = np.ascontiguousarray(inputs[name])
        arrays[f"in_{name}"] = a
        aps[name] = nc.dram_tensor(f"in_{name}", a.shape, mybir.dt.from_np(a.dtype), kind="ExternalInput").ap()
    out = nc.dram_tensor("out", inputs["x"].shape, F32, kind="ExternalOutput").ap()
    hybrid_trunk(nc, aps, out)
    r = run_bass_kernel_spmd(nc, [arrays], core_ids=[0])
    return r.results[0]["out"]
```

```python
from contextlib import ExitStack

import concourse.bass as bass
from concourse import mybir

ALU = mybir.AluOpType
ACT = mybir.ActivationFunctionType
F32 = mybir.dt.float32
F32R = mybir.dt.float32r

P = 128
EPS = 1e-6
RING = 3
UNIT = 2048
BANK = 512
POOL_WINDOWS = (2, 4, 8, 16)


def hybrid_trunk(nc, A, out):
    DEPTH, D, F = A["ffn1_w_gate"].shape
    SEQ = A["x"].shape[1]
    TT = SEQ // P
    KD = D // P
    FC = 2 * P
    NCH = F // FC
    GR = len(POOL_WINDOWS)
    WB = A["w_pool_out"].shape[1]
    CB = WB // P
    TAPS = A["conv_dw_k"].shape[1]
    PAD = TAPS - 1
    PLE = A["p"].shape[3]
    ROOT = 32
    assert ROOT * ROOT == D
    assert (SEQ, D, NCH * FC, WB, PLE) == (2 * P, 8 * P, F, 4 * P, 2 * P) and NCH == 11

    FFN_UNITS = 3 * NCH
    U_FFN1 = 0
    U_MIX = U_FFN1 + FFN_UNITS
    U_V, U_GLU, U_POOL, U_U = U_MIX, U_MIX + 2, U_MIX + 6, U_MIX + 8
    n = U_U + 2
    U_GATE = [[n, n + 1, n + 2, n + 4], list(range(n + 7, n + 11)), list(range(n + 11, n + 15))]
    U_PW = n + 3
    U_OUT = [[n + 5, n + 6], [n + 15, n + 16], [n + 17, n + 18]]
    U_WOUT = n + 19
    U_FFN2 = U_WOUT + 4
    U_EMB = U_FFN2 + FFN_UNITS
    U_PLEG = U_EMB + 1
    UNITS = U_PLEG + 5
    assert UNITS % RING == 0 and U_FFN2 % RING == 0

    def width(n):
        n = n % UNITS
        return GR * P if n == U_PW else D if U_PLEG <= n < U_PLEG + 2 else UNIT

    with ExitStack() as ctx:
        def sb(name, shape, dt=F32):
            return ctx.enter_context(nc.sbuf_tensor(name, [P] + shape, dt))

        per_layer = {}

        def sem(name, per=None):
            s = ctx.enter_context(nc.semaphore(name))
            per_layer[name] = per
            sems[name] = s
            return name

        sems = {}

        def at(name, l, k, by=1):
            return l * (per_layer[name] * by) + k * by

        raw = sb("raw", [RING, UNIT])
        w_hi = sb("w_hi", [RING, UNIT], F32R)
        w_lo = sb("w_lo", [RING, UNIT], F32R)
        h = sb("h", [TT, D])
        xs = sb("xs", [TT, D])
        nt_hi = sb("nt_hi", [KD, SEQ], F32R)
        nt_lo = sb("nt_lo", [KD, SEQ], F32R)
        pre_gain = sb("pre_gain", [D])
        gain = sb("gain", [2, D])
        sg = sb("sg", [2, 2, SEQ])
        prod = sb("prod", [2, 2, SEQ])
        act_hi = sb("act_hi", [2, 2, SEQ], F32R)
        act_lo = sb("act_lo", [2, 2, SEQ], F32R)
        xg = sb("xg", [CB, PAD + SEQ])
        acc = sb("acc", [CB, SEQ])
        gates = sb("gates", [KD, SEQ])
        merged = sb("merged", [KD, SEQ])
        y_hi = sb("y_hi", [3, CB, SEQ], F32R)
        y_lo = sb("y_lo", [3, CB, SEQ], F32R)
        u = sb("u", [CB, SEQ])
        ctmp = sb("ctmp", [CB, SEQ])
        wst_hi = sb("wst_hi", [4, P], F32R)
        wst_lo = sb("wst_lo", [4, P], F32R)
        bs = sb("bs", [4, P])
        vln_g = sb("vln_g", [WB])
        vln_b = sb("vln_b", [WB])
        pt_hi = sb("pt_hi", [2, SEQ], F32R)
        pt_lo = sb("pt_lo", [2, SEQ], F32R)
        ident = sb("ident", [P])
        ones = sb("ones", [P])
        mean_w = sb("mean_w", [P])
        diag = sb("diag", [TT, P])
        inv = sb("inv", [GR, 16])
        minus_half = sb("minus_half", [1])
        ss = sb("ss", [8, TT, 2])
        ms = sb("ms", [8, TT])
        rs = sb("rs", [8, TT])
        vst = sb("vst", [TT, 6])
        vmv = sb("vmv", [TT, 2])
        vms = sb("vms", [TT])
        vrs = sb("vrs", [TT])
        cvar = sb("cvar", [TT])
        crs = sb("crs", [TT])
        VECS = ("pool_scale", "conv_dw_b", "conv_ln_g", "conv_ln_b")
        NV = len(VECS)
        vec4 = sb("vec4", [NV, CB])
        tap = sb("tap", [TAPS, CB])
        vec_rows = u[:, 0, 0:P]
        tap_rows = u[:, 1, 0:P]
        ws = ctmp[:, 0:2, :].rearrange("p c (h s) -> p (c h) s", h=2)
        p_in = ctmp[:, 2:4, :]
        pooled = merged[:, 0:CB, :]
        sum_a = sg[:, :, :, :].rearrange("p a b n -> p (a b) n")
        sum_b = prod[:, :, :, :].rearrange("p a b n -> p (a b) n")
        pl_hi = act_hi[:, :, :, :].rearrange("p a b n -> p (a b) n")
        pl_lo = act_lo[:, :, :, :].rearrange("p a b n -> p (a b) n")

        def gate_of(b, k):
            if b == 0:
                return gates[:, 4 * k:4 * k + 4, :]
            return (sum_a, sum_b)[k] if b == 1 else xs[:, k, :].rearrange("p (c n) -> p c n", c=CB)

        vf = xs[:, 0, :].rearrange("p (t n) -> p t n", t=TT)
        us = xs[:, 0, :].rearrange("p (c n) -> p c n", c=CB)
        s1 = xs[:, 1, :].rearrange("p (c n) -> p c n", c=CB)
        half_sum = [ctmp[:, 0, :], ctmp[:, 1, :]]
        v_hi = y_hi[:, 2, :, :].rearrange("p c n -> p (c n)").rearrange("p (t n) -> p t n", t=TT)
        v_lo = y_lo[:, 2, :, :].rearrange("p c n -> p (c n)").rearrange("p (t n) -> p t n", t=TT)
        junk = gates[:, :, :].rearrange("p k n -> p (k n)").rearrange("p (t n) -> p t n", t=TT)
        ge = merged[:, :, :].rearrange("p k n -> p (k n)").rearrange("p (t n) -> p t n", t=TT)

        ps = ctx.enter_context(nc.psum_tensor("ps", [P, 8, BANK], F32))

        def pair(b):
            return ps[:, b, :].rearrange("p (c n) -> p c n", c=2)

        def gate_bank(c):
            return 4 + 2 * (c % 2)

        def up_bank(c):
            return 5 + 2 * (c % 2)

        def quads(s, t, b):
            bank = 2 + b if t == 1 else b if s == 3 else 4 + b
            return ps[:, bank, :].rearrange("p (k n) -> p k n", k=4)

        def half(b):
            return slice(b * BANK, (b + 1) * BANK)

        def rows(t, base=0):
            return ps[:, base + 2 * t:base + 2 * t + 2, :].rearrange("p b n -> p (b n)")

        OUT_READ = ((1, 2), (3, 5), (4, 6))
        MERGED = ((0, 0), (1, 3), (2, 4))

        def out_bank(b, k):
            return ((0, 2), (6, 0), (2, 4))[b][k]

        def chunk_parts(c):
            if c == NCH - 1:
                return y_hi[:, 0, 0:2, :], y_lo[:, 0, 0:2, :]
            return act_hi[:, c % 2, :, :], act_lo[:, c % 2, :, :]

        landed = [sem(f"landed{s}", UNITS // RING) for s in range(RING)]
        for name, per in {
            "w_hi_ready": UNITS, "w_lo_ready": UNITS, "unit_done": UNITS,
            "h_ready": 16, "ssq_ready": 32, "ms_ready": 16, "rstd_ready": 16, "xn_ready": 16,
            "xt_done": 16, "nt_hi_ready": 16, "nt_lo_ready": 16, "pre_gain_landed": 4, "row_gained": 16,
            "tile0_done": 4,
            "vecs_ready": 2, "vecs_turned": 1, "vec_landed": NV + 1,
            "sg_ready": 2 * NCH, "gate_read": 2 * NCH, "prod_ready": 2 * NCH,
            "act_hi_ready": 2 * NCH, "act_lo_ready": 2 * NCH,
            "ws_landed": 1, "ws_masked": 1, "p_landed": 1, "gain_landed0": 2, "gain_landed1": 2,
            "rowvecs_landed": 3, "prep_done": 2, "prep_hi": 2, "prep_lo": 2,
            "glu_sig": 2, "xg_ready": 2, "px_ready": 2, "dve_step": 0, "pooled_ready": 1,
            "pooled_hi": 1, "pooled_lo": 1, "v_gelu": 2, "v_stats": 2, "v_ready": 1,
            "v_ms": 2, "v_rstd": 2, "v_hi_ready": 1, "v_lo_ready": 1,
            "u_gelu": 2, "yp_hi": 4, "yp_lo": 4, "act_turned": 4, "half_lo_ready": 6,
            "s_done": 1, "us_ready": 1, "us_hi": 1, "us_lo": 1,
            "gate_sig": 12, "out_read": 6, "merged_ready": 4, "mg_hi": 2, "mg_lo": 2,
            "tap_added": PAD * CB, "stat_done": 3, "centred": 1, "csq_ready": 1, "cvar_ready": 1,
            "crstd_ready": 1, "diag_ready": 1, "z_ready": 2, "zsig_ready": 2,
            "conv_y": 2, "cy_hi": 2, "cy_lo": 2,
            "ple_sig": 4, "ge_ready": 4, "acc_summed": 2, "conv_begun": 4,
            "first_gain_landed": 0, "x_landed0": 0, "x_landed1": 0, "zero_ready": 0, "ident_ready": 0,
            "const_ready": 0, "inv_ready": 0, "stored": 0,
            "sp_waited": 0, "pool_waited": 0, "dve_waited": 0, "pe_waited": 0,
        }.items():
            sem(name, per)
        S = sems
        DVE_STEPS = 12
        per_layer["dve_step"] = DVE_STEPS

        NORM_IN = (0, 2, 4, 6)
        NORM_OUT = (1, 3, 5, 7)

        def sums(name, l, q, k):
            return at(name, l, 4 * q + k) + TT

        def half_sums(l, q, k, b):
            return at("ssq_ready", l, 8 * q + 2 * k - 1 + b) + 2 * TT

        def half_lo(l, s, i):
            return at("half_lo_ready", l, (1, 2, 4)[s] + i)

        def landing(n):
            return n % RING, n // RING + 1

        def after(eng, name):
            eng.sem_inc(S[name], 1)

        block = ctx.enter_context(nc.Block())

        @block.sync
        def _(sp):
            def load(src, l, n, first=False, wait=None):
                s = n % RING
                if not first:
                    sp.wait_ge(S["w_lo_ready"], at("w_lo_ready", l, n - 2) if wait is None else wait)
                    after(sp, "sp_waited")
                k = src.shape[1]
                dst = raw[:, s, 0:k * src.shape[2]].rearrange("p (k n) -> p k n", k=k)
                sp.dma_start(dst, src).then_inc(S[landed[s]], 16)

            def cols(name, l, c, n):
                w = A[name]
                return w[bass.ds(l, 1), :, bass.ds(c, n)].rearrange("o (k p) n -> p (o k) n", p=P)

            def rws(name, l, r, n):
                w = A[name]
                return w[bass.ds(l, 1), bass.ds(r, n), :].rearrange("o (k p) n -> p (o k) n", p=P)

            def ffn(l, f, base):
                g, u_, d = f"{f}_w_gate", f"{f}_w_up", f"{f}_w_down"
                if f == "ffn2":
                    load(cols(g, l, 0, FC), l, base)
                    load(cols(u_, l, 0, FC), l, base + 1)
                    load(cols(g, l, FC, FC), l, base + 2)
                load(cols(u_, l, FC, FC), l, base + 3)
                load(rws(d, l, 0, FC), l, base + 4)
                with sp.Fori(0, (NCH - 5) // 2) as i:
                    for k in range(2):
                        n = base + 5 + 3 * k
                        lo = at("w_lo_ready", l, n - 2) + i * 6
                        load(cols(g, l, i * (2 * FC) + (2 + k) * FC, FC), l, n, wait=lo)
                        load(cols(u_, l, i * (2 * FC) + (2 + k) * FC, FC), l, n + 1, wait=lo + 1)
                        load(rws(d, l, i * (2 * FC) + (1 + k) * FC, FC), l, n + 2, wait=lo + 2)
                n = base + 3 * NCH - 10
                for c in range(NCH - 3, NCH):
                    load(cols(g, l, c * FC, FC), l, n)
                    load(cols(u_, l, c * FC, FC), l, n + 1)
                    n += 2
                    if c == NCH - 3:
                        load(rws(d, l, (c - 1) * FC, FC), l, n)
                        n += 1
                for k in range(3):
                    load(rws(d, l, (NCH - 3 + k) * FC, FC), l, n + k)

            def first_units(l, first):
                if not first:
                    load(cols("ffn1_w_gate", l, 0, FC), l, 0)
                load(cols("ffn1_w_up", l, 0, FC), l, 1, first)
                load(cols("ffn1_w_gate", l, FC, FC), l, 2, first)

            x_in = A["x"][0].rearrange("(t p) n -> t p n", p=P)
            sp.dma_start(h[:, 0, :], x_in[0]).then_inc(S["x_landed0"], 16)
            sp.dma_start(pre_gain[:, :], A["ffn1_pre_g"][0:1, :].broadcast_to([P, D])
                         ).then_inc(S["first_gain_landed"], 16)
            load(cols("ffn1_w_gate", 0, 0, FC), 0, 0, True)
            sp.dma_start(h[:, 1, :], x_in[1]).then_inc(S["x_landed1"], 16)
            first_units(0, True)
            with sp.Fori(0, DEPTH) as l:
                ffn(l, "ffn1", U_FFN1)
                OFF_U, OFF_V, OFF_A, OFF_B, OFF_G = WB, 2 * WB, 3 * WB, 4 * WB, 5 * WB
                blocks = [OFF_V, OFF_V + FC, OFF_A, OFF_B, OFF_A + FC, OFF_B + FC, 0, FC, OFF_U, OFF_U + FC]
                for k, c in enumerate(blocks):
                    load(cols("w_in", l, c, FC), l, U_V + k)

                def gates_in(b):
                    for k, n in enumerate(U_GATE[b]):
                        if n == U_PW + 1:
                            load(A["pool_w"][bass.ds(l, 1)].rearrange("o g i n -> i (o g) n"), l, U_PW)
                        load(cols("w_in", l, OFF_G + b * D + k * FC, FC), l, n)

                def branch_out(b, name):
                    for k, n in enumerate(U_OUT[b]):
                        load(cols(name, l, k * BANK, BANK), l, n)

                gates_in(0)
                branch_out(0, "w_pool_out")
                gates_in(1)
                gates_in(2)
                branch_out(1, "w_sgu_out")
                branch_out(2, "w_conv_out")
                for k in range(4):
                    load(rws("w_out", l, k * FC, FC), l, U_WOUT + k)
                ffn(l, "ffn2", U_FFN2)
                load(rws("ple_w_proj", l, 0, PLE), l, U_EMB)
                for k in range(2):
                    load(rws("ple_w_gate", l, k * P, P), l, U_PLEG + k)
                for k in range(1, 4):
                    load(rws("ple_w_gate", l, k * FC, FC), l, U_PLEG + 1 + k)
                with sp.If(DEPTH - 1 - l):
                    following = nc.s_assert_within(
                        l + 1, 1, DEPTH - 1, skip_runtime_bounds_check_because="this If runs below the last layer only")
                    first_units(following, False)
            o = out[0].rearrange("(t p) n -> t p n", p=P)
            for t in range(TT):
                for b in range(2):
                    sp.wait_ge(S["h_ready"], 16 * DEPTH - 4 + 2 * t + b + 1)
                    sp.dma_start(o[t][:, half(b)], h[:, t, half(b)]).then_inc(S["stored"], 16)
            sp.wait_ge(S["stored"], 2 * TT * 16)

        @block.gpsimd
        def _(pool):
            g = nc.gpsimd
            g.memset(ident[:, :], 1.0).then_inc(S["zero_ready"], 1)
            g.memset(minus_half[:, :], -0.5).then_inc(S["const_ready"], 1)
            pool.wait_ge(S["zero_ready"], 1)
            g.affine_select(out=ident[:, :], in_=ident[:, :], compare_op=ALU.is_equal, fill=0.0, base=0,
                            pattern=[[-1, P]], channel_multiplier=1).then_inc(S["ident_ready"], 1)
            g.memset(ones[:, :], 1.0).then_inc(S["const_ready"], 1)
            g.memset(mean_w[:, :], 1.0 / WB).then_inc(S["const_ready"], 1)
            for j in range(16):
                last = g.memset(inv[:, GR - 1, j:j + 1], 1.0 / (j + 1))
            last.then_inc(S["inv_ready"], 1)
            pool.wait_ge(S["const_ready"], 1)

            def rstd(e, t, ssq, val):
                pool.wait_ge(S["ssq_ready"], ssq)
                after(pool, "pool_waited")
                g.tensor_scalar(ms[:, e, t:t + 1], ss[:, e, t, 0:1], ss[:, e, t, 1:2], EPS, ALU.add, ALU.add
                                ).then_inc(S["ms_ready"], 1)
                pool.wait_ge(S["ms_ready"], val)
                g.tensor_tensor(rs[:, e, t:t + 1], ms[:, e, t:t + 1], minus_half[:, :], ALU.pow
                                ).then_inc(S["rstd_ready"], 1)

            def boundary(l, q):
                for t in range(TT):
                    rstd(NORM_OUT[q], t, half_sums(l, q, 2 * t + 1, 1), sums("ms_ready", l, q, 2 * t + 1))
                    rstd(NORM_IN[(q + 1) % 4], t, half_sums(l, q, 2 * t + 2, 1), sums("ms_ready", l, q, 2 * t + 2))

            def row(name, l):
                v = A[name]
                return v[bass.ds(l, 1), :].broadcast_to([P, v.shape[1]])

            def load_gain(dst, name, l, landed_):
                pool.dma_start(dst, row(name, l)).then_inc(S[landed_], 16)

            def load_pre_gain(name, l, l_before, s_before):
                pool.wait_ge(S["xn_ready"], at("xn_ready", l_before, 4 * s_before + 2 * TT))
                after(pool, "pool_waited")
                load_gain(pre_gain[:, :], name, l, "pre_gain_landed")

            def small_loads(l):
                pool.dma_start(ws, A["sgu_w_s"][bass.ds(l, 1)].rearrange("o h t s -> t (o h) s")
                               ).then_inc(S["ws_landed"], 16)
                pool.dma_start(p_in, A["p"][bass.ds(l, 1), 0].rearrange("o (t q) n -> q (o t) n", q=P)
                               ).then_inc(S["p_landed"], 16)
                for k, name in enumerate(VECS):
                    pool.dma_start(vec_rows[k * CB:(k + 1) * CB, :], A[name][bass.ds(l, 1), :]
                                   .rearrange("o (k p) -> (o k) p", p=P)).then_inc(S["vec_landed"], 16)
                pool.dma_start(tap_rows[0:TAPS * CB, :], A["conv_dw_k"][bass.ds(l, 1)]
                               .rearrange("a t o (c p) -> (a t o c) p", p=P)).then_inc(S["vec_landed"], 16)
                pool.dma_start(vln_g[:, :], row("sgu_ln_g", l)).then_inc(S["rowvecs_landed"], 16)
                pool.dma_start(vln_b[:, :], row("sgu_ln_b", l)).then_inc(S["rowvecs_landed"], 16)
                pool.dma_start(bs[:, :, :], A["sgu_b_s"][bass.ds(l, 1)].rearrange("o h t -> o (h t)")
                               .broadcast_to([P, 4 * P]).rearrange("p (h t) -> p h t", h=4)
                               ).then_inc(S["rowvecs_landed"], 16)

            def mask(l):
                pool.wait_ge(S["ws_landed"], at("ws_landed", l, 1, 16))
                after(pool, "pool_waited")
                g.affine_select(out=ws, in_=ws, compare_op=ALU.is_ge, fill=0.0, base=0,
                                pattern=[[0, 4], [-1, P]], channel_multiplier=1).then_inc(S["ws_masked"], 1)

            for t in range(TT):
                rstd(NORM_IN[0], t, 2 * t + 2, t + 1)
            load_pre_gain("mix_pre_g", 0, 0, 0)
            small_loads(0)
            load_gain(gain[:, 0, :], "ffn1_post_g", 0, "gain_landed0")
            load_gain(gain[:, 1, :], "mix_post_g", 0, "gain_landed1")
            mask(0)
            with pool.Fori(0, DEPTH) as l:
                boundary(l, 0)
                load_pre_gain("ffn2_pre_g", l, l, 1)
                load_gain(gain[:, 0, :], "ffn2_post_g", l, "gain_landed0")
                for t in range(TT):
                    pool.wait_ge(S["v_stats"], at("v_stats", l, t + 1))
                    after(pool, "pool_waited")
                    g.tensor_scalar(vms[:, t:t + 1], vmv[:, t, 1:2], 1.0, EPS, ALU.mult, ALU.add
                                    ).then_inc(S["v_ms"], 1)
                    pool.wait_ge(S["v_ms"], at("v_ms", l, t + 1))
                    g.tensor_tensor(vrs[:, t:t + 1], vms[:, t:t + 1], minus_half[:, :], ALU.pow
                                    ).then_inc(S["v_rstd"], 1)
                pool.wait_ge(S["cvar_ready"], at("cvar_ready", l, 1))
                g.tensor_tensor(crs[:, :], cvar[:, :], minus_half[:, :].broadcast_to([P, TT]), ALU.pow
                                ).then_inc(S["crstd_ready"], 1)
                boundary(l, 1)
                load_pre_gain("ple_pre_g", l, l, 2)
                load_gain(gain[:, 1, :], "ple_post_g", l, "gain_landed1")
                boundary(l, 2)
                with pool.If(DEPTH - 1 - l):
                    following = nc.s_assert_within(
                        l + 1, 1, DEPTH - 1, skip_runtime_bounds_check_because="this If runs below the last layer only")
                    load_pre_gain("ffn1_pre_g", following, l, 3)
                    load_gain(gain[:, 0, :], "ffn1_post_g", following, "gain_landed0")
                    small_loads(following)
                    mask(l + 1)
                    boundary(l, 3)
                    load_pre_gain("mix_pre_g", following, l + 1, 0)
                    load_gain(gain[:, 1, :], "mix_post_g", following, "gain_landed1")
                with pool.Else():
                    for t in range(TT):
                        rstd(NORM_OUT[3], t, half_sums(l, 3, t + 1, 1), sums("ms_ready", l, 3, t + 1))

        @block.scalar
        def _(act):
            sc = nc.scalar

            def split(l, n, ud=None, ld=None):
                s, k = landing(n)
                act.wait_ge(S[landed[s]], at(landed[s], l, k, 16) if ld is None else ld)
                if ud is not False:
                    act.wait_ge(S["unit_done"], at("unit_done", l, n - 2) if ud is None else ud)
                w = width(n)
                sc.activation(w_hi[:, s, 0:w], raw[:, s, 0:w], ACT.Copy).then_inc(S["w_hi_ready"], 1)

            def square(e, t, b, source):
                sc.activation(junk[:, t, half(b)], source, ACT.Square, scale=1.0 / ROOT,
                              accum_out=ss[:, e, t, b:b + 1]).then_inc(S["ssq_ready"], 1)

            def square_in(l, s, t):
                for b in range(2):
                    act.wait_ge(S["h_ready"], at("h_ready", l, 4 * (s - 1) + 2 * t + b + 1))
                    square(NORM_IN[s], t, b, h[:, t, half(b)])

            def square_out(q, t, name, val):
                act.wait_ge(S[name], val)
                for b in range(2):
                    square(NORM_OUT[q], t, b, ps[:, 2 * t + b, :])

            def rows_hi(l, s, t):
                for b in range(2):
                    act.wait_ge(S["xt_done"], at("xt_done", l, 4 * s + 2 * t + b + 1))
                    sc.activation(nt_hi[:, 4 * b:4 * b + 4, t * P:(t + 1) * P], quads(s, t, b), ACT.Copy
                                  ).then_inc(S["nt_hi_ready"], 1)

            def boundary(l, q, a):
                square_out(q, 0, "tile0_done", at("tile0_done", l, q + 1))
                square_in(l, q + 1, 0)
                split(l, a + 3)
                rows_hi(l, q + 1, 0)
                split(l, a + 4)
                square_out(q, 1, "unit_done", at("unit_done", l, a + 3))
                if q > 0:
                    split(l, a + 5)
                square_in(l, q + 1, 1)
                rows_hi(l, q + 1, 1)
                if q == 0:
                    split(l, a + 5)

            def sigmoid_gate(par, n_done):
                act.wait_ge(S["unit_done"], n_done)
                sc.activation(sg[:, par, :, :], pair(gate_bank(par)), ACT.Sigmoid).then_inc(S["sg_ready"], 1)

            def chunk_hi(c, prod_val, free_val):
                act.wait_ge(S["prod_ready"], prod_val)
                if free_val is not None:
                    act.wait_ge(S["unit_done"], free_val)
                sc.activation(chunk_parts(c)[0], prod[:, c % 2, :, :], ACT.Copy).then_inc(S["act_hi_ready"], 1)

            def ffn(l, f, base):
                c0 = NCH * f

                def chunk(c, n, off=0, loff=0, freed=None, coff=0):
                    par = c % 2
                    sigmoid_gate(par, at("unit_done", l, n + 1) + off)
                    s, k = landing(n + 3)
                    split(l, n + 3, ud=False, ld=at(landed[s], l, k, 16) + loff)
                    s, k = landing(n + 4)
                    split(l, n + 4, ud=at("unit_done", l, n + 2) + off, ld=at(landed[s], l, k, 16) + loff)
                    chunk_hi(c, at("prod_ready", l, c0 + c + 1) + coff, freed)

                def down(n, off=0, loff=0):
                    s, k = landing(n + 3)
                    split(l, n + 3, ud=at("unit_done", l, n + 1) + off, ld=at(landed[s], l, k, 16) + loff)

                for c in range(2):
                    n = base + 2 * c
                    sigmoid_gate(c, at("unit_done", l, n + 1))
                    split(l, n + 3)
                    if f == 0 and c == 0:
                        for k, (dst, b) in enumerate(((wst_hi[:, :, :], 1), (pt_hi[:, :, :], 2))):
                            act.wait_ge(S["prep_done"], at("prep_done", l, k + 1))
                            src = ps[:, b, :].rearrange("p (c n) -> p c n", c=dst.shape[1])
                            sc.activation(dst, src, ACT.Copy).then_inc(S["prep_hi"], 1)
                    split(l, n + 4)
                    act.wait_ge(S["act_turned"], at("act_turned", l, 2 * f + c + 1))
                    sc.activation(act_hi[:, c, :, :], pair(gate_bank(c)), ACT.Copy).then_inc(S["act_hi_ready"], 1)
                down(base + 4)
                with act.Fori(0, (NCH - 5) // 2) as i:
                    for k in range(2):
                        n = base + 5 + 3 * k
                        chunk(2 + k, n, off=i * 6, loff=i * (2 * 16), coff=i * 2,
                              freed=at("unit_done", l, n) + i * 6)
                        down(n + 2, off=i * 6, loff=i * (2 * 16))
                n = base + 3 * NCH - 10
                chunk(NCH - 3, n, freed=at("unit_done", l, n))
                down(n + 2)
                chunk(NCH - 2, n + 3, freed=at("unit_done", l, n + 3))
                chunk(NCH - 1, n + 5)
                boundary(l, 2 * f, n + 7)

            def square_x(t):
                act.wait_ge(S[f"x_landed{t}"], 16)
                for b in range(2):
                    square(NORM_IN[0], t, b, h[:, t, half(b)])

            square_x(0)
            rows_hi(0, 0, 0)
            split(0, 0, ud=False)
            square_x(1)
            for n in (1, 2):
                split(0, n, ud=False)
            rows_hi(0, 0, 1)
            with act.Fori(0, DEPTH) as l:
                ffn(l, 0, U_FFN1)
                split(l, U_V + 3)
                act.wait_ge(S["unit_done"], at("unit_done", l, U_V + 2))
                for t in range(TT):
                    sc.activation(vf[:, t, :], ps[:, 4 + t, :], ACT.Gelu).then_inc(S["v_gelu"], 1)
                split(l, U_V + 4)
                for i in range(2):
                    split(l, U_GLU + 2 * i + 3)
                    act.wait_ge(S["unit_done"], at("unit_done", l, U_GLU + 2 * i + 2))
                    sc.activation(ctmp[:, 2 * i:2 * i + 2, :], pair(2 * i + 1), ACT.Sigmoid
                                  ).then_inc(S["glu_sig"], 1)
                    split(l, U_GLU + 2 * i + 4)
                    act.wait_ge(S["xg_ready"], at("xg_ready", l, i + 1))
                    for c in range(2 * i, 2 * i + 2):
                        sc.activation(acc[:, c, :], xg[:, c, 0:SEQ], ACT.Identity, bias=vec4[:, 1, c:c + 1],
                                      scale=tap[:, 0, c:c + 1]).then_inc(S["conv_begun"], 1)
                for i in range(2):
                    act.wait_ge(S["unit_done"], at("unit_done", l, U_POOL + i + 1))
                    sc.activation(pooled[:, 2 * i:2 * i + 2, :], pair(6 + i), ACT.Copy).then_inc(S["px_ready"], 1)
                    split(l, U_POOL + i + 3)
                for i in range(2):
                    act.wait_ge(S["unit_done"], at("unit_done", l, U_U + i + 1))
                    sc.activation(u[:, 2 * i:2 * i + 2, :], pair(i), ACT.Gelu).then_inc(S["u_gelu"], 1)
                    split(l, U_U + i + 3)
                    if i == 0:
                        act.wait_ge(S["pooled_ready"], at("pooled_ready", l, 1))
                        sc.activation(pl_hi, pooled, ACT.Copy).then_inc(S["pooled_hi"], 1)
                    else:
                        act.wait_ge(S["v_ready"], at("v_ready", l, 1))
                        sc.activation(v_hi, vf, ACT.Copy).then_inc(S["v_hi_ready"], 1)
                for b in range(3):
                    for k, n in enumerate(U_GATE[b]):
                        act.wait_ge(S["unit_done"], at("unit_done", l, n + 1))
                        if b == 1 and k == 0:
                            act.wait_ge(S["pooled_ready"], at("pooled_ready", l, 1))
                        if b == 2 and k == 0:
                            act.wait_ge(S["us_lo"], at("us_lo", l, 1))
                        if b == 2 and k == 3:
                            act.wait_ge(S["centred"], at("centred", l, 1))
                            sc.activation(ctmp[:, :, :], acc[:, :, :], ACT.Square).then_inc(S["csq_ready"], 1)
                        sc.activation(gate_of(b, k // 2)[:, 2 * (k % 2):2 * (k % 2) + 2, :],
                                      pair(6 + k % 2), ACT.Sigmoid).then_inc(S["gate_sig"], 1)
                        split(l, n + 3)
                        if n == U_PW - 1:
                            act.wait_ge(S["unit_done"], at("unit_done", l, U_PW + 1))
                            for i in range(GR):
                                sc.activation(y_hi[:, 0, i, :], pair(2 + i // 2)[:, i % 2, :], ACT.Copy,
                                              scale=vec4[:, 0, i:i + 1]).then_inc(S["yp_hi"], 1)
                            split(l, U_PW + 3)
                        if b == 1 and k == 1:
                            act.wait_ge(S["us_ready"], at("us_ready", l, 1))
                            sc.activation(y_hi[:, 1, :, :], us, ACT.Copy).then_inc(S["us_hi"], 1)
                    if b == 0:
                        for n in U_OUT[0]:
                            split(l, n + 3)
                for i in range(2):
                    act.wait_ge(S["z_ready"], at("z_ready", l, i + 1))
                    for c in range(2 * i, 2 * i + 2):
                        last = sc.activation(ctmp[:, c, :], acc[:, c, :], ACT.Sigmoid,
                                             bias=vec4[:, 3, c:c + 1], scale=vec4[:, 2, c:c + 1])
                    last.then_inc(S["zsig_ready"], 1)
                for i in range(2):
                    act.wait_ge(S["conv_y"], at("conv_y", l, i + 1))
                    m = slice(2 * i, 2 * i + 2)
                    sc.activation(y_hi[:, 2, m, :], u[:, m, :], ACT.Copy).then_inc(S["cy_hi"], 1)
                for n in U_OUT[1]:
                    split(l, n + 3)
                split(l, U_OUT[2][0] + 3)
                for k in range(2):
                    act.wait_ge(S["merged_ready"], at("merged_ready", l, MERGED[2][k]))
                    sc.activation(nt_hi[:, 4 * k:4 * k + 4, :], merged[:, 4 * k:4 * k + 4, :], ACT.Copy
                                  ).then_inc(S["mg_hi"], 1)
                    split(l, (U_OUT[2][1], U_WOUT)[k] + 3)
                boundary(l, 1, U_WOUT + 1)
                ffn(l, 1, U_FFN2)
                split(l, U_EMB + 3)
                for k in range(2):
                    split(l, U_PLEG + k + 3)

                def gate_sigmoid(t):
                    if t == 0:
                        act.wait_ge(S["tile0_done"], at("tile0_done", l, 4))
                    else:
                        act.wait_ge(S["unit_done"], at("unit_done", l, UNITS))
                    for b in range(2):
                        sc.activation(ge[:, t, half(b)], ps[:, 2 * t + b, :], ACT.Sigmoid).then_inc(S["ple_sig"], 1)

                def square_ge(t):
                    for b in range(2):
                        act.wait_ge(S["ge_ready"], at("ge_ready", l, 2 * t + b + 1))
                        square(NORM_OUT[3], t, b, ge[:, t, half(b)])

                gate_sigmoid(0)
                with act.If(DEPTH - 1 - l):
                    square_ge(0)
                    split(l, UNITS)
                    square_in(l + 1, 0, 0)
                    gate_sigmoid(1)
                    rows_hi(l + 1, 0, 0)
                    split(l, UNITS + 1)
                    square_ge(1)
                    split(l, UNITS + 2)
                    square_in(l + 1, 0, 1)
                    rows_hi(l + 1, 0, 1)
                with act.Else():
                    square_ge(0)
                    gate_sigmoid(1)
                    square_ge(1)

        @block.vector
        def _(dve):
            v = nc.vector

            def split(l, n, hi=None):
                s, w = n % RING, width(n)
                dve.wait_ge(S["w_hi_ready"], at("w_hi_ready", l, n + 1) if hi is None else hi)
                v.tensor_tensor(w_lo[:, s, 0:w], raw[:, s, 0:w], w_hi[:, s, 0:w].bitcast(F32), ALU.subtract
                                ).then_inc(S["w_lo_ready"], 1)

            def scale_rows(l, s, t, val, gain_landed=True):
                e = NORM_IN[s]
                dve.wait_ge(S["rstd_ready"], val)
                if t == 0 and gain_landed:
                    dve.wait_ge(S["pre_gain_landed"], at("pre_gain_landed", l, s, 16))
                for b in range(2):
                    v.scalar_tensor_tensor(xs[:, t, half(b)], h[:, t, half(b)], rs[:, e, t:t + 1],
                                           pre_gain[:, half(b)], ALU.mult, ALU.mult).then_inc(S["xn_ready"], 1)

            def rows_lo(l, s, t, halves=(0, 1)):
                for b in halves:
                    dve.wait_ge(S["nt_hi_ready"], at("nt_hi_ready", l, 4 * s + 2 * t + b + 1))
                    part = (slice(None), slice(4 * b, 4 * b + 4), slice(t * P, (t + 1) * P))
                    v.tensor_tensor(nt_lo[part], quads(s, t, b), nt_hi[part].bitcast(F32), ALU.subtract
                                    ).then_inc(S["nt_lo_ready"], 1)

            def half_unit_lo(l, n, b):
                if b == 0:
                    dve.wait_ge(S["w_hi_ready"], at("w_hi_ready", l, n + 1))
                part = (slice(None), n % RING, slice(b * UNIT // 2, (b + 1) * UNIT // 2))
                v.tensor_tensor(w_lo[part], raw[part], w_hi[part].bitcast(F32), ALU.subtract
                                ).then_inc(S[("half_lo_ready", "w_lo_ready")[b]], 1)

            def first_lo(l, s, n):
                for b in range(2):
                    half_unit_lo(l, n, b)
                    rows_lo(l, s, 0, (b,))

            def gain_rows(l, q, t, k, weight, source):
                slot, count = q % 2, q // 2 + 1
                if t == 0:
                    dve.wait_ge(S[f"gain_landed{slot}"], at(f"gain_landed{slot}", l, count, 16))
                for b in range(2):
                    dve.wait_ge(S["ssq_ready"], half_sums(l, q, k, b))
                    v.scalar_tensor_tensor(xs[:, t, half(b)], source[:, half(b)], weight, gain[:, slot, half(b)],
                                           ALU.mult, ALU.mult).then_inc(S["row_gained"], 1)

            def add_rows(l, q, t, val):
                e = NORM_OUT[q]
                dve.wait_ge(S["rstd_ready"], val)
                dve.wait_ge(S["row_gained"], at("row_gained", l, 4 * q + 2 * t + 2))
                for b in range(2):
                    v.scalar_tensor_tensor(h[:, t, half(b)], xs[:, t, half(b)], rs[:, e, t:t + 1],
                                           h[:, t, half(b)], ALU.mult, ALU.add).then_inc(S["h_ready"], 1)

            def boundary(l, q, a, weight):
                gain_rows(l, q, 0, 1, weight, rows(0))
                add_rows(l, q, 0, sums("rstd_ready", l, q, 1))
                scale_rows(l, q + 1, 0, sums("rstd_ready", l, q, 2))
                if q < 2:
                    first_lo(l, q + 1, a + 3)
                    half_unit_lo(l, a + 4, 0)
                    gain_rows(l, q, 1, 3, weight, rows(1))
                    half_unit_lo(l, a + 4, 1)
                else:
                    split(l, a + 3)
                    rows_lo(l, 3, 0)
                    split(l, a + 4)
                    gain_rows(l, q, 1, 3, weight, rows(1))
                add_rows(l, q, 1, sums("rstd_ready", l, q, 3))
                if q == 1:
                    half_unit_lo(l, a + 5, 0)
                if q == 2:
                    split(l, a + 5)
                scale_rows(l, q + 1, 1, sums("rstd_ready", l, q, 4))
                if q == 1:
                    half_unit_lo(l, a + 5, 1)
                rows_lo(l, q + 1, 1)
                if q == 0:
                    split(l, a + 5)

            def ffn(l, f, base):
                c0 = NCH * f

                def prepare():
                    dve.wait_ge(S["vecs_turned"], at("vecs_turned", l, 1))
                    v.tensor_copy(vec4[:, :, :], ps[:, 0, 0:NV * CB].rearrange("p (a c) -> p a c", a=NV)
                                  ).then_inc(S["vecs_ready"], 1)
                    v.tensor_copy(tap[:, :, :], ps[:, 0, P:P + TAPS * CB].rearrange("p (a c) -> p a c", c=CB)
                                  ).then_inc(S["vecs_ready"], 1)
                    for k, (hi, lo, b) in enumerate(((wst_hi, wst_lo, 1), (pt_hi, pt_lo, 2))):
                        dve.wait_ge(S["prep_hi"], at("prep_hi", l, k + 1))
                        src = ps[:, b, :].rearrange("p (c n) -> p c n", c=hi.shape[1])
                        v.tensor_tensor(lo[:, :, :], src, hi[:, :, :].bitcast(F32), ALU.subtract
                                        ).then_inc(S["prep_lo"], 1)

                def chunk(c, n, off=0, coff=0):
                    par = c % 2
                    dve.wait_ge(S["sg_ready"], at("sg_ready", l, c0 + c + 1) + coff)
                    v.tensor_tensor(sg[:, par, :, :], sg[:, par, :, :], pair(gate_bank(par)), ALU.mult
                                    ).then_inc(S["gate_read"], 1)
                    split(l, n + 3, hi=at("w_hi_ready", l, n + 4) + off)
                    dve.wait_ge(S["unit_done"], at("unit_done", l, n + 2) + off)
                    dve.wait_ge(S["gate_read"], at("gate_read", l, c0 + c + 1) + coff)
                    v.tensor_tensor(prod[:, par, :, :], sg[:, par, :, :], pair(up_bank(par)), ALU.mult
                                    ).then_inc(S["prod_ready"], 1)
                    if c == 0 and f == 0:
                        prepare()
                    split(l, n + 4, hi=at("w_hi_ready", l, n + 5) + off)
                    dve.wait_ge(S["act_hi_ready"], at("act_hi_ready", l, c0 + c + 1) + coff)
                    whole = pair(gate_bank(par)) if c < 2 else prod[:, par, :, :]
                    hi, lo = chunk_parts(c)
                    v.tensor_tensor(lo, whole, hi.bitcast(F32), ALU.subtract).then_inc(S["act_lo_ready"], 1)

                chunk(0, base)
                chunk(1, base + 2)
                split(l, base + 7)
                with dve.Fori(0, (NCH - 5) // 2) as i:
                    for k in range(2):
                        n = base + 5 + 3 * k
                        chunk(2 + k, n, off=i * 6, coff=i * 2)
                        split(l, n + 5, hi=at("w_hi_ready", l, n + 6) + i * 6)
                n = base + 3 * NCH - 10
                chunk(NCH - 3, n)
                split(l, n + 5)
                chunk(NCH - 2, n + 3)
                chunk(NCH - 1, n + 5)
                boundary(l, 2 * f, n + 7, 0.5)

            v.memset(xg[:, :, 0:PAD], 0.0)
            dve.wait_ge(S["inv_ready"], 1)
            for gi in range(GR - 1):
                last = v.tensor_scalar(inv[:, gi, :], inv[:, GR - 1, :], 1.0 / POOL_WINDOWS[gi], None, ALU.max)
            last.then_inc(S["const_ready"], 1)
            dve.wait_ge(S["first_gain_landed"], 16)
            scale_rows(0, 0, 0, 1, gain_landed=False)
            first_lo(0, 0, 0)
            scale_rows(0, 0, 1, 2, gain_landed=False)
            for n in (1, 2):
                split(0, n)
            rows_lo(0, 0, 1)

            with dve.Fori(0, DEPTH) as l:
                ffn(l, 0, U_FFN1)

                jobs = [(j, c + i) for c in range(0, CB, 2) for j in range(1, TAPS) for i in range(2)]
                total = len(jobs)

                def convolve(count):
                    if not jobs:
                        return
                    for _ in range(min(count, len(jobs))):
                        j, c = jobs.pop(0)
                        src = xg[:, c, j:j + SEQ]
                        if j == 1:
                            dve.wait_ge(S["conv_begun"], at("conv_begun", l, c + 1))
                        else:
                            dve.wait_ge(S["tap_added"], at("tap_added", l, total - len(jobs) - 2))
                        ins = v.scalar_tensor_tensor(acc[:, c, :], src, tap[:, j, c:c + 1], acc[:, c, :],
                                                     ALU.mult, ALU.add)
                        ins.then_inc(S["tap_added"], 1)

                steps = [0]

                def step(ins):
                    steps[0] += 1
                    ins.then_inc(S["dve_step"], 1)

                def steps_done():
                    dve.wait_ge(S["dve_step"], at("dve_step", l, steps[0]))

                split(l, U_V + 3)
                for t in range(TT):
                    dve.wait_ge(S["v_gelu"], at("v_gelu", l, t + 1))
                    step(v.bn_stats(vst[:, t, :], vf[:, t, :]))
                steps_done()
                after(dve, "dve_waited")
                for t in range(TT):
                    v.bn_aggr(vmv[:, t, :], vst[:, t, :]).then_inc(S["v_stats"], 1)
                split(l, U_V + 4)
                dve.wait_ge(S["rowvecs_landed"], at("rowvecs_landed", l, 3, 16))
                dve.wait_ge(S["v_stats"], at("v_stats", l, 2))
                for t in range(TT):
                    step(v.scalar_tensor_tensor(vf[:, t, :], vf[:, t, :], vmv[:, t, 0:1], vln_g[:, :],
                                                ALU.subtract, ALU.mult))
                split(l, U_GLU + 3)
                steps_done()
                dve.wait_ge(S["v_rstd"], at("v_rstd", l, 2))
                for t in range(TT):
                    last = v.scalar_tensor_tensor(vf[:, t, :], vf[:, t, :], vrs[:, t:t + 1], vln_b[:, :],
                                                  ALU.mult, ALU.add)
                last.then_inc(S["v_ready"], 1)
                dve.wait_ge(S["vecs_ready"], at("vecs_ready", l, 2))
                for i in range(2):
                    dve.wait_ge(S["glu_sig"], at("glu_sig", l, i + 1))
                    v.tensor_tensor(xg[:, 2 * i:2 * i + 2, PAD:], ctmp[:, 2 * i:2 * i + 2, :], pair(2 * i), ALU.mult
                                    ).then_inc(S["xg_ready"], 1)
                    if i == 0:
                        split(l, U_GLU + 4)
                        convolve(8)
                        split(l, U_GLU + 5)
                        convolve(4)
                    else:
                        split(l, U_GLU + 6)
                        convolve(10)
                split(l, U_POOL + 3)

                dve.wait_ge(S["px_ready"], at("px_ready", l, 2))
                source = pooled
                for gi, w in enumerate(POOL_WINDOWS):
                    d = w // 2
                    target = (sum_a, sum_b)[gi % 2]
                    v.tensor_copy(target[:, gi:, 0:d], source[:, gi:, 0:d])
                    step(v.tensor_tensor(target[:, gi:, d:], source[:, gi:, d:], source[:, gi:, 0:SEQ - d], ALU.add))
                    steps_done()
                    source = target
                W0 = POOL_WINDOWS[-1]
                for k, part_sums in enumerate((sum_a, sum_b)):
                    ins = v.tensor_tensor(part_sums[:, k::2, 0:W0], part_sums[:, k::2, 0:W0], inv[:, k::2, :], ALU.mult)
                step(ins)
                for gi, w in enumerate(POOL_WINDOWS):
                    part_sums = (sum_a, sum_b)[gi % 2]
                    v.scalar_tensor_tensor(pooled[:, gi, W0:], part_sums[:, gi, W0:], 1.0 / w, pooled[:, gi, W0:],
                                           ALU.mult, ALU.subtract)
                steps_done()
                for k, part_sums in enumerate((sum_a, sum_b)):
                    ins = v.tensor_tensor(pooled[:, k::2, 0:W0], part_sums[:, k::2, 0:W0], pooled[:, k::2, 0:W0],
                                          ALU.subtract)
                ins.then_inc(S["pooled_ready"], 1)
                split(l, U_POOL + 4)
                convolve(8)
                split(l, U_U + 3)
                dve.wait_ge(S["pooled_hi"], at("pooled_hi", l, 1))
                v.tensor_tensor(pl_lo, pooled, pl_hi.bitcast(F32), ALU.subtract).then_inc(S["pooled_lo"], 1)
                convolve(6)
                split(l, U_U + 4)
                convolve(5)
                dve.wait_ge(S["v_hi_ready"], at("v_hi_ready", l, 1))
                v.tensor_tensor(v_lo, vf, v_hi.bitcast(F32), ALU.subtract).then_inc(S["v_lo_ready"], 1)
                xa = u[:, :, :]

                def weigh(b, k):
                    bank = out_bank(b, k)
                    made = ps[:, bank:bank + 2, :].rearrange("p b (c n) -> p (b c) n", c=2)
                    dve.wait_ge(S["unit_done"], at("unit_done", l, U_OUT[b][k] + 1))
                    dve.wait_ge(S["gate_sig"], at("gate_sig", l, 4 * b + 2 * k + 2))
                    v.tensor_tensor(merged[:, 4 * k:4 * k + 4, :] if b == 0 else gate_of(b, k), gate_of(b, k), made,
                                    ALU.mult).then_inc(S["out_read"], 1)

                def add_branch(b, k):
                    m = slice(4 * k, 4 * k + 4)
                    dve.wait_ge(S["out_read"], at("out_read", l, OUT_READ[b][k]))
                    v.tensor_tensor(merged[:, m, :], merged[:, m, :], gate_of(b, k), ALU.add
                                    ).then_inc(S["merged_ready"], 1)

                for k, n in enumerate(U_GATE[0]):
                    split(l, n + 3)
                    convolve((4, 4, 0, 8)[k])
                    if n == U_PW - 1:
                        for i in range(GR):
                            if i % 2 == 0:
                                dve.wait_ge(S["yp_hi"], at("yp_hi", l, i + 2))
                            v.scalar_tensor_tensor(y_lo[:, 0, i, :], pair(2 + i // 2)[:, i % 2, :],
                                                   vec4[:, 0, i:i + 1], y_hi[:, 0, i, :].bitcast(F32),
                                                   ALU.mult, ALU.subtract).then_inc(S["yp_lo"], 1)
                        split(l, U_PW + 3)
                        convolve(5)
                for n in U_OUT[0]:
                    split(l, n + 3)
                    convolve(8)

                def sum_tiles(i):
                    dve.wait_ge(S["tap_added"], at("tap_added", l, (i + 1) * total // 2))
                    v.tensor_tensor(half_sum[i], acc[:, 2 * i, :], acc[:, 2 * i + 1, :], ALU.add
                                    ).then_inc(S["acc_summed"], 1)

                assert len(jobs) < total // 2
                sum_tiles(0)
                for k, n in enumerate(U_GATE[1] + U_GATE[2]):
                    if k == 6:
                        dve.wait_ge(S["stat_done"], at("stat_done", l, 1))
                        mean = ps[:, 4, 0:SEQ].unsqueeze(1).broadcast_to([P, CB, SEQ])
                        v.tensor_tensor(acc[:, :, :], acc[:, :, :], mean, ALU.subtract
                                        ).then_inc(S["centred"], 1)
                        weigh(0, 0)
                    if k == 7:
                        weigh(0, 1)
                        break
                    split(l, n + 3)
                    if k == 1:
                        dve.wait_ge(S["s_done"], at("s_done", l, 1))
                        for c in range(TT):
                            part = (slice(None), slice(None), slice(c * P, (c + 1) * P))
                            gated = ps[:, 4:6, :].rearrange("p b (c n) -> p (b c) n", c=2)
                            step(v.tensor_tensor(s1[part], gated[part], bs[:, :, :], ALU.add))
                        steps_done()
                        dve.wait_ge(S["u_gelu"], at("u_gelu", l, 2))
                        v.tensor_tensor(us, s1, u[:, :, :], ALU.mult).then_inc(S["us_ready"], 1)
                        convolve(4)
                        dve.wait_ge(S["us_hi"], at("us_hi", l, 1))
                        v.tensor_tensor(y_lo[:, 1, :, :], us, y_hi[:, 1, :, :].bitcast(F32), ALU.subtract
                                        ).then_inc(S["us_lo"], 1)
                    else:
                        convolve(8)
                    if k == 5:
                        assert not jobs
                        sum_tiles(1)
                dve.wait_ge(S["stat_done"], at("stat_done", l, 2))
                v.tensor_scalar(cvar[:, :], ps[:, 5, 0:TT], EPS, None, ALU.add).then_inc(S["cvar_ready"], 1)
                dve.wait_ge(S["crstd_ready"], at("crstd_ready", l, 1))
                for t in range(TT):
                    ins = v.tensor_scalar(diag[:, t, :], ident[:, :], crs[:, t:t + 1], None, ALU.mult)
                ins.then_inc(S["diag_ready"], 1)
                split(l, U_GATE[2][3] + 3)
                dve.wait_ge(S["stat_done"], at("stat_done", l, 3))
                pairs = [slice(0, 2), slice(2, 4)]
                root = ps[:, 4, SEQ:2 * SEQ].unsqueeze(1).broadcast_to([P, 2, SEQ])
                for m in pairs:
                    v.tensor_tensor(acc[:, m, :], acc[:, m, :], root, ALU.mult).then_inc(S["z_ready"], 1)
                dve.wait_ge(S["z_ready"], at("z_ready", l, 2))
                for c in range(CB):
                    ins = v.tensor_scalar(xa[:, c, :], acc[:, c, :], vec4[:, 2, c:c + 1], vec4[:, 3, c:c + 1],
                                          ALU.mult, ALU.add)
                step(ins)
                steps_done()
                for i, m in enumerate(pairs):
                    dve.wait_ge(S["zsig_ready"], at("zsig_ready", l, i + 1))
                    v.tensor_tensor(xa[:, m, :], xa[:, m, :], ctmp[:, m, :], ALU.mult).then_inc(S["conv_y"], 1)
                for i, m in enumerate(pairs):
                    dve.wait_ge(S["cy_hi"], at("cy_hi", l, i + 1))
                    v.tensor_tensor(y_lo[:, 2, m, :], xa[:, m, :], y_hi[:, 2, m, :].bitcast(F32), ALU.subtract
                                    ).then_inc(S["cy_lo"], 1)
                weigh(1, 0)
                split(l, U_OUT[1][0] + 3)
                add_branch(1, 0)
                split(l, U_OUT[1][1] + 3)

                def merged_lo(k):
                    dve.wait_ge(S["mg_hi"], at("mg_hi", l, k + 1))
                    m = slice(4 * k, 4 * k + 4)
                    v.tensor_tensor(nt_lo[:, m, :], merged[:, m, :], nt_hi[:, m, :].bitcast(F32), ALU.subtract
                                    ).then_inc(S["mg_lo"], 1)

                weigh(2, 0)
                add_branch(2, 0)
                weigh(1, 1)
                merged_lo(0)
                add_branch(1, 1)
                split(l, U_OUT[2][0] + 3)
                weigh(2, 1)
                add_branch(2, 1)
                split(l, U_OUT[2][1] + 3)
                merged_lo(1)
                assert steps[0] == DVE_STEPS, steps
                split(l, U_WOUT + 3)
                boundary(l, 1, U_WOUT + 1, 1.0)
                ffn(l, 1, U_FFN2)
                split(l, U_EMB + 3)
                for k in range(2):
                    split(l, U_PLEG + k + 3)

                def gate_rows(t):
                    for b in range(2):
                        dve.wait_ge(S["ple_sig"], at("ple_sig", l, 2 * t + b + 1))
                        v.tensor_tensor(ge[:, t, half(b)], ge[:, t, half(b)], ps[:, 4 + 2 * t + b, :], ALU.mult
                                        ).then_inc(S["ge_ready"], 1)

                gate_rows(0)
                with dve.If(DEPTH - 1 - l):
                    gain_rows(l, 3, 0, 1, 1.0, ge[:, 0, :])
                    add_rows(l, 3, 0, sums("rstd_ready", l, 3, 1))
                    for b in range(2):
                        half_unit_lo(l, UNITS, b)
                    scale_rows(l + 1, 0, 0, sums("rstd_ready", l, 3, 2))
                    gate_rows(1)
                    rows_lo(l + 1, 0, 0)
                    split(l, UNITS + 1)
                    gain_rows(l, 3, 1, 3, 1.0, ge[:, 1, :])
                    add_rows(l, 3, 1, sums("rstd_ready", l, 3, 3))
                    split(l, UNITS + 2)
                    scale_rows(l + 1, 0, 1, sums("rstd_ready", l, 3, 4))
                    rows_lo(l + 1, 0, 1)
                with dve.Else():
                    gain_rows(l, 3, 0, 1, 1.0, ge[:, 0, :])
                    add_rows(l, 3, 0, sums("rstd_ready", l, 3, 1))
                    gate_rows(1)
                    gain_rows(l, 3, 1, 2, 1.0, ge[:, 1, :])
                    add_rows(l, 3, 1, sums("rstd_ready", l, 3, 2))

        @block.tensor
        def _(pe):
            te = nc.tensor

            def product(o, a_hi, a_lo, b_hi, b_lo, start, stop):
                te.matmul(o, a_hi, b_hi, start=start, stop=False)
                te.matmul(o, a_hi, b_lo, start=False, stop=False)
                return te.matmul(o, a_lo, b_hi, start=False, stop=stop)

            def loaded(l, n, off=0):
                pe.wait_ge(S["w_lo_ready"], at("w_lo_ready", l, n + 1) + off)

            def turn(l, s, t):
                for k in range(KD):
                    if k % 4 == 0:
                        pe.wait_ge(S["xn_ready"], at("xn_ready", l, 4 * s + 2 * t + k // 4 + 1))
                    ins = te.transpose(quads(s, t, k // 4)[:, k % 4, :], xs[:, t, k * P:(k + 1) * P], ident[:, :])
                    if k % 4 == 3:
                        ins.then_inc(S["xt_done"], 1)

            def rows_split(l, s, t, b):
                pe.wait_ge(S["nt_lo_ready"], at("nt_lo_ready", l, 4 * s + 2 * t + b + 1))

            def by_channel(n, bank, x_hi, x_lo, kt, tiles, between=None):
                s = n % RING
                w = width(n) // kt
                for c in range(tiles):
                    if c == tiles // 2 and between is not None:
                        between()
                    for k in range(kt):
                        at_ = slice(k * w + c * P, k * w + (c + 1) * P)
                        ins = product(pair(bank + c // 2)[:, c % 2, :], w_hi[:, s, at_], w_lo[:, s, at_],
                                      x_hi[:, k, :], x_lo[:, k, :], k == 0, k == kt - 1)
                return ins

            def across(n, bank, col, t, first=None, second=None):
                x_at = slice(t * P, (t + 1) * P)
                for k in range(KD):
                    if k == 0 and first is not None:
                        first()
                    if k == KD // 2 and second is not None:
                        second()
                    at_ = slice(k * FC, (k + 1) * FC)
                    ins = product(ps[:, bank, col:col + FC], nt_hi[:, k, x_at], nt_lo[:, k, x_at],
                                  w_hi[:, n % RING, at_], w_lo[:, n % RING, at_], k == 0, k == KD - 1)
                return ins

            def first_units(l, s, n, count, place):
                def halves(t, b):
                    if t == 0 and b == 0:
                        pe.wait_ge(S["half_lo_ready"], half_lo(l, s, 0))
                    elif t == 0:
                        loaded(l, n)
                    rows_split(l, s, t, b)

                across(n, *place(0, 0), 0, lambda: halves(0, 0), lambda: halves(0, 1))
                if s == 0:
                    loaded(l, n + 1)
                    across(n + 1, *place(1, 0), 0)
                else:
                    across(n + 1, *place(1, 0), 0, lambda: pe.wait_ge(S["half_lo_ready"], half_lo(l, s, 1)),
                           lambda: loaded(l, n + 1))

                def in_third():
                    turn(l, s, 1)
                    loaded(l, n + 2)

                if count == 3:
                    if s == 0:
                        loaded(l, n + 2)
                    else:
                        pe.wait_ge(S["half_lo_ready"], half_lo(l, s, 2))
                    across(n + 2, *place(2, 0), 0, None, in_third)
                if count == 2:
                    turn(l, s, 1)
                done(across(n, *place(0, 1), 1, lambda: halves(1, 0), lambda: halves(1, 1)))
                for i in range(1, count):
                    done(across(n + i, *place(i, 1), 1))

            def by_token(t, n, base, x_hi, x_lo, k0, kt, start, stop, between=None):
                s = n % RING
                x_at = slice(t * P, (t + 1) * P)
                for k in range(kt):
                    if k == kt - 1 and between is not None:
                        between()
                    for b in range(2):
                        at_ = slice(k * D + b * BANK, k * D + (b + 1) * BANK)
                        ins = product(ps[:, base + 2 * t + b, :], x_hi[:, k0 + k, x_at], x_lo[:, k0 + k, x_at],
                                      w_hi[:, s, at_], w_lo[:, s, at_], start and k == 0, stop and k == kt - 1)
                return ins

            def done(ins):
                ins.then_inc(S["unit_done"], 1)

            def last_three(l, n, part, following=None):
                for t in range(TT):
                    for k in range(3):
                        if t == 0:
                            loaded(l, n + k)
                        last = t == 1 and k == 2 and following is not None
                        ins = part(k, t, (lambda: turn(l, following, 0)) if last else None)
                        if t == 1:
                            done(ins)
                    if t == 0:
                        ins.then_inc(S["tile0_done"], 1)

            def ffn(l, f, base):
                c0 = NCH * f

                def gate(c, n, off=0, coff=0):
                    loaded(l, n, off)
                    pe.wait_ge(S["gate_read"], at("gate_read", l, c0 + c - 1) + coff)
                    done(by_channel(n, gate_bank(c), nt_hi, nt_lo, KD, 2))

                def up(c, n, off=0, coff=0):
                    loaded(l, n, off)
                    pe.wait_ge(S["prod_ready"], at("prod_ready", l, c0 + c - 1) + coff)
                    done(by_channel(n, up_bank(c), nt_hi, nt_lo, KD, 2))

                def down(c, n, off=0, coff=0, start=False):
                    loaded(l, n, off)
                    pe.wait_ge(S["act_lo_ready"], at("act_lo_ready", l, c0 + c + 1) + coff)
                    for t in range(TT):
                        ins = by_token(t, n, 0, *chunk_parts(c), 0, 2, start, False)
                    done(ins)

                def last_down(k, t, between):
                    c = NCH - 3 + k
                    pe.wait_ge(S["act_lo_ready"], at("act_lo_ready", l, c0 + c + 1))
                    return by_token(t, base + 3 * NCH - 3 + k, 0, *chunk_parts(c), 0, 2, False, k == 2, between)

                if f == 0:
                    turn(l, 0, 0)
                first_units(l, 2 * f, base, 3, lambda i, t: ((gate_bank(0), up_bank(0), gate_bank(1))[i], t * FC))
                if f == 0:
                    pe.wait_ge(S["vec_landed"], at("vec_landed", l, NV + 1, 16))
                    after(pe, "pe_waited")
                    te.transpose(ps[:, 0, 0:NV * CB], vec_rows[0:NV * CB, :], ident[0:NV * CB, 0:NV * CB])
                    te.transpose(ps[:, 0, P:P + TAPS * CB], tap_rows[0:TAPS * CB, :], ident[0:TAPS * CB, 0:TAPS * CB]
                                 ).then_inc(S["vecs_turned"], 1)
                    pe.wait_ge(S["ws_masked"], at("ws_masked", l, 1))
                    for i in range(4):
                        ins = te.transpose(ps[:, 1, i * P:(i + 1) * P], ws[:, i, :], ident[:, :])
                    ins.then_inc(S["prep_done"], 1)
                    pe.wait_ge(S["p_landed"], at("p_landed", l, 1, 16))
                    for k in range(2):
                        for t in range(TT):
                            ins = te.transpose(pair(2)[:, k, t * P:(t + 1) * P], p_in[:, t, k * P:(k + 1) * P],
                                               ident[:, :])
                    ins.then_inc(S["prep_done"], 1)

                def turn_hidden(c):
                    pe.wait_ge(S["prod_ready"], at("prod_ready", l, c0 + c + 1))
                    for k in range(2):
                        for t in range(TT):
                            ins = te.transpose(pair(gate_bank(c))[:, k, t * P:(t + 1) * P],
                                               prod[:, c, t, k * P:(k + 1) * P], ident[:, :])
                    ins.then_inc(S["act_turned"], 1)

                loaded(l, base + 3)
                across(base + 3, up_bank(1), 0, 0)
                turn_hidden(0)
                done(across(base + 3, up_bank(1), FC, 1))
                if f == 0:
                    pe.wait_ge(S["vecs_ready"], at("vecs_ready", l, 2))
                    pe.wait_ge(S["prep_lo"], at("prep_lo", l, 2))
                down(0, base + 4, start=True)
                turn_hidden(1)
                with pe.Fori(0, (NCH - 5) // 2) as i:
                    for k in range(2):
                        n = base + 5 + 3 * k
                        gate(2 + k, n, i * 6, i * 2)
                        up(2 + k, n + 1, i * 6, i * 2)
                        down(1 + k, n + 2, i * 6, i * 2)
                n = base + 3 * NCH - 10
                for c in range(NCH - 3, NCH):
                    gate(c, n)
                    up(c, n + 1)
                    n += 2
                    if c == NCH - 3:
                        down(c - 1, n)
                        n += 1
                last_three(l, n, last_down, 2 * f + 1)

            pe.wait_ge(S["ident_ready"], 1)
            with pe.Fori(0, DEPTH) as l:
                ffn(l, 0, U_FFN1)
                first_units(l, 1, U_V, 2, lambda i, t: (4 + t, i * FC))
                for k in range(4):
                    n = U_GLU + k
                    loaded(l, n)
                    done(by_channel(n, k, nt_hi, nt_lo, KD, 2))
                for k in range(2):
                    n = U_POOL + k
                    loaded(l, n)
                    done(by_channel(n, 6 + k, nt_hi, nt_lo, KD, 2))
                for i in range(2):
                    n = U_U + i
                    loaded(l, n)
                    pe.wait_ge(S["xg_ready"], at("xg_ready", l, 1))
                    done(by_channel(n, i, nt_hi, nt_lo, KD, 2))

                def gates_unit(b, k):
                    n, j = U_GATE[b][k], 4 * b + k
                    loaded(l, n)
                    if j >= 2:
                        pe.wait_ge(S["gate_sig"], at("gate_sig", l, j - 1))
                    else:
                        pe.wait_ge(S["px_ready"], at("px_ready", l, j + 1))
                    done(by_channel(n, 6 + k % 2, nt_hi, nt_lo, KD, 2))

                def out_unit(b, k, between=None):
                    n = U_OUT[b][k]
                    loaded(l, n)
                    if (b, k) in ((1, 1), (2, 0)):
                        pe.wait_ge(S["out_read"], at("out_read", l, OUT_READ[0][1 - k]))
                    done(by_channel(n, out_bank(b, k), y_hi[:, b, :, :], y_lo[:, b, :, :], CB, 4,
                                    between=between))

                for k in range(3):
                    gates_unit(0, k)
                loaded(l, U_PW)
                pe.wait_ge(S["xg_ready"], at("xg_ready", l, 2))
                pe.wait_ge(S["pooled_lo"], at("pooled_lo", l, 1))
                s = U_PW % RING
                for i in range(GR):
                    ins = product(pair(2 + i // 2)[:, i % 2, :], w_hi[:, s, i * P:(i + 1) * P],
                                  w_lo[:, s, i * P:(i + 1) * P], pl_hi[:, i, :], pl_lo[:, i, :], True, True)
                done(ins)
                gates_unit(0, 3)
                pe.wait_ge(S["yp_lo"], at("yp_lo", l, 4))
                pe.wait_ge(S["u_gelu"], at("u_gelu", l, 2))
                for k in range(2):
                    out_unit(0, k)
                gates_unit(1, 0)
                pe.wait_ge(S["v_lo_ready"], at("v_lo_ready", l, 1))
                for i in range(4):
                    for t in range(TT):
                        ins = product(pair(4 + i // 2)[:, i % 2, t * P:(t + 1) * P], v_hi[:, t, i * P:(i + 1) * P],
                                      v_lo[:, t, i * P:(i + 1) * P], wst_hi[:, i, :], wst_lo[:, i, :], True, True)
                ins.then_inc(S["s_done"], 1)
                for k in range(1, 4):
                    gates_unit(1, k)

                def means():
                    for i in range(2):
                        pe.wait_ge(S["acc_summed"], at("acc_summed", l, i + 1))
                        ins = te.matmul(ps[:, 4, 0:SEQ], mean_w[:, :], half_sum[i], start=i == 0, stop=i == 1)
                    ins.then_inc(S["stat_done"], 1)

                for k in range(4):
                    gates_unit(2, k)
                means()

                def variances():
                    pe.wait_ge(S["gate_sig"], at("gate_sig", l, 12))
                    pe.wait_ge(S["csq_ready"], at("csq_ready", l, 1))
                    for t in range(TT):
                        for c in range(CB):
                            ins = te.matmul(ps[:, 5, t:t + 1], ctmp[:, c, t * P:(t + 1) * P], mean_w[:, 0:1],
                                            start=c == 0, stop=c == CB - 1)
                    ins.then_inc(S["stat_done"], 1)

                def roots():
                    pe.wait_ge(S["diag_ready"], at("diag_ready", l, 1))
                    for t in range(TT):
                        ins = te.matmul(ps[:, 4, SEQ + t * P:SEQ + (t + 1) * P], ones[:, :], diag[:, t, :],
                                        start=True, stop=True)
                    ins.then_inc(S["stat_done"], 1)

                pe.wait_ge(S["gate_sig"], at("gate_sig", l, 11))
                pe.wait_ge(S["us_lo"], at("us_lo", l, 1))
                out_unit(1, 0, variances)
                roots()
                out_unit(1, 1)
                pe.wait_ge(S["cy_lo"], at("cy_lo", l, 2))
                for k in range(2):
                    out_unit(2, k)
                pe.wait_ge(S["out_read"], at("out_read", l, OUT_READ[1][1]))
                loaded(l, U_WOUT)
                pe.wait_ge(S["mg_lo"], at("mg_lo", l, 1))
                for t in range(TT):
                    ins = by_token(t, U_WOUT, 0, nt_hi, nt_lo, 0, 2, True, False)
                done(ins)

                def last_out(k, t, between):
                    if k == 1:
                        pe.wait_ge(S["mg_lo"], at("mg_lo", l, 2))
                    return by_token(t, U_WOUT + 1 + k, 0, nt_hi, nt_lo, 2 + 2 * k, 2, False, k == 2,
                                    between)

                last_three(l, U_WOUT + 1, last_out, 2)
                ffn(l, 1, U_FFN2)
                loaded(l, U_EMB)
                pe.wait_ge(S["prod_ready"], at("prod_ready", l, 2 * NCH))
                for t in range(TT):
                    ins = by_token(t, U_EMB, 4, pt_hi, pt_lo, 0, 2, True, True)
                done(ins)
                rows_split(l, 3, 0, 1)
                for k in range(2):
                    loaded(l, U_PLEG + k)
                    by_token(0, U_PLEG + k, 0, nt_hi, nt_lo, k, 1, k == 0, False)
                    if k == 0:
                        turn(l, 3, 1)
                rows_split(l, 3, 1, 1)
                for k in range(2):
                    done(by_token(1, U_PLEG + k, 0, nt_hi, nt_lo, k, 1, k == 0, False))

                last_three(l, U_PLEG + 2, lambda k, t, between: by_token(
                    t, U_PLEG + 2 + k, 0, nt_hi, nt_lo, 2 + 2 * k, 2, False, k == 2))


_INS = [
    "x", "p", "ffn1_pre_g", "ffn1_w_gate", "ffn1_w_up", "ffn1_w_down", "ffn1_post_g", "mix_pre_g", "w_in",
    "pool_w", "pool_scale", "w_pool_out", "sgu_ln_g", "sgu_ln_b", "sgu_w_s", "sgu_b_s", "w_sgu_out",
    "conv_dw_k", "conv_dw_b", "conv_ln_g", "conv_ln_b", "w_conv_out", "w_out", "mix_post_g", "ffn2_pre_g",
    "ffn2_w_gate", "ffn2_w_up", "ffn2_w_down", "ffn2_post_g", "ple_w_proj", "ple_pre_g", "ple_w_gate",
    "ple_post_g",
]


def kernel(**inputs):
    import numpy as np
    import concourse.bacc as bacc
    from concourse.bass_utils import run_bass_kernel_spmd

    nc = bacc.Bacc("TRN2", target_bir_lowering=False, num_devices=1)
    arrays, aps = {}, {}
    for name in _INS:
        a = np.ascontiguousarray(inputs[name])
        arrays[f"in_{name}"] = a
        aps[name] = nc.dram_tensor(f"in_{name}", a.shape, mybir.dt.from_np(a.dtype), kind="ExternalInput").ap()
    out = nc.dram_tensor("out", inputs["x"].shape, F32, kind="ExternalOutput").ap()
    hybrid_trunk(nc, aps, out)
    r = run_bass_kernel_spmd(nc, [arrays], core_ids=[0])
    return r.results[0]["out"]
```
